# Optimizing a Trainium2 kernel written in Bass

```python
import math
import jax, jax.numpy as jnp
from jax import lax
import numpy as np

D_MODEL = 1024
BATCH = 1
SEQ = 512
DEPTH = 1

HEAD_DIM = 64
A_HEADS = 8
A_KV_HEADS = 2
A_WINDOW = 128
B_HEADS = 8
B_KV_GROUPS = 2
CMP_BLOCK = 32
CMP_STRIDE = 16
CMP_HIDDEN = 256
SLC_BLOCK = 64
SLC_TOPK = 16
NSA_WINDOW = 512
NUM_BUCKETS = 32
MAX_DISTANCE = 128
D_FF = 2816
CONV_WIDTH = 3
Q_BLOCK = 128
EPS = 1e-6
NEG = -1e30
BIG = 1e30

A_Q_DIM = A_HEADS * HEAD_DIM
A_KV_DIM = A_KV_HEADS * HEAD_DIM
B_Q_DIM = B_HEADS * HEAD_DIM
B_KV_DIM = B_KV_GROUPS * HEAD_DIM
B_GATE_DIM = 3 * B_HEADS
IN_SPLITS = (A_Q_DIM, A_KV_DIM, A_KV_DIM, B_Q_DIM, B_KV_DIM, B_KV_DIM, B_KV_DIM, B_KV_DIM, B_KV_DIM, B_KV_DIM, B_GATE_DIM, D_MODEL, D_MODEL)
IN_DIM = sum(IN_SPLITS)
IN_OFFSETS = tuple(int(o) for o in np.cumsum(IN_SPLITS)[:-1])


def rmsnorm(x, g):
    xf = x.astype(jnp.float32)
    y = xf * lax.rsqrt(jnp.mean(xf * xf, axis=-1, keepdims=True) + EPS)
    return (y * g.astype(jnp.float32)).astype(x.dtype)

def t5_bucket(dist):
    dist = jnp.maximum(dist, 0)
    max_exact = NUM_BUCKETS // 2
    d = jnp.maximum(dist, 1).astype(jnp.float32)
    large = max_exact + (jnp.log(d / max_exact) / math.log(MAX_DISTANCE / max_exact)
                         * (NUM_BUCKETS - max_exact)).astype(jnp.int32)
    large = jnp.minimum(large, NUM_BUCKETS - 1)
    return jnp.where(dist < max_exact, dist, large)

def head_bias(table_gr, dist):
    return jnp.transpose(table_gr[t5_bucket(dist)], (2, 3, 0, 1))

def selection_overlap(n_cmp, n_slc):
    r = SLC_BLOCK // CMP_STRIDE
    c = CMP_BLOCK // CMP_STRIDE
    j, m, n = np.meshgrid(np.arange(n_slc), np.arange(r), np.arange(c), indexing='ij')
    i = r * j + m - n
    ok = (i >= 0) & (i < n_cmp)
    mat = np.zeros((n_cmp, n_slc), np.float32)
    np.add.at(mat, (i[ok], j[ok]), 1.0)
    return mat

def causal_dwconv(u, w, b):
    c = u.shape[-1]
    out = lax.conv_general_dilated(u, w[:, None, :].astype(u.dtype), window_strides=(1,),
                                   padding=[(CONV_WIDTH - 1, 0)],
                                   dimension_numbers=('NWC', 'WIO', 'NWC'),
                                   feature_group_count=c)
    return out + b

def swa_sink_attention(q, k, v, sinks, table):
    bsz, seq, n_heads, dh = q.shape
    n_groups = k.shape[2]
    rep = n_heads // n_groups
    span = A_WINDOW + Q_BLOCK
    qg = q.reshape(bsz, seq, n_groups, rep, dh)
    kp = jnp.pad(k, ((0, 0), (A_WINDOW, 0), (0, 0), (0, 0)))
    vp = jnp.pad(v, ((0, 0), (A_WINDOW, 0), (0, 0), (0, 0)))
    qi = jnp.arange(Q_BLOCK)[:, None]
    ki = jnp.arange(span)[None, :]
    dist = qi + A_WINDOW - ki
    in_window = (dist >= 0) & (dist < A_WINDOW)
    bias = head_bias(table.reshape(NUM_BUCKETS, n_groups, rep), dist)
    sink = sinks.astype(jnp.float32).reshape(n_groups, rep)
    scale = dh ** -0.5

    def block(b):
        start = b * Q_BLOCK
        qb = lax.dynamic_slice_in_dim(qg, start, Q_BLOCK, axis=1)
        kb = lax.dynamic_slice_in_dim(kp, start, span, axis=1)
        vb = lax.dynamic_slice_in_dim(vp, start, span, axis=1)
        valid = in_window & (start - A_WINDOW + ki >= 0)
        logits = jnp.einsum('bqgrd,bkgd->bgrqk', qb, kb, preferred_element_type=jnp.float32) * scale + bias
        logits = jnp.where(valid, logits, NEG)
        sink_col = jnp.broadcast_to(sink[None, :, :, None, None], logits.shape[:-1] + (1,))
        probs = jax.nn.softmax(jnp.concatenate([logits, sink_col], axis=-1), axis=-1)[..., :span]
        out = jnp.einsum('bgrqk,bkgd->bqgrd', probs.astype(v.dtype), vb)
        return out.reshape(bsz, Q_BLOCK, n_heads * dh)

    out = lax.map(block, jnp.arange(seq // Q_BLOCK))
    return jnp.transpose(out, (1, 0, 2, 3)).reshape(bsz, seq, n_heads * dh)

def compress(kv, pos, w1, w2):
    bsz, seq, n_groups, dh = kv.shape
    n_cmp = (seq - CMP_BLOCK) // CMP_STRIDE + 1
    idx = jnp.arange(n_cmp)[:, None] * CMP_STRIDE + jnp.arange(CMP_BLOCK)[None, :]
    blocks = kv[:, idx] + pos[None, None, :, None, :]
    blocks = jnp.transpose(blocks, (0, 1, 3, 2, 4)).reshape(bsz, n_cmp, n_groups, CMP_BLOCK * dh)
    return jax.nn.gelu(blocks @ w1) @ w2

def nsa_attention(q, k_cmp, v_cmp, k_slc, v_slc, k_win, v_win, gates, table):
    bsz, seq, n_heads, dh = q.shape
    n_groups = k_slc.shape[2]
    rep = n_heads // n_groups
    n_cmp = k_cmp.shape[1]
    n_slc = seq // SLC_BLOCK
    topk = min(SLC_TOPK, n_slc)
    n_tok = topk * SLC_BLOCK
    scale = dh ** -0.5
    qg = q.reshape(bsz, seq, n_groups, rep, dh)
    table_gr = table.reshape(NUM_BUCKETS, n_groups, rep)
    table_g = jnp.transpose(table_gr, (1, 0, 2))
    cmp_end = jnp.arange(n_cmp) * CMP_STRIDE + CMP_BLOCK - 1
    overlap = jnp.asarray(selection_overlap(n_cmp, n_slc))
    k_slc_g = jnp.transpose(k_slc, (0, 2, 1, 3))
    v_slc_g = jnp.transpose(v_slc, (0, 2, 1, 3))
    span = NSA_WINDOW + Q_BLOCK
    kwp = jnp.pad(k_win, ((0, 0), (NSA_WINDOW, 0), (0, 0), (0, 0)))
    vwp = jnp.pad(v_win, ((0, 0), (NSA_WINDOW, 0), (0, 0), (0, 0)))
    qi = jnp.arange(Q_BLOCK)[:, None]
    ki = jnp.arange(span)[None, :]
    dist_w = qi + NSA_WINDOW - ki
    in_window = (dist_w >= 0) & (dist_w < NSA_WINDOW)
    bias_w = head_bias(table_gr, dist_w)
    bidx = jnp.arange(bsz)[:, None, None, None]
    gidx = jnp.arange(n_groups)[None, :, None, None]
    slc_ids = jnp.arange(n_slc)[None, :]

    def block(b):
        start = b * Q_BLOCK
        qpos = start + jnp.arange(Q_BLOCK)
        qb = lax.dynamic_slice_in_dim(qg, start, Q_BLOCK, axis=1)
        dist_c = qpos[:, None] - cmp_end[None, :]
        valid_c = dist_c >= 0
        lc = jnp.einsum('bqgrd,bcgd->bgrqc', qb, k_cmp, preferred_element_type=jnp.float32) * scale
        lc = jnp.where(valid_c, lc + head_bias(table_gr, dist_c), NEG)
        p_c = jax.nn.softmax(lc, axis=-1) * valid_c
        o_c = jnp.einsum('bgrqc,bcgd->bqgrd', p_c.astype(v_cmp.dtype), v_cmp)
        imp = jnp.einsum('bgrqc,cj->bgqj', p_c, overlap)
        qblk = (qpos // SLC_BLOCK)[:, None]
        forced = (slc_ids == 0) | (slc_ids == qblk) | (slc_ids == qblk - 1)
        score = jnp.where(forced, BIG, jnp.where(slc_ids > qblk, NEG, imp))
        _, sel = lax.top_k(score, topk)
        tok = (sel[..., None] * SLC_BLOCK + jnp.arange(SLC_BLOCK)).reshape(bsz, n_groups, Q_BLOCK, n_tok)
        ks = k_slc_g[bidx, gidx, tok]
        vs = v_slc_g[bidx, gidx, tok]
        dist_s = qpos[None, None, :, None] - tok
        bias_s = jnp.transpose(table_g[gidx, t5_bucket(dist_s)], (0, 1, 4, 2, 3))
        ls = jnp.einsum('bqgrd,bgqtd->bgrqt', qb, ks, preferred_element_type=jnp.float32) * scale + bias_s
        ls = jnp.where((dist_s >= 0)[:, :, None], ls, NEG)
        p_s = jax.nn.softmax(ls, axis=-1)
        o_s = jnp.einsum('bgrqt,bgqtd->bqgrd', p_s.astype(v_slc.dtype), vs)
        kb = lax.dynamic_slice_in_dim(kwp, start, span, axis=1)
        vb = lax.dynamic_slice_in_dim(vwp, start, span, axis=1)
        valid_w = in_window & (start - NSA_WINDOW + ki >= 0)
        lw = jnp.einsum('bqgrd,bkgd->bgrqk', qb, kb, preferred_element_type=jnp.float32) * scale + bias_w
        p_w = jax.nn.softmax(jnp.where(valid_w, lw, NEG), axis=-1)
        o_w = jnp.einsum('bgrqk,bkgd->bqgrd', p_w.astype(v_win.dtype), vb)
        gb = lax.dynamic_slice_in_dim(gates, start, Q_BLOCK, axis=1)
        out = gb[..., 0:1] * o_c + gb[..., 1:2] * o_s + gb[..., 2:3] * o_w
        return out.reshape(bsz, Q_BLOCK, n_heads * dh)

    out = lax.map(block, jnp.arange(seq // Q_BLOCK))
    return jnp.transpose(out, (1, 0, 2, 3)).reshape(bsz, seq, n_heads * dh)

def first_inputs(seed: int = 0) -> dict:
    key = jax.random.key(seed)
    ks = jax.random.split(key, 20)
    f32 = jnp.float32

    def nrm(k, shape, scale):
        return jax.random.normal(k, shape, f32) * scale

    L, D = DEPTH, D_MODEL
    cmp_in = CMP_BLOCK * HEAD_DIM
    return {
        'x': nrm(ks[0], (BATCH, SEQ, D), 1.0),
        'norm_mix': 1.0 + nrm(ks[1], (L, D), 0.02),
        'w_in': nrm(ks[2], (L, D, IN_DIM), D ** -0.5),
        'attn_sinks': nrm(ks[3], (L, A_HEADS), 0.5),
        'cmp_pos_k': nrm(ks[4], (L, CMP_BLOCK, HEAD_DIM), 0.1),
        'cmp_w1_k': nrm(ks[5], (L, cmp_in, CMP_HIDDEN), cmp_in ** -0.5),
        'cmp_w2_k': nrm(ks[6], (L, CMP_HIDDEN, HEAD_DIM), CMP_HIDDEN ** -0.5),
        'cmp_pos_v': nrm(ks[7], (L, CMP_BLOCK, HEAD_DIM), 0.1),
        'cmp_w1_v': nrm(ks[8], (L, cmp_in, CMP_HIDDEN), cmp_in ** -0.5),
        'cmp_w2_v': nrm(ks[9], (L, CMP_HIDDEN, HEAD_DIM), CMP_HIDDEN ** -0.5),
        'w_up_a': nrm(ks[10], (L, A_Q_DIM, D), A_Q_DIM ** -0.5),
        'w_up_b': nrm(ks[11], (L, B_Q_DIM, D), B_Q_DIM ** -0.5),
        'w_out': nrm(ks[12], (L, D, D), D ** -0.5),
        'norm_ffn': 1.0 + nrm(ks[13], (L, D), 0.02),
        'w_ffn_in': nrm(ks[14], (L, D, 2 * D_FF), D ** -0.5),
        'conv_w': nrm(ks[15], (L, CONV_WIDTH, 2 * D_FF), CONV_WIDTH ** -0.5),
        'conv_b': nrm(ks[16], (L, 2 * D_FF), 0.01),
        'w_ffn_out': nrm(ks[17], (L, D_FF, D), D_FF ** -0.5),
        'rel_bias_table': nrm(ks[18], (NUM_BUCKETS, A_HEADS + B_HEADS), 0.5),
        'norm_final': 1.0 + nrm(ks[19], (D,), 0.02),
    }

def first_block(x, norm_mix, w_in, attn_sinks, cmp_pos_k, cmp_w1_k, cmp_w2_k, cmp_pos_v, cmp_w1_v, cmp_w2_v,
              w_up_a, w_up_b, w_out, norm_ffn, w_ffn_in, conv_w, conv_b, w_ffn_out, rel_bias_table, norm_final):
    bsz, seq, _ = x.shape
    table_a = rel_bias_table[:, :A_HEADS]
    table_b = rel_bias_table[:, A_HEADS:]

    def heads(t, n):
        return t.reshape(bsz, seq, n, HEAD_DIM)

    for l in range(DEPTH):
        h = rmsnorm(x, norm_mix[l])
        proj = h @ w_in[l]
        (qa, ka, va, qb, kc, vc, ksl, vsl, kw, vw, g_nsa, g_a, g_b) = jnp.split(proj, IN_OFFSETS, axis=-1)
        y_a = swa_sink_attention(heads(qa, A_HEADS), heads(ka, A_KV_HEADS), heads(va, A_KV_HEADS),
                                 attn_sinks[l], table_a)
        k_cmp = compress(heads(kc, B_KV_GROUPS), cmp_pos_k[l], cmp_w1_k[l], cmp_w2_k[l])
        v_cmp = compress(heads(vc, B_KV_GROUPS), cmp_pos_v[l], cmp_w1_v[l], cmp_w2_v[l])
        nsa_gates = jax.nn.sigmoid(g_nsa).reshape(bsz, seq, B_KV_GROUPS, B_HEADS // B_KV_GROUPS, 3)
        y_b = nsa_attention(heads(qb, B_HEADS), k_cmp, v_cmp, heads(ksl, B_KV_GROUPS), heads(vsl, B_KV_GROUPS),
                            heads(kw, B_KV_GROUPS), heads(vw, B_KV_GROUPS), nsa_gates, table_b)
        merged = jax.nn.sigmoid(g_a) * (y_a @ w_up_a[l]) + jax.nn.sigmoid(g_b) * (y_b @ w_up_b[l])
        x = x + merged @ w_out[l]
        h = rmsnorm(x, norm_ffn[l])
        ug = causal_dwconv(h @ w_ffn_in[l], conv_w[l], conv_b[l])
        u, g = jnp.split(ug, 2, axis=-1)
        x = x + (jax.nn.silu(g) * u) @ w_ffn_out[l]
    return rmsnorm(x, norm_final)


MEM_TOKENS = 256
ROPE_THETA = 10000.0
RMS_EPS = 1e-6
NEG_INF = -1e30

MLA_HEADS = 8
Q_LORA = 256
KV_LORA = 128
MLA_NOPE = 64
MLA_ROPE = 32
MLA_QK = MLA_NOPE + MLA_ROPE
MLA_V = 64
MLA_W = MLA_HEADS * MLA_V

DIFF_HEADS = 4
DIFF_D = 32
DIFF_V = 2 * DIFF_D
DIFF_W = DIFF_HEADS * DIFF_V

MEM_HEADS = 4
MEM_D = 64
MEM_W = MEM_HEADS * MEM_D

D_MIX = MLA_W + DIFF_W + MEM_W

IN_SPLITS_2 = [
    Q_LORA,
    KV_LORA,
    MLA_ROPE,
    DIFF_HEADS * 2 * DIFF_D,
    DIFF_HEADS * 2 * DIFF_D,
    DIFF_W,
    MEM_W,
    D_MIX,
]
D_IN = int(sum(IN_SPLITS_2))
IN_OFFSETS_2 = [int(v) for v in np.cumsum(IN_SPLITS_2)[:-1]]


def rms_norm(x, g, eps=RMS_EPS):
    xf = x.astype(jnp.float32)
    y = xf * lax.rsqrt(jnp.mean(xf * xf, axis=-1, keepdims=True) + eps)
    return (y * g.astype(jnp.float32)).astype(x.dtype)

def rope(x, pos):
    d = x.shape[-1]
    inv = ROPE_THETA ** (-jnp.arange(0, d, 2, dtype=jnp.float32) / d)
    ang = pos.astype(jnp.float32)[..., None] * inv
    cos = jnp.cos(ang)[:, :, None, :]
    sin = jnp.sin(ang)[:, :, None, :]
    xf = x.astype(jnp.float32)
    x1, x2 = xf[..., : d // 2], xf[..., d // 2:]
    out = jnp.concatenate([x1 * cos - x2 * sin, x2 * cos + x1 * sin], axis=-1)
    return out.astype(x.dtype)

def causal_mask(start, s_len):
    q_idx = start + jnp.arange(Q_BLOCK, dtype=jnp.int32)
    return jnp.arange(s_len, dtype=jnp.int32)[None, :] <= q_idx[:, None]

def causal_block_sweep(block_fn, q):
    b, s = q.shape[0], q.shape[1]
    nb = s // Q_BLOCK
    qb = jnp.moveaxis(q.reshape((b, nb, Q_BLOCK) + q.shape[2:]), 1, 0)
    starts = jnp.arange(nb, dtype=jnp.int32) * Q_BLOCK
    out = lax.map(lambda a: block_fn(a[0], a[1]), (qb, starts))
    return jnp.moveaxis(out, 0, 1).reshape((b, s) + out.shape[3:])

def mla_branch(cq, ckv, kr, pos, q_norm_g, kv_norm_g, w_uq, w_ukv, qn_g, kn_g):
    b, s, _ = cq.shape
    q = (rms_norm(cq, q_norm_g) @ w_uq).reshape(b, s, MLA_HEADS, MLA_QK)
    kv = (rms_norm(ckv, kv_norm_g) @ w_ukv).reshape(b, s, MLA_HEADS, MLA_NOPE + MLA_V)
    k_nope, v = kv[..., :MLA_NOPE], kv[..., MLA_NOPE:]
    k_rope = jnp.broadcast_to(kr.reshape(b, s, 1, MLA_ROPE), (b, s, MLA_HEADS, MLA_ROPE))
    k = jnp.concatenate([k_nope, k_rope], axis=-1)
    q = rms_norm(q, qn_g)
    k = rms_norm(k, kn_g)
    q = jnp.concatenate([q[..., :MLA_NOPE], rope(q[..., MLA_NOPE:], pos)], axis=-1)
    k = jnp.concatenate([k[..., :MLA_NOPE], rope(k[..., MLA_NOPE:], pos)], axis=-1)
    scale = 1.0 / math.sqrt(MLA_QK)

    def block_fn(qblk, start):
        sc = jnp.einsum('bqhd,bkhd->bhqk', qblk, k).astype(jnp.float32) * scale
        sc = jnp.where(causal_mask(start, s)[None, None], sc, NEG_INF)
        p = jax.nn.softmax(sc, axis=-1).astype(v.dtype)
        return jnp.einsum('bhqk,bkhd->bqhd', p, v)

    o = causal_block_sweep(block_fn, q)
    return o.reshape(b, s, MLA_W)

def diff_branch(dq, dk, dv, pos, qn_g, kn_g, lam_vecs, subln_g, lam_init):
    b, s, _ = dq.shape
    q = rms_norm(dq.reshape(b, s, DIFF_HEADS * 2, DIFF_D), qn_g)
    k = rms_norm(dk.reshape(b, s, DIFF_HEADS * 2, DIFF_D), kn_g)
    q = rope(q, pos).reshape(b, s, DIFF_HEADS, 2, DIFF_D)
    k = rope(k, pos).reshape(b, s, DIFF_HEADS, 2, DIFF_D)
    v = dv.reshape(b, s, DIFF_HEADS, DIFF_V)
    lv = lam_vecs.astype(jnp.float32)
    lam = jnp.exp(jnp.sum(lv[0] * lv[1])) - jnp.exp(jnp.sum(lv[2] * lv[3])) + lam_init
    scale = 1.0 / math.sqrt(DIFF_D)

    def block_fn(qblk, start):
        sc = jnp.einsum('bqhmd,bkhmd->bhmqk', qblk, k).astype(jnp.float32) * scale
        sc = jnp.where(causal_mask(start, s)[None, None, None], sc, NEG_INF)
        p = jax.nn.softmax(sc, axis=-1)
        a = (p[:, :, 0] - lam * p[:, :, 1]).astype(v.dtype)
        return jnp.einsum('bhqk,bkhd->bqhd', a, v)

    o = causal_block_sweep(block_fn, q)
    o = rms_norm(o, subln_g) * (1.0 - lam_init)
    return o.reshape(b, s, DIFF_W)

def mem_branch(mq, mem, mem_norm_g, w_mem_kv, qn_g, kn_g):
    b, s, _ = mq.shape
    m = mem.shape[1]
    kv = rms_norm(mem, mem_norm_g) @ w_mem_kv
    k = rms_norm(kv[..., :MEM_W].reshape(b, m, MEM_HEADS, MEM_D), kn_g)
    v = kv[..., MEM_W:].reshape(b, m, MEM_HEADS, MEM_D)
    q = rms_norm(mq.reshape(b, s, MEM_HEADS, MEM_D), qn_g)
    sc = jnp.einsum('bshd,bmhd->bhsm', q, k).astype(jnp.float32) / math.sqrt(MEM_D)
    p = jax.nn.softmax(sc, axis=-1).astype(v.dtype)
    o = jnp.einsum('bhsm,bmhd->bshd', p, v)
    return o.reshape(b, s, MEM_W)

def second_inputs(seed: int = 0) -> dict:
    key = jax.random.key(seed)
    ks = jax.random.split(key, 24)
    f32 = jnp.float32

    def nrm(k, shape, fan_in):
        return jax.random.normal(k, shape, f32) * (fan_in ** -0.5)

    def gain(k, shape):
        return 1.0 + 0.01 * jax.random.normal(k, shape, f32)

    x = jax.random.normal(ks[0], (BATCH, SEQ, D_MODEL), f32)
    mem = jax.random.normal(ks[1], (BATCH, MEM_TOKENS, D_MODEL), f32)
    offsets = jax.random.randint(ks[2], (BATCH, 1), 0, 4096, dtype=jnp.int32)
    positions = offsets + jnp.arange(SEQ, dtype=jnp.int32)[None, :]
    return {
        "x": x,
        "mem": mem,
        "positions": positions,
        "norm_g": gain(ks[3], (DEPTH, D_MODEL)),
        "w_in": nrm(ks[4], (DEPTH, D_MODEL, D_IN), D_MODEL),
        "mla_q_norm_g": gain(ks[5], (DEPTH, Q_LORA)),
        "mla_kv_norm_g": gain(ks[6], (DEPTH, KV_LORA)),
        "w_uq": nrm(ks[7], (DEPTH, Q_LORA, MLA_HEADS * MLA_QK), Q_LORA),
        "w_ukv": nrm(ks[8], (DEPTH, KV_LORA, MLA_HEADS * (MLA_NOPE + MLA_V)), KV_LORA),
        "mla_qn_g": gain(ks[9], (DEPTH, MLA_QK)),
        "mla_kn_g": gain(ks[10], (DEPTH, MLA_QK)),
        "diff_qn_g": gain(ks[11], (DEPTH, DIFF_D)),
        "diff_kn_g": gain(ks[12], (DEPTH, DIFF_D)),
        "diff_lambda": 0.1 * jax.random.normal(ks[13], (DEPTH, 4, DIFF_D), f32),
        "diff_subln_g": gain(ks[14], (DEPTH, DIFF_V)),
        "mem_norm_g": gain(ks[15], (DEPTH, D_MODEL)),
        "w_mem_kv": nrm(ks[16], (DEPTH, D_MODEL, 2 * MEM_W), D_MODEL),
        "mem_qn_g": gain(ks[17], (DEPTH, MEM_D)),
        "mem_kn_g": gain(ks[18], (DEPTH, MEM_D)),
        "w_out": nrm(ks[19], (DEPTH, D_MIX, D_MODEL), D_MIX),
    }

def second_block(x, mem, positions, norm_g, w_in, mla_q_norm_g, mla_kv_norm_g, w_uq, w_ukv,
              mla_qn_g, mla_kn_g, diff_qn_g, diff_kn_g, diff_lambda, diff_subln_g,
              mem_norm_g, w_mem_kv, mem_qn_g, mem_kn_g, w_out):
    for l in range(DEPTH):
        lam_init = 0.8 - 0.6 * math.exp(-0.3 * l)
        h = rms_norm(x, norm_g[l])
        proj = h @ w_in[l]
        cq, ckv, kr, dq, dk, dv, mq, z = jnp.split(proj, IN_OFFSETS_2, axis=-1)
        y_mla = mla_branch(cq, ckv, kr, positions, mla_q_norm_g[l], mla_kv_norm_g[l],
                           w_uq[l], w_ukv[l], mla_qn_g[l], mla_kn_g[l])
        y_diff = diff_branch(dq, dk, dv, positions, diff_qn_g[l], diff_kn_g[l],
                             diff_lambda[l], diff_subln_g[l], lam_init)
        y_mem = mem_branch(mq, mem, mem_norm_g[l], w_mem_kv[l], mem_qn_g[l], mem_kn_g[l])
        y = jnp.concatenate([y_mla, y_diff, y_mem], axis=-1) * jax.nn.silu(z)
        x = x + y @ w_out[l]
    return x


def setup_inputs(seed=0):
    out = dict(first_inputs(seed))
    for name, value in second_inputs(seed + 1).items():
        if name != "x":
            out[name + "_2"] = value
    return out


def reference(
    x, norm_mix, w_in, attn_sinks, cmp_pos_k, cmp_w1_k, cmp_w2_k, cmp_pos_v, cmp_w1_v, cmp_w2_v,
    w_up_a, w_up_b, w_out, norm_ffn, w_ffn_in, conv_w, conv_b, w_ffn_out, rel_bias_table,
    norm_final, mem_2, positions_2, norm_g_2, w_in_2, mla_q_norm_g_2, mla_kv_norm_g_2, w_uq_2,
    w_ukv_2, mla_qn_g_2, mla_kn_g_2, diff_qn_g_2, diff_kn_g_2, diff_lambda_2, diff_subln_g_2,
    mem_norm_g_2, w_mem_kv_2, mem_qn_g_2, mem_kn_g_2, w_out_2,
):
    x = first_block(
        x, norm_mix, w_in, attn_sinks, cmp_pos_k, cmp_w1_k, cmp_w2_k, cmp_pos_v, cmp_w1_v,
        cmp_w2_v, w_up_a, w_up_b, w_out, norm_ffn, w_ffn_in, conv_w, conv_b, w_ffn_out,
        rel_bias_table, norm_final,
    )
    return second_block(
        x, mem_2, positions_2, norm_g_2, w_in_2, mla_q_norm_g_2, mla_kv_norm_g_2, w_uq_2,
        w_ukv_2, mla_qn_g_2, mla_kn_g_2, diff_qn_g_2, diff_kn_g_2, diff_lambda_2,
        diff_subln_g_2, mem_norm_g_2, w_mem_kv_2, mem_qn_g_2, mem_kn_g_2, w_out_2,
    )


_drawn_inputs = setup_inputs


def setup_inputs(seed=0):
    import zlib

    import numpy as np

    out = dict(_drawn_inputs(seed))
    spreads = {}
    factors = {'norm_mix': 8.0,
     'attn_sinks': 8.0,
     'cmp_pos_k': 8.0,
     'norm_ffn': 3.42,
     'conv_b': 6.588,
     'norm_g_2': 8.0,
     'mla_q_norm_g_2': 8.0,
     'mla_kv_norm_g_2': 8.0,
     'mla_qn_g_2': 8.0,
     'mla_kn_g_2': 8.0,
     'diff_qn_g_2': 8.0,
     'diff_kn_g_2': 8.0,
     'diff_lambda_2': 3.683,
     'diff_subln_g_2': 8.0,
     'mem_norm_g_2': 8.0,
     'mem_qn_g_2': 8.0,
     'mem_kn_g_2': 8.0}
    for name, (base, spread) in spreads.items():
        noise = np.random.default_rng([zlib.crc32(name.encode()), seed]).standard_normal(out[name].shape)
        drawn = base * np.exp(spread * noise) if base else spread * noise
        out[name] = __import__('jax').numpy.asarray(drawn.astype(out[name].dtype))
    for name, factor in factors.items():
        out[name] = (out[name] * factor).astype(out[name].dtype)
    return out
```

```python
import math

import numpy as np
import concourse.bass as bass
from concourse import mybir

F = mybir.dt.float32
R = mybir.dt.float32r
I32 = mybir.dt.int32
ALU = mybir.AluOpType
ACT = mybir.ActivationFunctionType
AX = mybir.AxisListType

P = 128
SEQ = 512
NT = SEQ // P
D = 1024
KT = D // P
DH = 64
NH = 8
NBUCKET = 32
N_CMP = (SEQ - 32) // 16 + 1
CMP_A = 66
D_FF = 2816
NF = D_FF // P
EPS = 1e-6
NEG = -1e30
LAM_INIT = 0.8 - 0.6 * math.exp(0.0)

_PLAN = [("proj", 13), ("vtok", 4), ("cmp", 8), ("merge", 24), ("wout", 8), ("ffn", 2 * NF),
         ("down", 24), ("mem", 4), ("tok2", 12), ("z", 8), ("uq", 2), ("ukv", 1), ("wout2", 8)]
UNIT = {}
NU = 0
for _n, _c in _PLAN:
    UNIT[_n] = NU
    NU += _c

OH_A, OH_B, OH_C = 384, 640, 16 * CMP_A
OH = OH_A + OH_B + OH_C

COL = {}
_at = 0
for _n, _c in [("g_mix", 8), ("g_ffn", 8), ("g_final", 8), ("g_2", 8), ("g_mem", 8), ("g_q2", 2),
               ("g_kv2", 1), ("subln", 1), ("pos_k", 32), ("pos_v", 32), ("conv", 4 * 2 * NF)]:
    COL[_n] = _at
    _at += _c
NCOL = _at
ROW = {}
_at = 0
for _n, _c in [("qn", 96), ("kn", 96), ("dqn", 32), ("dkn", 32), ("mqn", 64), ("mkn", 64),
               ("sinks", 8), ("inv", 16), ("lam", 128)]:
    ROW[_n] = _at
    _at += _c
NROW = _at


class Chain:

    def __init__(self, eng, sem):
        self.eng, self.sem, self.n = eng, sem, 0

    def link(self, ins):
        self.n += 1
        ins.then_inc(self.sem, 1)
        self.eng.wait_ge(self.sem, self.n)


def build(nc, t, out):
    from contextlib import ExitStack
    ctx = ExitStack()
    with ctx:
        def sb(name, shape, dt=F):
            return ctx.enter_context(nc.sbuf_tensor(name, shape, dt))

        def sem(name):
            return ctx.enter_context(nc.semaphore(name))

        X = sb("X", [P, KT, SEQ])
        FX = sb("FX", [P, 8, SEQ])
        HHI = sb("HHI", [P, KT, SEQ], R)
        HLO = sb("HLO", [P, KT, SEQ], R)
        BHI = sb("BHI", [P, 24, SEQ], R)
        BLO = sb("BLO", [P, 24, SEQ], R)
        RAW = sb("RAW", [P, 2, 1024])
        WHI = sb("WHI", [P, 2, 1024], R)
        WLO = sb("WLO", [P, 2, 1024], R)
        PB = sb("PB", [P, 7 * SEQ])
        TRI = sb("TRI", [P, SEQ])
        IDN = sb("IDN", [P, P])
        ONE = sb("ONE", [P, P])
        BONE = sb("BONE", [P, P])
        CL = sb("CL", [P, NCOL])
        RW = sb("RW", [P, NROW])
        GATE = sb("GATE", [P, NT, 24])
        KR = sb("KR", [P, NT, 32])
        COS = sb("COS", [P, NT, 32])
        SIN = sb("SIN", [P, NT, 32])
        POS = sb("POS", [P, NT], I32)
        ST = sb("ST", [P, 4, 24])
        SS = sb("SS", [P, 64])
        MSK = sb("MSK", [P, NT])
        LAM = sb("LAM", [P, 4])
        TBL = sb("TBL", [NBUCKET + 1, 16])
        PS = ctx.enter_context(nc.psum_tensor("PS", [P, 8, SEQ], F))
        tb_dram = nc.dram_tensor("bias_rows", [16, OH], F, kind="Internal").ap()
        bias_a = nc.dram_tensor("bias_a", [NH, P, 256], F, kind="Internal").ap()
        bias_b = nc.dram_tensor("bias_b", [NH, P, SEQ], F, kind="Internal").ap()
        bias_c = nc.dram_tensor("bias_c", [NH, P, NT, N_CMP], F, kind="Internal").ap()

        RSTD = PB[:, 3 * SEQ:4 * SEQ]
        YT, YSQ = PB[:, 5 * SEQ:6 * SEQ], PB[:, 6 * SEQ:7 * SEQ]
        W2 = YT.rearrange("p (w h n) -> p w h n", w=2, h=2)

        def hi(tile):
            return BHI[:, tile, :] if tile < 24 else HHI[:, tile - 24, :]

        def lo(tile):
            return BLO[:, tile, :] if tile < 24 else HLO[:, tile - 24, :]

        def part(w, tile):
            return (hi, lo)[w](tile)

        def cat(w, tile, n):
            a = ((BHI, BLO) if tile < 24 else (HHI, HLO))[w]
            tile %= 24
            return a[:, tile:tile + n, :].rearrange("p a b -> p (a b)")

        def col(name, j=0):
            return CL[:, COL[name] + j:COL[name] + j + 1]

        def row(name, n):
            return RW[:, ROW[name]:ROW[name] + n]

        ld_x, ld_small, ld_mem, ld_bias = sem("ld_x"), sem("ld_small"), sem("ld_mem"), [sem("ld_bias0"), sem("ld_bias1")]
        ld_oh, ld_cmp, st_rows, ld_w2 = sem("ld_oh"), sem("ld_cmp"), sem("st_rows"), sem("ld_w2")
        raw_loaded = [sem("raw_loaded0"), sem("raw_loaded1")]
        split_hi, split_lo, unit_used = sem("split_hi"), sem("split_lo"), sem("unit_used")
        consts, dve_step, act_step = sem("consts"), sem("dve_step"), sem("act_step")
        n_sq, n_acc, n_tot, n_rin, n_rstd, n_t, n_hi, n_lo = [sem("norm_" + s) for s in
            ("sq", "acc", "tot", "rin", "rstd", "t", "hi", "lo")]
        spread = sem("spread")
        oh_mm, oh_ev, tbl_ready = sem("oh_mm"), sem("oh_ev"), sem("tbl_ready")
        ang_ready = sem("ang_ready")
        sin_ready = sem("sin_ready")
        proj_hi, proj_out = sem("proj_hi"), sem("proj_out")
        v_hi, v_lo = sem("v_hi"), sem("v_lo")
        cb_built, cb_hi, cb_lo = sem("cb_built"), sem("cb_hi"), sem("cb_lo")
        gelu_done, gelu_t, gelu_copied, cmp_mm, cmp_hi, cmp_lo = [sem(s) for s in
            ("gelu_done", "gelu_t", "gelu_copied", "cmp_mm", "cmp_hi", "cmp_lo")]
        merge_act, merge_dve = sem("merge_act"), sem("merge_dve")
        x1_done, x2_done, xf_done = sem("x1_done"), sem("x2_done"), sem("xf_done")
        ffn_act, ffn_dve = sem("ffn_act"), sem("ffn_dve")
        h_tok, h_sq, h_v, h_rin, h_rs, h_nrm, h_tr, h_hi, h_lo = [sem("head_" + s) for s in
            ("tok", "sq", "v", "rin", "rs", "nrm", "tr", "hi", "lo")]
        z_done, lam_sum, lam_exp, vm_hi, vm_lo = [sem(s) for s in ("z_done", "lam_sum", "lam_exp", "vm_hi", "vm_lo")]
        y_out, stored = sem("y_out"), sem("stored")
        ATT = {g: {s: sem(f"{g}_{s}") for s in
                   ("scores", "biased", "exped", "normed", "turned", "p_hi", "p_lo", "pv", "y_f", "y_hi", "y_lo")}
               for g in ("ab", "dm", "mla")}
        dm_sq, dm_tot, dm_rin, dm_rstd, dm_y, dm_hi, k_mm = [sem(s) for s in
            ("dm_sq", "dm_tot", "dm_rin", "dm_rstd", "dm_y", "dm_hi", "k_mm")]

        CAUSAL = dict(spans=[(0, 128), (0, 256), (0, 384), (0, 512)], place=[(0, 0), (2, 0), (0, 128), (1, 0)])
        WINDOW = dict(spans=[(0, 128), (0, 256), (128, 256), (256, 256)],
                      place=[(0, 0), (0, 128), (1, 0), (1, 256)])
        MEMORY = dict(spans=[(0, 256)] * 4, place=[(0, 0), (0, 256), (1, 0), (1, 256)])
        V_AT = 11
        PT_AB = (14, 18)
        KC, VC = 0, 128

        def causal_kb(kb):
            return kb * P, SEQ

        def window_kb(kb):
            return kb * P, min(SEQ, kb * P + 2 * P)

        def vtok(w, b):
            v = cat(w, V_AT, 3).rearrange("p (t n) -> p t n", t=NT)
            return lambda kb: v[:, kb, b * P:(b + 1) * P]

        ab = []
        heads = [(0, r, g) for r in range(4) for g in range(2)] + [(1, r, g) for r in range(4) for g in range(2)]
        for y, (blk, r, g) in enumerate(heads):
            rows = slice(g * DH, g * DH + DH)
            q = [part(w, 4 * blk + r)[rows] for w in (0, 1)]
            base = dict(q=q, y=y, rows=rows, ytile=4 * blk + r, bank=6 + y % 2, bias=y, h=4 * g + r, scale=DH ** -0.5)
            if blk == 0:
                ab.append(dict(base, kind="bias", k=[part(w, 8)[rows] for w in (0, 1)], v=[vtok(w, 0) for w in (0, 1)],
                               nkb=4, kb=window_kb, b0=[128, 0, 0, 0], sink=True, first=True, last=True, **WINDOW))
            else:
                for b, tile in ((1, 9), (2, 10)):
                    ab.append(dict(base, kind="bias", k=[part(w, tile)[rows] for w in (0, 1)],
                                   v=[vtok(w, b) for w in (0, 1)], nkb=4, kb=causal_kb,
                                   b0=[384 - 128 * q_ for q_ in range(4)], gate=12 * g + 3 * r + b,
                                   first=b == 1, last=False, **CAUSAL))
                ab.append(dict(base, kind="cmp", k=[part(w, 22)[rows, KC:KC + 32] for w in (0, 1)],
                               v=[(lambda kb, w=w: part(w, 22)[0:32, VC:VC + P]) for w in (0, 1)], nkb=1,
                               kb=lambda kb: (0, SEQ), gate=12 * g + 3 * r, first=False, last=True))
        DQ, DK, DV, MQ, MK, MV, Y_DM, PT_DM, CQ, CKV = 0, 2, 4, 6, 8, 9, 12, (16, 24), 20, 22
        LQ, LK, LV, PT_L = 0, 24, 16, (8, 20)
        dm = []
        for h in range(4):
            for m in range(2):
                f = 64 * (h % 2) + 32 * m
                rows = slice(f, f + 32)
                dv = [cat(w, DV, 2).rearrange("p (t n) -> p t n", t=NT) for w in (0, 1)]
                dm.append(dict(kind="bias", q=[part(w, DQ + h // 2)[rows] for w in (0, 1)],
                               k=[part(w, DK + h // 2)[rows] for w in (0, 1)],
                               v=[(lambda kb, w=w, h=h, dv=dv: dv[w][:, kb, (h // 2) * P:(h // 2 + 1) * P]) for w in (0, 1)],
                               nkb=4, kb=causal_kb, b0=[384 - 128 * q_ for q_ in range(4)], scale=32 ** -0.5,
                               y=h, rows=slice(64 * (h % 2), 64 * (h % 2) + 64), ytile=Y_DM + h // 2, ztile=4 + h // 2,
                               bank=6 + h % 2, first=m == 1, last=m == 1, mode=("hold", "sub")[m], diff=True, **CAUSAL))
        for h in range(4):
            rows = slice(64 * (h % 2), 64 * (h % 2) + 64)
            mk = [cat(w, MK, 1).rearrange("p (t n) -> p t n", t=2) for w in (0, 1)]
            mv = [cat(w, MV, 1).rearrange("p (t n) -> p t n", t=2) for w in (0, 1)]
            dm.append(dict(kind="mem", q=[part(w, MQ + h // 2)[rows] for w in (0, 1)],
                           k=[mk[w][rows, h // 2, :] for w in (0, 1)],
                           v=[(lambda kb, w=w, h=h, mv=mv: mv[w][:, kb, (h // 2) * P:(h // 2 + 1) * P]) for w in (0, 1)],
                           nkb=2, kb=lambda kb: (0, SEQ), scale=64 ** -0.5, y=4 + h, rows=rows,
                           ytile=Y_DM + 2 + h // 2, ztile=6 + h // 2, bank=6 + h % 2, first=True, last=True, **MEMORY))
        mla = []
        for h in range(NH):
            lv = [cat(w, LV, 4).rearrange("p (t n) -> p t n", t=NT) for w in (0, 1)]
            mla.append(dict(kind="bias", q=[part(w, LQ + h)[0:96] for w in (0, 1)],
                            k=[part(w, LK + h)[0:96] for w in (0, 1)],
                            v=[(lambda kb, w=w, h=h, lv=lv: lv[w][:, kb, (h // 2) * P:(h // 2 + 1) * P]) for w in (0, 1)],
                            nkb=4, kb=causal_kb, b0=[384 - 128 * q_ for q_ in range(4)], scale=96 ** -0.5,
                            y=h, rows=slice(64 * (h % 2), 64 * (h % 2) + 64), ytile=LQ + h // 2, ztile=h // 2,
                            bank=6 + h % 2, first=True, last=True, **CAUSAL))
        for maps in (ab, dm, mla):
            n = 0
            for i, m in enumerate(maps):
                m["i"], m["prev"] = i, maps[i - 1]
                m["prev2"] = maps[i - 2]["n"] if i >= 2 else 0
                if m.get("mode") != "hold":
                    n += 1
                m["n"] = n
                m["yf"] = m["y"] - 3 if maps is dm else m["y"] + 1
                m["ylo"] = {1: 1, 3: 2}.get(m["y"], m["y"] - 1) if maps is dm else m["y"] + 1
                if m["kind"] != "cmp":
                    at, m["p"] = 0, []
                    for k0, nk in m["spans"]:
                        m["p"].append(at)
                        at += nk
        GROUP = {"ab": (ab, PT_AB), "dm": (dm, PT_DM), "mla": (mla, PT_L)}

        def prob(m):
            return PB[:, (m["i"] % 2) * 1280:(m["i"] % 2 + 1) * 1280]

        def bias_row(m):
            if "bias" in m:
                return FX[:, 2 + m["bias"] % 2, :]
            return TRI[:, :]

        def stat(m, k):
            return ST[:, m["i"] % 4, 4 * k:4 * k + 4]

        MAX, NMAX, SUM, SINK, WT = range(5)

        TOK = PB[:, 0:2048]
        HEADS = [
            dict(nt=2, n=512, parts=[(0, 4, 64, "mkn")], rope=None, turn=[(0, 128), (128, 128)], tiles=[MK], memk=True, v=(256, 256, MV)),
            dict(nt=4, n=416, parts=[(0, 1, 256, None), (256, 1, 128, None)], rope=None,
                 turn=[(0, 128), (128, 128), (256, 128)], tiles=[CQ, CQ + 1, CKV], gain=[("g_q2", 0), ("g_q2", 1), ("g_kv2", 0)]),
            dict(nt=4, n=512, parts=[(0, 8, 32, "dqn"), (256, 8, 32, "dkn")], rope=(0, 16, 32, 0),
                 turn=[(128 * j, 128) for j in range(4)], tiles=[DQ, DQ + 1, DK, DK + 1]),
            dict(nt=4, n=512, parts=[(256, 4, 64, "mqn")], rope=None, turn=[(256, 128), (384, 128)], tiles=[MQ, MQ + 1],
                 v=(0, 256, DV)),
        ] + [dict(nt=4, n=384, parts=[(0, 4, 96, g)], rope=(0, 4, 96, 64), turn=[(96 * j, 96) for j in range(4)],
                  tiles=[base + j for j in range(4)], kpart=kp)
             for g, base, kp in (("qn", LQ, False), ("qn", LQ + 4, False), ("kn", LK, True), ("kn", LK + 4, True))]

        def scratch(k):
            fx = FX[:, :, :].rearrange("p a b -> p (a b)")
            if k < 4:
                return fx[:, 0:2048], fx[:, 0:2048], fx[:, 2048:4096]
            return PB[:, 1536:3072], PB[:, 3072:3584], PB[:, 1536:2048]

        def turned_aps(m, pt, q, w):
            if m["kind"] == "cmp":
                return part(w, pt)[0:32, :], PS[0:32, 3, :]
            (b, o), (k0, nk) = m["place"][q], m["spans"][q]
            arena = ((BHI, BLO) if pt < 24 else (HHI, HLO))[w]
            t0, n = pt % 24 + k0 // P, nk // P
            return arena[:, t0:t0 + n, q * P:(q + 1) * P], PS[:, 3 + b, o:o + nk].rearrange("p (n c) -> p n c", n=n)

        HI_NORMS = {0: 0, 1: 8, 3: 16, 4: 24}

        block = ctx.enter_context(nc.Block())

        @block.sync
        def _(sp):
            for s in range(2):
                sp.dma_start(RAW[:, s, :], t["wstream"][s]).then_inc(raw_loaded[s], 16)
            with sp.Fori(1, NU // 2) as i:
                for s in range(2):
                    sp.wait_ge(split_lo, 2 * i + (s - 1))
                    sp.dma_start(RAW[:, s, :], t["wstream"][2 * i + s]).then_inc(raw_loaded[s], 16)

        @block.gpsimd
        def _(pool):
            pool.memset(IDN[:, :], 0.0)
            pool.memset(TRI[:, :], 0.0)
            pool.memset(BONE[:, :], 0.0)
            pool.memset(ONE[:, :], 1.0).then_inc(consts, 1)
            pool.wait_ge(consts, 1)
            pool.affine_select(out=IDN[:, :], in_=IDN[:, :], compare_op=ALU.not_equal, fill=1.0, base=0,
                               pattern=[[-1, P]], channel_multiplier=1)
            pool.affine_select(out=TRI[:, :], in_=TRI[:, :], compare_op=ALU.is_ge, fill=NEG, base=SEQ - P,
                               pattern=[[-1, SEQ]], channel_multiplier=1).then_inc(consts, 1)
            pool.wait_ge(consts, 2)
            pool.memset(BONE[0:64, 0:64], 1.0).then_inc(consts, 1)
            pool.wait_ge(consts, 3)
            pool.memset(BONE[64:128, 64:128], 1.0).then_inc(consts, 1)
            pool.wait_ge(consts, 4)
            with pool.Fori(0, NU // 2) as i:
                for s in range(2):
                    pool.wait_ge(split_hi, 2 * i + (s + 1))
                    pool.tensor_tensor(WLO[:, s, :], RAW[:, s, :], WHI[:, s, :].bitcast(F), ALU.subtract).then_inc(split_lo, 1)

        @block.scalar
        def _(act):
            chain = Chain(act, act_step)

            def stream(c, n=0, i=0):
                if isinstance(c, int) and n == 0 and c >= NU:
                    return
                act.wait_ge(raw_loaded[c % 2], 16 * (c // 2 + 1) + 8 * n * i)
                if c >= 2 or n:
                    act.wait_ge(unit_used, (c - 1) + n * i)
                act.activation(WHI[:, c % 2, :], RAW[:, c % 2, :], ACT.Copy).then_inc(split_hi, 1)

            def used(c, n=0, i=0):
                act.wait_ge(unit_used, (c + 1) + n * i)

            def norm_sums(k, src, width, ready):
                for kt in range(KT):
                    ready(kt)
                    if kt >= 2:
                        act.wait_ge(n_acc, 7 * k + max(1, kt - 2))
                    act.activation(PB[:, (kt % 2) * SEQ:(kt % 2) * SEQ + width], src(kt), ACT.Square).then_inc(n_sq, 1)

            def norm_root(k, width):
                act.wait_ge(n_rin, 2 * k + 2)
                act.activation(RSTD[:, 0:width], RSTD[:, 0:width], ACT.Sqrt).then_inc(n_rstd, 1)

            def norm_split(k, dst, width):
                for kt in range(KT):
                    act.wait_ge(n_t, 8 * k + kt + 1)
                    tt = PB[:, (4 + kt % 2) * SEQ:(4 + kt % 2) * SEQ + width]
                    act.activation(dst(kt), tt, ACT.Copy).then_inc(n_hi, 1)

            xv = t["xT"]
            act.dma_start(X[:, :, :], xv).then_inc(ld_x, 16)
            act.dma_start(CL[:, :], t["cols"]).then_inc(ld_small, 16)
            act.dma_start(RW[:, :], bass.AP(t["rows"].tensor, 0, [[0, P], [1, NROW]])).then_inc(ld_small, 16)
            act.dma_start(TBL[0:NBUCKET, :], t["table"]).then_inc(ld_small, 16)
            act.dma_start(POS[:, :], t["pos"]).then_inc(ld_small, 16)
            act.dma_start(FX[0:NBUCKET + 1, :, :].rearrange("p a b -> p (a b)")[:, 0:OH], t["onehot"]).then_inc(ld_oh, 16)
            stream(0)
            stream(1)
            act.wait_ge(ld_x, 16)
            norm_sums(0, lambda kt: X[:, kt, :], SEQ, lambda kt: None)
            norm_root(0, SEQ)
            norm_split(0, lambda kt: HHI[:, kt, :], SEQ)

            act.wait_ge(oh_mm, 1)
            for b in range(5):
                a, e = OH * b // 5, OH * (b + 1) // 5
                ins = act.activation(FX[0:16, :, :].rearrange("p a b -> p (a b)")[:, a:e], PS[0:16, 2 + b, 0:e - a], ACT.Copy)
            ins.then_inc(oh_ev, 1)
            act.wait_ge(oh_ev, 1)
            act.dma_start(tb_dram, FX[0:16, :, :].rearrange("p a b -> p (a b)")[:, 0:OH]).then_inc(st_rows, 16)
            act.wait_ge(ang_ready, 1)
            act.activation(COS[:, :, 16:32], COS[:, :, 16:32], ACT.Sin)
            act.activation(SIN[:, :, 16:32], SIN[:, :, 16:32], ACT.Sin).then_inc(sin_ready, 1)

            act.dma_start(W2, t["w2"]).then_inc(ld_w2, 16)

            u = UNIT["proj"]

            def proj_epilogue(c, n, i, tile):
                used(c, n, i)
                act.activation(tile, PS[:, c % 2, :], ACT.Copy).then_inc(proj_hi, 1)
                stream(c + 2, n, i)

            for c in range(2):
                proj_epilogue(u + c, 0, 0, hi(c))
            with act.Fori(1, 5) as i:
                for s in range(2):
                    proj_epilogue(u + s, 2, i, BHI[:, bass.ds(2 * i + s, 1), :].rearrange("p a b -> p (a b)"))
            proj_epilogue(u + 10, 0, 0, hi(10))
            for c in (11, 12):
                stream(u + c + 2)

            def bias_load(y):
                h = (y % 8 // 2) + 4 * (y % 2) + (8 if y >= 8 else 0)
                n, src = (256, bias_a) if y < 8 else (SEQ, bias_b)
                act.dma_start(FX[:, 2 + y % 2, 0:n], src[h % 8]).then_inc(ld_bias[y % 2], 16)

            act.wait_ge(st_rows, 16)
            for dst, h0, off, n in ((bias_a, 0, 0, 256), (bias_b, 8, OH_A, SEQ)):
                src = bass.AP(tb_dram.tensor, h0 * OH + off + P - 1, [[OH, NH], [-1, P], [1, n]])
                act.dma_start(dst, src).then_inc(spread, 16)
            for qt in range(NT):
                for pg in range(8):
                    src = bass.AP(tb_dram.tensor, 8 * OH + OH_A + OH_B + 15 * CMP_A + 33 - 8 * qt - pg,
                                  [[OH, NH], [-CMP_A, 16], [1, N_CMP]])
                    act.dma_start(bias_c[:, 16 * pg:16 * pg + 16, qt, :], src).then_inc(spread, 16)

            u = UNIT["vtok"]
            for c in range(4):
                if c == 3:
                    used(u + 3)
                    vh = cat(0, V_AT, 3).rearrange("p (t n) -> p t n", t=NT)
                    for tk in range(NT):
                        act.activation(vh[:, tk, :], PS[:, 2 + tk, 0:384], ACT.Copy).then_inc(v_hi, 1)
                    for tk in range(NT):
                        ins = act.activation(GATE[:, tk, :], PS[:, 2 + tk, 384:408], ACT.Sigmoid)
                    ins.then_inc(v_hi, 1)
                stream(u + c + 2)

            for w in range(2):
                act.wait_ge(cb_built, w + 1)
                act.activation(cat(0, 14 + 4 * w, 4), PB[:, 0:2048], ACT.Copy).then_inc(cb_hi, 1)
            u = UNIT["cmp"]
            for c in range(8):
                stream(u + c + 2)
                if c == 0:
                    act.wait_ge(spread, 16 * 34)
                    act.wait_ge(tbl_ready, 2)
                    for h in range(NH):
                        dst = FX[:, 4 + h // 4, (h % 4) * P:(h % 4 + 1) * P].rearrange("p (q c) -> p q c", q=NT)[:, :, 0:N_CMP]
                        act.dma_start(dst, bias_c[h]).then_inc(ld_cmp, 16)
                    bias_load(0)
                    bias_load(1)
                if c % 4 == 3:
                    used(u + c)
                    w = c // 4
                    act.activation(FX[:, 6, 256 * w:256 * w + 256], PS[:, 6 + w, 0:256], ACT.Gelu_apprx_tanh).then_inc(gelu_done, 1)
            act.wait_ge(gelu_t, 1)
            act.activation(FX[:, 7, :], PS[:, 0, :], ACT.Copy).then_inc(gelu_copied, 1)
            act.wait_ge(cmp_mm, 1)
            for g in range(2):
                act.activation(hi(22)[64 * g:64 * g + 64, KC:KC + 32], PS[64 * g:64 * g + 64, 1, 64 * g:64 * g + 32], ACT.Copy)
            act.activation(hi(22)[0:32, VC:VC + P], PS[0:32, 2, 0:P], ACT.Copy).then_inc(cmp_hi, 1)

            def attention(name):
                maps, pts = GROUP[name]
                A = ATT[name]
                for i in range(-1, len(maps) + 2):
                    if 0 <= i - 1 < len(maps) and maps[i - 1].get("mode") != "hold":
                        m = maps[i - 1]
                        act.wait_ge(A["turned"], m["n"])
                        if m["n"] > 2:
                            act.wait_ge(A["pv"], m["n"] - 2)
                        pt = pts[m["n"] % 2]
                        for q in range(1 if m["kind"] == "cmp" else NT):
                            ins = act.activation(*turned_aps(m, pt, q, 0), ACT.Copy)
                        ins.then_inc(A["p_hi"], 1)
                    if i + 1 < len(maps):
                        m = maps[i + 1]
                        pr = prob(m)
                        act.wait_ge(A["biased"], m["i"] + 1)
                        if m["kind"] == "cmp":
                            ins = act.activation(pr[:, 0:P], pr[:, 0:P], ACT.Exp, scale=m["scale"])
                        else:
                            if m.get("sink"):
                                act.wait_ge(A["biased"], m["i"] + 1)
                                for q in range(NT):
                                    act.activation(stat(m, SINK)[:, q:q + 1], row("sinks", 8)[:, m["h"]:m["h"] + 1],
                                                   ACT.Exp, bias=stat(m, NMAX)[:, q:q + 1])
                            for q in range(NT):
                                nk = m["spans"][q][1]
                                dst = pr[:, m["p"][q]:m["p"][q] + nk]
                                b, o = m["place"][q]
                                if m["kind"] == "mem":
                                    src, sc = PS[:, b, o:o + nk], m["scale"]
                                else:
                                    src, sc = dst, 1.0
                                ins = act.activation(dst, src, ACT.Exp, bias=stat(m, NMAX)[:, q:q + 1], scale=sc,
                                                     accum_out=stat(m, SUM)[:, q:q + 1])
                        ins.then_inc(A["exped"], 1)
                        if "bias" in m and m["last"] and m["bias"] + 1 < 16 and m["bias"] >= 1:
                            act.wait_ge(A["biased"], m["i"])
                            bias_load(m["bias"] + 1)
                    if 0 <= i - 2 < len(maps) and maps[i - 2]["last"]:
                        m = maps[i - 2]
                        rows, yt = m["rows"], hi(m["ytile"])
                        act.wait_ge(A["pv"], m["n"])
                        if name == "ab":
                            act.activation(yt[rows, :], PS[rows, m["bank"], :], ACT.Copy).then_inc(A["y_hi"], 1)
                        elif m.get("diff"):
                            j = m["y"] // 2
                            if m["y"] == 2:
                                act.wait_ge(A["y_lo"], 1)
                            act.activation(YT[rows, :], PS[rows, m["bank"], :], ACT.Copy).then_inc(A["y_hi"], 1)
                            if m["bank"] == 7:
                                act.wait_ge(A["y_hi"], m["y"] + 1)
                                act.activation(YSQ, YT, ACT.Square).then_inc(dm_sq, 1)
                                act.wait_ge(dm_rin, 2 * j + 2)
                                act.activation(YSQ, YSQ, ACT.Sqrt).then_inc(dm_rstd, 1)
                                act.wait_ge(dm_y, j + 1)
                                act.activation(yt, YT, ACT.Copy).then_inc(dm_hi, 1)
                        else:
                            act.wait_ge(A["y_f"], m["yf"])
                            act.activation(yt[rows, :], YT[rows, :], ACT.Copy).then_inc(A["y_hi"], 1)

            attention("ab")

            u = UNIT["merge"]
            def merge(i):
                for s in range(2):
                    for e in range(2):
                        c = u + 3 * s + e
                        used(c, 6, i)
                        if isinstance(i, int) and i == 0:
                            pass
                        else:
                            act.wait_ge(merge_dve, 8 * i + (4 * s - 8 + 2 + 1))
                        act.activation(FX[:, 2 * e + s, :], PS[:, 4 * s + e, :], ACT.Sigmoid).then_inc(merge_act, 1)
                        stream(c + 2, 6, i)
                    c = u + 3 * s + 2
                    stream(c + 2, 6, i)
                    act.wait_ge(merge_dve, 8 * i + (4 * s + 3))
                    dst = hi(14 + s) if isinstance(i, int) else \
                        BHI[:, bass.ds(2 * i + (14 + s), 1), :].rearrange("p a b -> p (a b)")
                    act.activation(dst, FX[:, 4 + s, :], ACT.Copy).then_inc(merge_act, 1)
            merge(0)
            with act.Fori(1, 4) as i:
                merge(i)

            def plain_stream(name):
                c0, n = UNIT[name], dict(_PLAN)[name]
                assert n % 2 == 0
                with act.Fori(0, n // 2) as i:
                    for s in range(2):
                        stream(c0 + s + 2, 2, i)

            plain_stream("wout")
            norm_sums(1, lambda kt: X[:, kt, :], SEQ, lambda kt: act.wait_ge(x1_done, kt + 1))
            norm_root(1, SEQ)
            norm_split(1, lambda kt: HHI[:, kt, :], SEQ)

            u = UNIT["ffn"]
            def ffn(i):
                for s in range(2):
                    pair = 2 * i + s
                    for e in range(2):
                        c = u + 2 * s + e
                        used(c, 4, i)
                        if not isinstance(i, int):
                            act.wait_ge(ffn_dve, 12 * i + (6 * s - 12 + 5))
                        at = COL["conv"] + 4 * e + 8 * s
                        cv = CL[:, at:at + 4] if isinstance(i, int) else CL[:, bass.ds(16 * i + at, 4)]
                        act.activation(FX[:, 2 * e + s, :], PS[:, 2 * e + s, :], ACT.Identity,
                                       bias=cv[:, 3:4], scale=cv[:, 2:3]).then_inc(ffn_act, 1)
                        stream(c + 2, 4, i)
                    act.wait_ge(ffn_dve, 12 * i + (6 * s + 4))
                    act.activation(FX[:, 4 + s, :], FX[:, 2 + s, :], ACT.Silu).then_inc(ffn_act, 1)
                    act.wait_ge(ffn_dve, 12 * i + (6 * s + 5))
                    dst = hi(s) if isinstance(i, int) else BHI[:, bass.ds(pair, 1), :].rearrange("p a b -> p (a b)")
                    act.activation(dst, FX[:, 6 + s, :], ACT.Copy).then_inc(ffn_act, 1)
            ffn(0)
            with act.Fori(1, NF // 2) as i:
                ffn(i)

            act.wait_ge(ffn_dve, 6 * NF)
            act.dma_start(FX[:, 0:4, :].rearrange("p a b -> p (a b)"), t["memT"]).then_inc(ld_mem, 16)
            plain_stream("down")
            memx = FX[:, 0:4, :].rearrange("p a b -> p (a b)").rearrange("p (k n) -> p k n", k=KT)
            norm_sums(2, lambda kt: X[:, kt, :], SEQ, lambda kt: act.wait_ge(x2_done, kt + 1))
            norm_root(2, SEQ)
            norm_sums(3, lambda kt: X[:, kt, :], SEQ, lambda kt: act.wait_ge(n_t, 16 + kt + 1))
            norm_root(3, SEQ)
            norm_split(3, lambda kt: HHI[:, kt, :], SEQ)
            act.wait_ge(ld_mem, 16)
            act.wait_ge(n_lo, 24)
            norm_sums(4, lambda kt: memx[:, kt, :], 256, lambda kt: None)
            norm_root(4, 256)
            mn = cat(0, 16, 4).rearrange("p (k n) -> p k n", k=KT)
            norm_split(4, lambda kt: mn[:, kt, :], 256)

            def head_evac(k):
                h = HEADS[k]
                if k:
                    act.wait_ge(h_tr, k)
                for tk in range(h["nt"]):
                    if h.get("kpart"):
                        dst = TOK[:, 0:1536].rearrange("p (t h e) -> p t h e", t=NT, h=4)[:, tk]
                        act.activation(dst[:, :, 0:64], PS[:, tk, 0:256].rearrange("p (h e) -> p h e", h=4), ACT.Copy)
                        kr = KR[:, tk, :]
                        ins = act.activation(dst[:, :, 64:96], kr[:, None, :].broadcast_to([P, 4, 32]), ACT.Copy)
                    else:
                        ins = act.activation(TOK[:, tk * h["n"]:(tk + 1) * h["n"]], PS[:, tk, 0:h["n"]], ACT.Copy)
                ins.then_inc(h_tok, 1)

            def head_square(k):
                h = HEADS[k]
                act.wait_ge(h_tok, k + 1)
                n = h["nt"] * h["n"]
                act.activation(scratch(k)[0][:, 0:n], TOK[:, 0:n], ACT.Square).then_inc(h_sq, 1)
                if "v" in h:
                    o, w, tile = h["v"]
                    v = cat(0, tile, h["nt"] * w // SEQ).rearrange("p (t n) -> p t n", t=h["nt"])
                    src = TOK[:, 0:n].rearrange("p (t n) -> p t n", t=h["nt"])[:, :, o:o + w]
                    act.activation(v, src, ACT.Copy).then_inc(h_v, 1)

            def head_root(k):
                act.wait_ge(h_rin, k + 1)
                act.activation(SS[:, :], SS[:, :], ACT.Sqrt).then_inc(h_rs, 1)

            def head_hi(k):
                h = HEADS[k]
                act.wait_ge(h_tr, k + 1)
                for j, tile in enumerate(h["tiles"]):
                    w = h["turn"][0][1]
                    if h.get("memk"):
                        ins = act.activation(hi(tile), PS[:, 4, :], ACT.Copy)
                    elif "gain" in h:
                        ins = act.activation(hi(tile), PS[:, 4 + j, :], ACT.Copy, scale=col(*h["gain"][j]))
                    else:
                        ins = act.activation(hi(tile)[0:w, :], PS[0:w, 4 + j, :], ACT.Copy)
                ins.then_inc(h_hi, 1)

            u = UNIT["mem"]
            for c in range(4):
                stream(u + c + 2)
            used(u + 3)
            head_evac(0)
            head_square(0)
            for k in range(1, 4):
                u = UNIT["tok2"] + 4 * (k - 1)
                stream(u + 2)
                head_root(k - 1)
                for c in range(1, 4):
                    stream(u + c + 2)
                used(u + 3)
                head_evac(k)
                head_hi(k - 1)
                head_square(k)
            head_root(3)
            u = UNIT["z"]
            act.wait_ge(h_nrm, 4)
            for c in range(8):
                used(u + c)
                act.activation(FX[:, c, :], PS[:, c % 2, :], ACT.Silu).then_inc(z_done, 1)
                stream(u + c + 2)
            head_hi(3)
            act.wait_ge(lam_sum, 1)
            act.activation(LAM[:, 2:4], LAM[:, 0:2], ACT.Exp).then_inc(lam_exp, 1)
            attention("dm")

            u = UNIT["uq"]
            stream(u + 2)
            used(u)
            head_evac(4)
            head_square(4)
            stream(u + 3)
            head_root(4)
            used(u + 1)
            head_evac(5)
            head_hi(4)
            head_square(5)
            head_root(5)
            for k in (6, 7):
                act.wait_ge(k_mm, k - 5)
                head_evac(k)
                head_hi(k - 1)
                head_square(k)
                head_root(k)
            used(UNIT["ukv"])
            vh = cat(0, LV, 4).rearrange("p (t n) -> p t n", t=NT)
            for tk in range(NT):
                act.activation(vh[:, tk, :], PS[:, tk, :], ACT.Copy).then_inc(vm_hi, 1)
            head_hi(7)
            stream(UNIT["ukv"] + 2)
            attention("mla")
            u = UNIT["wout2"]
            with act.Fori(0, 3) as i:
                for s in range(2):
                    stream(u + 2 + s, 2, i)
            for n in range(KT):
                act.wait_ge(y_out, n + 1)
                act.dma_start(out[:, n, :], X[:, n, :]).then_inc(stored, 16)
            act.wait_ge(stored, 16 * KT)

        @block.vector
        def _(dve):
            chain = Chain(dve, dve_step)
            link = chain.link

            def norm_sum(k, width):
                acc = PB[:, 2 * SEQ:2 * SEQ + width]
                for kt in range(1, KT):
                    dve.wait_ge(n_sq, 8 * k + kt + 1)
                    if kt > 1:
                        dve.wait_ge(n_acc, 7 * k + kt - 1)
                    a = PB[:, 0:width] if kt == 1 else acc
                    dve.tensor_tensor(acc, a, PB[:, (kt % 2) * SEQ:(kt % 2) * SEQ + width], ALU.add).then_inc(n_acc, 1)

            def norm_inverse(k, width):
                dve.wait_ge(n_tot, k + 1)
                dve.tensor_scalar(RSTD[:, 0:width], PS[:, 7, 0:width], 1.0 / D, EPS, ALU.mult, ALU.add).then_inc(n_rin, 1)
                dve.wait_ge(n_rin, 2 * k + 1)
                dve.reciprocal(RSTD[:, 0:width], RSTD[:, 0:width]).then_inc(n_rin, 1)

            def norm_apply(k, src, gain, width, hi_of, lo_of, dst=None):
                base = HI_NORMS.get(k)
                dve.wait_ge(n_rstd, k + 1)

                def low(kt):
                    dve.wait_ge(n_hi, base + kt + 1)
                    tt = PB[:, (4 + kt % 2) * SEQ:(4 + kt % 2) * SEQ + width]
                    dve.tensor_tensor(lo_of(kt), tt, hi_of(kt).bitcast(F), ALU.subtract).then_inc(n_lo, 1)

                for kt in range(KT):
                    tt = dst(kt) if dst else PB[:, (4 + kt % 2) * SEQ:(4 + kt % 2) * SEQ + width]
                    if kt >= 2 and not dst:
                        dve.wait_ge(n_lo, base + kt - 1)
                    dve.scalar_tensor_tensor(out=tt, in0=src(kt), scalar=col(gain, kt), in1=RSTD[:, 0:width],
                                             op0=ALU.mult, op1=ALU.mult).then_inc(n_t, 1)
                    if kt >= 1 and not dst:
                        low(kt - 1)
                if not dst:
                    low(KT - 1)

            xt = lambda kt: X[:, kt, :]
            norm_sum(0, SEQ)
            dve.wait_ge(ld_small, 64)
            norm_inverse(0, SEQ)
            norm_apply(0, xt, "g_mix", SEQ, lambda kt: HHI[:, kt, :], lambda kt: HLO[:, kt, :])

            dve.memset(TBL[NBUCKET:NBUCKET + 1, :], NEG)
            link(dve.tensor_scalar(TBL[0:NBUCKET, :], TBL[0:NBUCKET, :], 8.0, None, ALU.mult))
            dve.memset(MSK[:, :], 1.0).then_inc(tbl_ready, 1)
            link(dve.tensor_copy(KR[:, :, 0], POS[:, :]))
            ang = COS[:, :, 0:16]
            link(dve.tensor_tensor(ang, KR[:, :, 0:1].broadcast_to([P, NT, 16]),
                                   row("inv", 16)[:, None, :].broadcast_to([P, NT, 16]), ALU.mult))
            magic = 1.5 * 2.0 ** 23
            c1, c2, c3 = 6.28125, float(np.float32(2 * math.pi - 6.28125)), 0.0
            c3 = 2 * math.pi - c1 - c2
            for dst, shift in ((COS, 0.25), (SIN, 0.0)):
                turns, r = KR[:, :, 16:32], dst[:, :, 16:32]
                link(dve.tensor_scalar(turns, ang, 1.0 / (2 * math.pi), shift, ALU.mult, ALU.add))
                link(dve.tensor_scalar(turns, turns, magic, magic, ALU.add, ALU.subtract))
                link(dve.scalar_tensor_tensor(out=r, in0=turns, scalar=-c1, in1=ang, op0=ALU.mult, op1=ALU.add))
                for c in (c2, c3):
                    link(dve.scalar_tensor_tensor(out=r, in0=turns, scalar=-c, in1=r, op0=ALU.mult, op1=ALU.add))
                link(dve.tensor_scalar(r, r, shift * 2 * math.pi, 3.1415925, ALU.add, ALU.min))
                link(dve.tensor_scalar(r, r, -3.1415925, None, ALU.max))
            dve.memset(SS[:, :], 1.0).then_inc(ang_ready, 1)
            dve.wait_ge(sin_ready, 1)
            link(dve.tensor_copy(COS[:, :, 0:16], COS[:, :, 16:32]))
            link(dve.tensor_scalar(SIN[:, :, 0:16], SIN[:, :, 16:32], -1.0, None, ALU.mult))

            def low_from_psum(dst_lo, dst_hi, src):
                return dve.tensor_tensor(dst_lo, src, dst_hi.bitcast(F), ALU.subtract)

            for c in range(2):
                dve.wait_ge(proj_hi, c + 1)
                low_from_psum(lo(c), hi(c), PS[:, c, :]).then_inc(proj_out, 1)
            with dve.Fori(1, 5) as i:
                for s in range(2):
                    dve.wait_ge(proj_hi, 2 * i + (s + 1))
                    low_from_psum(BLO[:, bass.ds(2 * i + s, 1), :].rearrange("p a b -> p (a b)"),
                                  BHI[:, bass.ds(2 * i + s, 1), :].rearrange("p a b -> p (a b)"),
                                  PS[:, s, :]).then_inc(proj_out, 1)
            dve.wait_ge(proj_hi, 11)
            low_from_psum(lo(10), hi(10), PS[:, 0, :]).then_inc(proj_out, 1)
            dve.wait_ge(st_rows, 16)
            for c in (11, 12):
                dve.wait_ge(unit_used, UNIT["proj"] + c + 1)
                dve.tensor_copy(FX[:, c - 11, :], PS[:, c % 2, :]).then_inc(proj_out, 1)
            link(dve.memset(MSK[0:31, 0:1], 0.0))
            dve.memset(FX[:, 4:6, :], NEG * 8).then_inc(tbl_ready, 1)

            vh, vl = [cat(w, V_AT, 3).rearrange("p (t n) -> p t n", t=NT) for w in (0, 1)]
            for tk in range(NT):
                dve.wait_ge(v_hi, NT + 1)
                low_from_psum(vl[:, tk, :], vh[:, tk, :], PS[:, 2 + tk, 0:384]).then_inc(v_lo, 1)

            cb = PB[:, 0:2048].rearrange("p (t g i) -> p t g i", t=16, g=2)
            dve.wait_ge(proj_out, 13)
            dve.wait_ge(n_lo, 8)
            link(dve.memset(PB[:, 0:2048], 0.0))
            for w in range(2):
                if w:
                    dve.wait_ge(cb_lo, 1)
                for g in range(2):
                    rows = slice(64 * g, 64 * g + 64)
                    for par in range(2):
                        src = FX[rows, w, par:par + 1]
                        src = bass.AP(src.tensor, src.offset, [list(src.ap[0]), [2, 16], [16, N_CMP]])
                        pos = CL[rows, COL[("pos_k", "pos_v")[w]] + par:COL[("pos_k", "pos_v")[w]] + 32:2]
                        ins = dve.tensor_tensor(cb[64 * par:64 * par + 64, :, g, 0:N_CMP], src,
                                                pos[:, :, None].broadcast_to([64, 16, N_CMP]), ALU.add)
                ins.then_inc(cb_built, 1)
                dve.wait_ge(cb_hi, w + 1)
                dve.tensor_tensor(cat(1, 14 + 4 * w, 4), PB[:, 0:2048], cat(0, 14 + 4 * w, 4).bitcast(F),
                                  ALU.subtract).then_inc(cb_lo, 1)
            dve.wait_ge(cmp_hi, 1)
            for g in range(2):
                low_from_psum(lo(22)[64 * g:64 * g + 64, KC:KC + 32], hi(22)[64 * g:64 * g + 64, KC:KC + 32],
                              PS[64 * g:64 * g + 64, 1, 64 * g:64 * g + 32])
            low_from_psum(lo(22)[0:32, VC:VC + P], hi(22)[0:32, VC:VC + P], PS[0:32, 2, 0:P]).then_inc(cmp_lo, 1)

            def biased(A, m):
                pr = prob(m)
                dve.wait_ge(A["scores"], m["i"] + 1)
                if m["i"] and m["prev"].get("mode") == "sub":
                    dve.wait_ge(A["normed"], m["prev"]["n"])
                if m["prev2"]:
                    dve.wait_ge(A["turned"], m["prev2"])
                if m["kind"] == "cmp":
                    p4 = pr[:, 0:P].rearrange("p (q c) -> p q c", q=NT)
                    bc = FX[:, 4:6, :].rearrange("p a b -> p (a b)").rearrange("p (h q c) -> p h q c", h=NH, q=NT)
                    if m["bias"] == 8:
                        dve.wait_ge(ld_cmp, 16 * NH)
                    link(dve.tensor_tensor(p4, PS[:, 2, 0:P].rearrange("p (q c) -> p q c", q=NT), bc[:, m["h"]], ALU.add))
                    link(dve.tensor_reduce(stat(m, MAX), p4, AX.X, ALU.max))
                    dve.tensor_tensor(p4, p4, stat(m, MAX)[:, :, None].broadcast_to([P, NT, 32]),
                                      ALU.subtract).then_inc(A["biased"], 1)
                    return
                if m["kind"] == "mem":
                    for b in range(2):
                        ins = dve.tensor_reduce(stat(m, MAX)[:, 2 * b:2 * b + 2],
                                                PS[:, b, :].rearrange("p (q c) -> p q c", q=2), AX.X, ALU.max)
                    link(ins)
                    dve.tensor_scalar(stat(m, NMAX), stat(m, MAX), -m["scale"], None, ALU.mult).then_inc(A["biased"], 1)
                    return
                if "bias" in m and m["first"]:
                    y = m["bias"]
                    dve.wait_ge(ld_bias[y % 2], 16 * (y // 2 + 1))
                for q in range(NT):
                    (b, o), (_, nk) = m["place"][q], m["spans"][q]
                    init = row("sinks", 8)[:, m["h"]:m["h"] + 1] if m.get("sink") else -3e38
                    ins = dve.tensor_tensor_reduce(pr[:, m["p"][q]:m["p"][q] + nk], PS[:, b, o:o + nk],
                                                   bias_row(m)[:, m["b0"][q]:m["b0"][q] + nk], m["scale"], init,
                                                   ALU.add, ALU.max, stat(m, MAX)[:, q:q + 1])
                link(ins)
                dve.tensor_scalar(stat(m, NMAX), stat(m, MAX), -1.0, None, ALU.mult).then_inc(A["biased"], 1)

            def normed(A, m):
                pr = prob(m)
                dve.wait_ge(A["exped"], m["i"] + 1)
                p4 = pr[:, 0:P].rearrange("p (q c) -> p q c", q=NT)
                if m["kind"] == "cmp":
                    link(dve.tensor_reduce(stat(m, SUM), p4, AX.X, ALU.add))
                if m.get("sink"):
                    link(dve.tensor_tensor(stat(m, SUM), stat(m, SUM), stat(m, SINK), ALU.add))
                link(dve.reciprocal(stat(m, WT), stat(m, SUM)))
                if "gate" in m:
                    link(dve.tensor_tensor(stat(m, WT), stat(m, WT), GATE[:, :, m["gate"]], ALU.mult))
                if m.get("mode") == "sub":
                    link(dve.tensor_tensor(stat(m, WT), stat(m, WT), LAM[:, 0:1].broadcast_to([P, NT]), ALU.mult))
                if m["kind"] == "cmp":
                    link(dve.tensor_tensor(stat(m, WT), stat(m, WT), MSK[:, :], ALU.mult))
                    dve.tensor_tensor(p4, p4, stat(m, WT)[:, :, None].broadcast_to([P, NT, 32]), ALU.mult).then_inc(A["normed"], 1)
                    return
                for q in range(NT):
                    ap = pr[:, m["p"][q]:m["p"][q] + m["spans"][q][1]]
                    w = stat(m, WT)[:, q:q + 1]
                    if m.get("mode") == "sub":
                        o = PB[:, (1 - m["i"] % 2) * 1280:(2 - m["i"] % 2) * 1280][:, m["p"][q]:m["p"][q] + m["spans"][q][1]]
                        ins = dve.scalar_tensor_tensor(out=ap, in0=ap, scalar=w, in1=o, op0=ALU.mult, op1=ALU.add)
                    else:
                        ins = dve.tensor_scalar(ap, ap, w, None, ALU.mult)
                if m.get("mode") == "hold":
                    link(ins)
                else:
                    ins.then_inc(A["normed"], 1)

            def attention(name):
                maps, pts = GROUP[name]
                A = ATT[name]
                for i in range(-1, len(maps) + 2):
                    steps = [(biased, i + 1), (normed, i)]
                    for f, j in (steps[::-1] if name == "dm" else steps):
                        if 0 <= j < len(maps):
                            f(A, maps[j])
                    if 0 <= i - 1 < len(maps) and maps[i - 1].get("mode") != "hold":
                        m = maps[i - 1]
                        dve.wait_ge(A["p_hi"], m["n"])
                        pt = pts[m["n"] % 2]
                        for q in range(1 if m["kind"] == "cmp" else NT):
                            dst, src = turned_aps(m, pt, q, 1)
                            ins = low_from_psum(dst, turned_aps(m, pt, q, 0)[0], src)
                        ins.then_inc(A["p_lo"], 1)
                    if 0 <= i - 2 < len(maps) and maps[i - 2]["last"]:
                        m = maps[i - 2]
                        rows, yh, yl = m["rows"], hi(m["ytile"]), lo(m["ytile"])
                        ps = PS[rows, m["bank"], :]
                        if name == "ab":
                            dve.wait_ge(A["y_hi"], m["y"] + 1)
                            low_from_psum(yl[rows, :], yh[rows, :], ps).then_inc(A["y_lo"], 1)
                        elif m.get("diff"):
                            if m["bank"] == 7:
                                j = m["y"] // 2
                                dve.wait_ge(dm_tot, j + 1)
                                dve.tensor_scalar(YSQ, PS[:, 7, :], 1.0 / 64, EPS, ALU.mult, ALU.add).then_inc(dm_rin, 1)
                                dve.wait_ge(dm_rin, 2 * j + 1)
                                dve.reciprocal(YSQ, YSQ).then_inc(dm_rin, 1)
                                dve.wait_ge(dm_rstd, j + 1)
                                link(dve.scalar_tensor_tensor(out=YT, in0=YT, scalar=col("subln"), in1=YSQ,
                                                              op0=ALU.mult, op1=ALU.mult))
                                dve.scalar_tensor_tensor(out=YT, in0=YT, scalar=1.0 - LAM_INIT, in1=FX[:, m["ztile"], :],
                                                         op0=ALU.mult, op1=ALU.mult).then_inc(dm_y, 1)
                                dve.wait_ge(dm_hi, j + 1)
                                low_from_psum(yl, yh, YT).then_inc(A["y_lo"], 1)
                        else:
                            dve.wait_ge(A["pv"], m["n"])
                            dve.tensor_tensor(YT[rows, :], ps, FX[rows, m["ztile"], :], ALU.mult).then_inc(A["y_f"], 1)
                            dve.wait_ge(A["y_hi"], m["y"] + 1)
                            low_from_psum(yl[rows, :], yh[rows, :], YT[rows, :]).then_inc(A["y_lo"], 1)

            attention("ab")

            def merge(i):
                for s in range(2):
                    d = 8 * i + 4 * s
                    dve.wait_ge(unit_used, UNIT["merge"] + 6 * i + (3 * s + 3))
                    for e in range(2):
                        dve.wait_ge(merge_act, 6 * i + (3 * s + 1 + e))
                        dve.tensor_tensor(FX[:, 4 + 2 * e + s, :], PS[:, 4 * s + 2 + e, :], FX[:, 2 * e + s, :],
                                          ALU.mult).then_inc(merge_dve, 1)
                    dve.wait_ge(merge_dve, d + 2)
                    dve.tensor_tensor(FX[:, 4 + s, :], FX[:, 4 + s, :], FX[:, 6 + s, :], ALU.add).then_inc(merge_dve, 1)
                    dve.wait_ge(merge_act, 6 * i + (3 * s + 3))
                    if isinstance(i, int):
                        h_, l_ = hi(14 + s), lo(14 + s)
                    else:
                        h_, l_ = [a[:, bass.ds(2 * i + (14 + s), 1), :].rearrange("p a b -> p (a b)") for a in (BHI, BLO)]
                    low_from_psum(l_, h_, FX[:, 4 + s, :]).then_inc(merge_dve, 1)
            merge(0)
            with dve.Fori(1, 4) as i:
                merge(i)

            def residual(name, per, done):
                def one(i):
                    for s in range(2):
                        dve.wait_ge(unit_used, UNIT[name] + 2 * per * i + per * (s + 1))
                        x = X[:, s, :] if isinstance(i, int) else X[:, bass.ds(2 * i + s, 1), :].rearrange("p a b -> p (a b)")
                        dve.tensor_tensor(x, PS[:, s, :], x, ALU.add).then_inc(done, 1)
                one(0)
                with dve.Fori(1, 4) as i:
                    one(i)

            residual("wout", 1, x1_done)
            norm_sum(1, SEQ)
            norm_inverse(1, SEQ)
            norm_apply(1, xt, "g_ffn", SEQ, lambda kt: HHI[:, kt, :], lambda kt: HLO[:, kt, :])

            def ffn(i):
                for s in range(2):
                    d = 12 * i + 6 * s
                    for tap in (1, 0):
                        for e in range(2):
                            at = COL["conv"] + 4 * e + 8 * s
                            cv = CL[:, at:at + 4] if isinstance(i, int) else CL[:, bass.ds(16 * i + at, 4)]
                            if tap == 1:
                                dve.wait_ge(ffn_act, 8 * i + (4 * s + 1 + e))
                            else:
                                dve.wait_ge(ffn_dve, d + (1 + e))
                            sh = 2 - tap
                            y = FX[:, 2 * e + s, sh:SEQ]
                            dve.scalar_tensor_tensor(out=y, in0=PS[:, 2 * e + s, 0:SEQ - sh], scalar=cv[:, tap:tap + 1],
                                                     in1=y, op0=ALU.mult, op1=ALU.add).then_inc(ffn_dve, 1)
                    dve.wait_ge(ffn_act, 8 * i + (4 * s + 3))
                    dve.tensor_tensor(FX[:, 6 + s, :], FX[:, 4 + s, :], FX[:, s, :], ALU.mult).then_inc(ffn_dve, 1)
                    dve.wait_ge(ffn_act, 8 * i + (4 * s + 4))
                    if isinstance(i, int):
                        h_, l_ = hi(s), lo(s)
                    else:
                        h_, l_ = [a[:, bass.ds(2 * i + s, 1), :].rearrange("p a b -> p (a b)") for a in (BHI, BLO)]
                    low_from_psum(l_, h_, FX[:, 6 + s, :]).then_inc(ffn_dve, 1)
            ffn(0)
            with dve.Fori(1, NF // 2) as i:
                ffn(i)

            residual("down", 3, x2_done)
            norm_sum(2, SEQ)
            norm_inverse(2, SEQ)
            norm_apply(2, xt, "g_final", SEQ, None, None, dst=xt)
            norm_sum(3, SEQ)
            norm_inverse(3, SEQ)
            norm_apply(3, xt, "g_2", SEQ, lambda kt: HHI[:, kt, :], lambda kt: HLO[:, kt, :])
            memx = FX[:, 0:4, :].rearrange("p a b -> p (a b)").rearrange("p (k n) -> p k n", k=KT)
            mh, ml = [cat(w, 16, 4).rearrange("p (k n) -> p k n", k=KT) for w in (0, 1)]
            norm_sum(4, 256)
            norm_inverse(4, 256)
            norm_apply(4, lambda kt: memx[:, kt, :], "g_mem", 256, lambda kt: mh[:, kt, :], lambda kt: ml[:, kt, :])

            def head_norm(k):
                h = HEADS[k]
                nt, n = h["nt"], h["n"]
                tok = TOK[:, 0:nt * n].rearrange("p (t n) -> p t n", t=nt)
                sq, ra, rb = scratch(k)
                dve.wait_ge(h_sq, k + 1)
                at = 0
                groups = []
                for o, g, w, gain in h["parts"]:
                    ss = SS[:, at:at + nt * g]
                    if g == 1:
                        src = sq[:, 0:nt * n].rearrange("p (t n) -> p t n", t=nt)[:, :, o:o + w]
                    else:
                        src = sq[:, 0:nt * n].rearrange("p (t n) -> p t n", t=nt)[:, :, o:o + g * w] \
                            .rearrange("p t (g w) -> p t g w", g=g)
                        ss = ss.rearrange("p (t g) -> p t g", t=nt)
                    link(dve.tensor_reduce(ss, src, AX.X, ALU.add))
                    flat = SS[:, at:at + nt * g]
                    link(dve.tensor_scalar(flat, flat, 1.0 / w, EPS, ALU.mult, ALU.add))
                    groups.append((at, o, g, w, gain))
                    at += nt * g
                dve.reciprocal(SS[:, 0:at], SS[:, 0:at]).then_inc(h_rin, 1)
                if k == 1:
                    link(dve.tensor_copy(KR[:, :, :], tok[:, :, 384:416]))
                dve.wait_ge(h_rs, k + 1)
                for a0, o, g, w, gain in groups:
                    for tk in range(nt):
                        v = tok[:, tk, o:o + g * w].rearrange("p (g w) -> p g w", g=g)
                        r = SS[:, a0 + tk * g:a0 + (tk + 1) * g]
                        ins = dve.tensor_tensor(v, v, r[:, :, None].broadcast_to([P, g, w]), ALU.mult)
                    link(ins)
                    if gain:
                        for tk in range(nt):
                            v = tok[:, tk, o:o + g * w].rearrange("p (g w) -> p g w", g=g)
                            ins = dve.tensor_tensor(v, v, row(gain, w)[:, None, :].broadcast_to([P, g, w]), ALU.mult)
                        link(ins)
                if h["rope"] is not None:
                    o, g, w, f = h["rope"]
                    for tk in range(nt):
                        v = tok[:, tk, o:o + g * w].rearrange("p (g w) -> p g w", g=g)[:, :, f:f + 32]
                        a = ra[:, tk * g * 32:(tk + 1) * g * 32].rearrange("p (g w) -> p g w", g=g)
                        b = rb[:, tk * g * 32:(tk + 1) * g * 32].rearrange("p (g w) -> p g w", g=g)
                        dve.tensor_tensor(a, v, COS[:, tk, None, :].broadcast_to([P, g, 32]), ALU.mult)
                        for x, y in ((0, 16), (16, 0)):
                            ins = dve.tensor_tensor(b[:, :, x:x + 16], v[:, :, y:y + 16],
                                                    SIN[:, tk, None, x:x + 16].broadcast_to([P, g, 16]), ALU.mult)
                    link(ins)
                    for tk in range(nt):
                        v = tok[:, tk, o:o + g * w].rearrange("p (g w) -> p g w", g=g)[:, :, f:f + 32]
                        a = ra[:, tk * g * 32:(tk + 1) * g * 32].rearrange("p (g w) -> p g w", g=g)
                        b = rb[:, tk * g * 32:(tk + 1) * g * 32].rearrange("p (g w) -> p g w", g=g)
                        ins = dve.tensor_tensor(v, a, b, ALU.add)
                    link(ins)
                if "v" in h:
                    o, w, tile = h["v"]
                    dve.wait_ge(h_v, {0: 1, 3: 2}[k])
                    v = [cat(w_, tile, nt * w // SEQ).rearrange("p (t n) -> p t n", t=nt) for w_ in (0, 1)]
                    link(dve.tensor_tensor(v[1], tok[:, :, o:o + w], v[0].bitcast(F), ALU.subtract))
                link(dve.memset(SS[:, at:at + 1], 1.0) if at < 64 else dve.memset(LAM[:, 3:4], 1.0))
                dve.nop().then_inc(h_nrm, 1)

            def head_lo(k):
                h = HEADS[k]
                dve.wait_ge(h_hi, k + 1)
                for j, tile in enumerate(h["tiles"]):
                    w = h["turn"][0][1]
                    if h.get("memk"):
                        ins = low_from_psum(lo(tile), hi(tile), PS[:, 4, :])
                    elif "gain" in h:
                        ins = dve.scalar_tensor_tensor(out=lo(tile), in0=PS[:, 4 + j, :], scalar=col(*h["gain"][j]),
                                                       in1=hi(tile).bitcast(F), op0=ALU.mult, op1=ALU.subtract)
                    else:
                        ins = low_from_psum(lo(tile)[0:w, :], hi(tile)[0:w, :], PS[0:w, 4 + j, :])
                ins.then_inc(h_lo, 1)

            head_norm(0)
            for k in range(1, 4):
                head_lo(k - 1)
                head_norm(k)
            lv = row("lam", 128).rearrange("p (a b c) -> p a b c", a=2, b=2)
            prod = YSQ[:, 0:64].rearrange("p (a c) -> p a c", a=2)
            link(dve.tensor_tensor(prod, lv[:, :, 0, :], lv[:, :, 1, :], ALU.mult))
            dve.tensor_reduce(LAM[:, 0:2], prod, AX.X, ALU.add).then_inc(lam_sum, 1)
            head_lo(3)
            dve.wait_ge(lam_exp, 1)
            link(dve.tensor_tensor(LAM[:, 0:1], LAM[:, 3:4], LAM[:, 2:3], ALU.subtract))
            link(dve.tensor_scalar(LAM[:, 0:1], LAM[:, 0:1], -LAM_INIT, None, ALU.add))
            attention("dm")
            head_norm(4)
            for k in range(5, 8):
                head_lo(k - 1)
                head_norm(k)
            vh, vl = [cat(w, LV, 4).rearrange("p (t n) -> p t n", t=NT) for w in (0, 1)]
            for tk in range(NT):
                dve.wait_ge(vm_hi, tk + 1)
                low_from_psum(vl[:, tk, :], vh[:, tk, :], PS[:, tk, :]).then_inc(vm_lo, 1)
            head_lo(7)
            attention("mla")

            residual("wout2", 1, y_out)

        @block.tensor
        def _(pe):
            def three(dst, a, b, first, last, **kw):
                pe.matmul(dst, a[0], b[0], start=first, stop=False, **kw)
                pe.matmul(dst, a[0], b[1], start=False, stop=False, **kw)
                return pe.matmul(dst, a[1], b[0], start=False, stop=last, **kw)

            def arrive(c, n=0, i=0):
                pe.wait_ge(split_lo, (c + 1) + n * i)

            def weight(c, sub, width=P, pitch=P):
                a = sub * pitch
                return WHI[:, c % 2, a:a + width], WLO[:, c % 2, a:a + width]

            def unit_T(c, bank, acts, n=0, i=0, subs=range(8), first=True, last=True):
                arrive(c, n, i)
                subs = list(subs)
                for j in subs:
                    ins = three(PS[:, bank, :], weight(c, j), acts(j), first and j == subs[0], last and j == subs[-1])
                return ins

            H = lambda kt: (HHI[:, kt, :], HLO[:, kt, :])

            def norm_total(k, width):
                pe.wait_ge(n_acc, 7 * k + 7)
                pe.matmul(PS[:, 7, 0:width], ONE[:, :], PB[:, 2 * SEQ:2 * SEQ + width], start=True, stop=True).then_inc(n_tot, 1)

            pe.wait_ge(consts, 4)
            norm_total(0, SEQ)
            pe.wait_ge(tbl_ready, 1)
            pe.wait_ge(ld_oh, 16)
            fx33 = FX[0:NBUCKET + 1, :, :].rearrange("p a b -> p (a b)")
            for b in range(5):
                a, e = OH * b // 5, OH * (b + 1) // 5
                ins = pe.matmul(PS[0:16, 2 + b, 0:e - a], TBL[:, :], fx33[:, a:e], start=True, stop=True)
            ins.then_inc(oh_mm, 1)

            u = UNIT["proj"]
            for c in range(2):
                if c == 0:
                    pe.wait_ge(n_lo, 8)
                unit_T(u + c, c, H).then_inc(unit_used, 1)
            with pe.Fori(1, 5) as i:
                for s in range(2):
                    pe.wait_ge(proj_out, 2 * i + (s - 1))
                    unit_T(u + s, s, H, 2, i).then_inc(unit_used, 1)
            for c in (10, 11, 12):
                pe.wait_ge(proj_out, c - 1)
                unit_T(u + c, c % 2, H).then_inc(unit_used, 1)
            def unit_tok(c, n, toks, acts, banks, first, last, kts=2, pitch=None, inc=True):
                arrive(c)
                for tk in toks:
                    for j in range(kts):
                        a = acts(c, j)
                        a = (a[0][:, tk * P:(tk + 1) * P], a[1][:, tk * P:(tk + 1) * P])
                        ins = three(PS[:, banks + tk, 0:n], a, weight(c, j, n, pitch or n), first and j == 0, last and j == kts - 1)
                if inc:
                    ins.then_inc(unit_used, 1)
                return ins

            u = UNIT["vtok"]
            pe.wait_ge(oh_ev, 1)
            for c in range(4):
                unit_tok(u + c, 408, range(4), lambda c_, j, c=c: H(2 * c + j), 2, c == 0, c == 3)
            u = UNIT["cmp"]
            pe.wait_ge(v_lo, 4)
            pe.wait_ge(v_hi, 5)
            for w in range(2):
                pe.wait_ge(cb_lo, w + 1)
                cbs = [cat(x, 14 + 4 * w, 4) for x in (0, 1)]
                for c in range(4):
                    arrive(u + 4 * w + c)
                    for j in range(4):
                        tp = 4 * c + j
                        ins = three(PS[:, 6 + w, 0:256], [b[:, tp * P:(tp + 1) * P] for b in cbs],
                                    weight(u + 4 * w + c, j, 256, 256), tp == 0, tp == 15)
                    ins.then_inc(unit_used, 1)
            pe.wait_ge(gelu_done, 2)
            pe.wait_ge(proj_out, 13)
            for j in range(4):
                ins = pe.transpose(PS[:, 0, j * P:(j + 1) * P], FX[:, 6, j * P:(j + 1) * P], IDN[:, :])
            ins.then_inc(gelu_t, 1)
            pe.wait_ge(gelu_copied, 1)
            pe.wait_ge(ld_w2, 16)
            gt = FX[:, 7, :].rearrange("p (w h n) -> p w h n", w=2, h=2)
            for c in range(2):
                pe.matmul(PS[:, 1, 0:P], W2[:, 0, c, :], gt[:, 0, c, :], start=c == 0, stop=c == 1)
            for g in range(2):
                for c in range(2):
                    ins = pe.matmul(PS[0:32, 2, 64 * g:64 * g + 64], gt[:, 1, c, 64 * g:64 * g + 32], W2[:, 1, c, 0:64],
                                    start=c == 0, stop=c == 1)
            ins.then_inc(cmp_mm, 1)
            pe.wait_ge(cmp_lo, 1)

            def scores(A, m):
                if m["i"] >= 1:
                    prev = m["prev"]
                    pe.wait_ge(A["exped" if prev["kind"] == "mem" else "biased"], m["i"])
                if m["kind"] == "cmp":
                    for q in range(NT):
                        a = [x[:, q * P:(q + 1) * P] for x in m["q"]]
                        ins = three(PS[:, 2, 32 * q:32 * q + 32], a, m["k"], True, True)
                else:
                    for q in range(NT):
                        (b, o), (k0, nk) = m["place"][q], m["spans"][q]
                        a = [x[:, q * P:(q + 1) * P] for x in m["q"]]
                        ins = three(PS[:, b, o:o + nk], a, [x[:, k0:k0 + nk] for x in m["k"]], True, True)
                ins.then_inc(A["scores"], 1)

            def turn(A, m):
                pe.wait_ge(A["normed"], m["n"])
                if m["n"] > 1:
                    pe.wait_ge(A["p_lo"], m["n"] - 1)
                pr = prob(m)
                for q in range(NT):
                    if m["kind"] == "cmp":
                        ins = pe.transpose(PS[0:32, 3, q * P:(q + 1) * P], pr[:, 32 * q:32 * q + 32], IDN[:, :])
                        continue
                    (b, o), (k0, nk) = m["place"][q], m["spans"][q]
                    for j in range(nk // P):
                        p0 = m["p"][q] + j * P
                        ins = pe.transpose(PS[:, 3 + b, o + j * P:o + (j + 1) * P], pr[:, p0:p0 + P], IDN[:, :])
                ins.then_inc(A["turned"], 1)

            def values(name, A, m, pts):
                pe.wait_ge(A["p_lo"], m["n"])
                y = m["y"]
                if m["first"] and y >= 2:
                    if name == "ab":
                        pe.wait_ge(A["y_lo"], y - 1)
                    elif name == "mla":
                        pe.wait_ge(A["y_f"], y - 1)
                    elif y >= 6:
                        pe.wait_ge(A["y_f"], y - 5)
                    elif y % 2:
                        pe.wait_ge(dm_rin, y - 1 if y == 3 else 4)
                    else:
                        pe.wait_ge(A["y_hi"], y - 1)
                pt = pts[m["n"] % 2]
                for kb in range(m["nkb"]):
                    q0, q1 = m["kb"](kb)
                    krows = slice(0, 32) if m["kind"] == "cmp" else slice(0, P)
                    ins = three(PS[:, m["bank"], q0:q1], [m["v"][w](kb) for w in (0, 1)],
                                [part(w, pt + kb)[krows, q0:q1] for w in (0, 1)],
                                m["first"] and kb == 0, m["last"] and kb == m["nkb"] - 1, skip_group_check=True)
                ins.then_inc(A["pv"], 1)

            def attention(name):
                maps, pts = GROUP[name]
                A = ATT[name]
                for i in range(-2, len(maps) + 2):
                    if 0 <= i + 2 < len(maps):
                        scores(A, maps[i + 2])
                    if 0 <= i < len(maps) and maps[i].get("mode") != "hold":
                        turn(A, maps[i])
                    if 0 <= i - 1 < len(maps) and maps[i - 1].get("mode") != "hold":
                        values(name, A, maps[i - 1], pts)
                    if 0 <= i - 2 < len(maps) and maps[i - 2].get("diff") and maps[i - 2]["last"] and maps[i - 2]["bank"] == 7:
                        m = maps[i - 2]
                        pe.wait_ge(dm_sq, m["y"] // 2 + 1)
                        pe.matmul(PS[:, 7, :], BONE[:, :], YSQ, start=True, stop=True, skip_group_check=True).then_inc(dm_tot, 1)

            attention("ab")

            u = UNIT["merge"]
            def merge(i):
                for s in range(2):
                    if not isinstance(i, int):
                        pe.wait_ge(merge_dve, 8 * i + (4 * s - 8 + 2))
                    for e in range(2):
                        unit_T(u + 3 * s + e, 4 * s + e, H, 6, i).then_inc(unit_used, 1)
                    c = u + 3 * s + 2
                    ya = lambda j: (hi(j), lo(j))
                    unit_T(c, 4 * s + 2, ya, 6, i, range(0, 4))
                    unit_T(c, 4 * s + 3, ya, 6, i, range(4, 8)).then_inc(unit_used, 1)
            pe.wait_ge(ATT["ab"]["y_lo"], 16)
            merge(0)
            with pe.Fori(1, 4) as i:
                merge(i)

            def dense(name, acts, done, ready):
                c0 = UNIT[name]
                ready()
                for s in range(2):
                    unit_T(c0 + s, s, acts).then_inc(unit_used, 1)
                with pe.Fori(1, 4) as i:
                    for s in range(2):
                        pe.wait_ge(done, 2 * i + (s - 1))
                        unit_T(c0 + s, s, acts, 2, i).then_inc(unit_used, 1)

            dense("wout", lambda j: (hi(14 + j), lo(14 + j)), x1_done, lambda: pe.wait_ge(merge_dve, 32))
            norm_total(1, SEQ)

            u = UNIT["ffn"]
            def ffn(i):
                for s in range(2):
                    if not isinstance(i, int):
                        pe.wait_ge(ffn_dve, 12 * i + (6 * s - 12 + 4))
                    for e in range(2):
                        unit_T(u + 2 * s + e, 2 * e + s, H, 4, i).then_inc(unit_used, 1)
            pe.wait_ge(n_lo, 16)
            ffn(0)
            with pe.Fori(1, NF // 2) as i:
                ffn(i)

            u = UNIT["down"]
            def down(i):
                for s in range(2):
                    if not isinstance(i, int):
                        pe.wait_ge(x2_done, 2 * i + (s - 1))
                    for e in range(3):
                        unit_T(u + 3 * s + e, s, lambda j, e=e: (hi(8 * e + j), lo(8 * e + j)), 6, i,
                               range(min(8, NF - 8 * e)), e == 0, e == 2).then_inc(unit_used, 1)
            pe.wait_ge(ffn_dve, 6 * NF)
            down(0)
            with pe.Fori(1, 4) as i:
                down(i)
            for k, width in ((2, SEQ), (3, SEQ), (4, 256)):
                norm_total(k, width)

            def head_turn(k):
                h = HEADS[k]
                pe.wait_ge(h_nrm, k + 1)
                if k:
                    pe.wait_ge(h_lo, k)
                for tk in range(h["nt"]):
                    for j, (o, w) in enumerate(h["turn"]):
                        dst = PS[0:w, 4, (2 * j + tk) * P:(2 * j + tk + 1) * P] if h.get("memk") \
                            else PS[0:w, 4 + j, tk * P:(tk + 1) * P]
                        ins = pe.transpose(dst, TOK[:, tk * h["n"] + o:tk * h["n"] + o + w], IDN[:, :])
                ins.then_inc(h_tr, 1)

            pe.wait_ge(n_lo, 32)
            u = UNIT["mem"]
            memn = [cat(w, 16, 4).rearrange("p (k n) -> p k n", k=KT) for w in (0, 1)]
            for c in range(4):
                unit_tok(u + c, 512, range(2), lambda c_, j, c=c: (memn[0][:, 2 * c + j, :], memn[1][:, 2 * c + j, :]),
                         0, c == 0, c == 3)
            for k in range(1, 4):
                u = UNIT["tok2"] + 4 * (k - 1)
                n = HEADS[k]["n"]
                pe.wait_ge(h_tok, k)
                for c in range(4):
                    unit_tok(u + c, n, range(4), lambda c_, j, c=c: H(2 * c + j), 0, c == 0, c == 3)
                head_turn(k - 1)
            u = UNIT["z"]
            pe.wait_ge(h_tok, 4)
            for c in range(8):
                if c >= 2:
                    pe.wait_ge(z_done, c - 1)
                unit_T(u + c, c % 2, H).then_inc(unit_used, 1)
            head_turn(3)
            pe.wait_ge(z_done, 8)
            pe.wait_ge(h_lo, 4)
            attention("dm")

            cq = lambda c_, j: (hi(CQ + j), lo(CQ + j))
            pe.wait_ge(ATT["dm"]["y_lo"], 6)
            for k in (4, 5):
                if k == 5:
                    pe.wait_ge(h_tok, 5)
                unit_tok(UNIT["uq"] + k - 4, 384, range(4), cq, 0, True, True)
                if k == 5:
                    head_turn(4)
            c = UNIT["ukv"]
            arrive(c)
            for k in (6, 7, 8):
                pe.wait_ge(h_tok, k)
                for tk in range(NT):
                    a = (hi(CKV)[:, tk * P:(tk + 1) * P], lo(CKV)[:, tk * P:(tk + 1) * P])
                    n, o = (512, 512) if k == 8 else (256, 256 * (k - 6))
                    b = (WHI[:, c % 2, o:o + n], WLO[:, c % 2, o:o + n])
                    ins = three(PS[:, tk, 0:n], a, b, True, True)
                ins.then_inc(unit_used if k == 8 else k_mm, 1)
                head_turn(k - 1)
            pe.wait_ge(vm_lo, 4)
            pe.wait_ge(h_lo, 8)
            attention("mla")

            yo = lambda j: (hi(LQ + j), lo(LQ + j)) if j < 4 else (hi(Y_DM + j - 4), lo(Y_DM + j - 4))
            dense("wout2", yo, y_out, lambda: pe.wait_ge(ATT["mla"]["y_lo"], 8))

    return nc


def _t5_bucket(dist):
    dist = np.maximum(dist, 0)
    d = np.maximum(dist, 1).astype(np.float32)
    large = 16 + (np.log(d / np.float32(16)) / np.float32(math.log(8.0)) * np.float32(16)).astype(np.int32)
    return np.where(dist < 16, dist, np.minimum(large, NBUCKET - 1))


def _onehot():
    def table(dist, valid):
        m = np.zeros((NBUCKET + 1, dist.size), np.float32)
        m[np.where(valid, _t5_bucket(dist), NBUCKET), np.arange(dist.size)] = 1.0
        return m
    da = 255 - np.arange(OH_A)
    db = SEQ - 1 - np.arange(OH_B)
    b, a = np.divmod(np.arange(OH_C), CMP_A)
    dc = SEQ - (16 * a + b)
    return np.concatenate([table(da, (da >= 0) & (da < 128)), table(db, db >= 0), table(dc, dc >= 0)], axis=1)


def kernel(**inputs):
    import concourse.bacc as _bacc
    from concourse.bass_utils import run_bass_kernel_spmd as _run

    a = {k: np.asarray(v) for k, v in inputs.items()}
    f32 = np.float32

    def tiles(w):
        k, n = w.shape
        return w.reshape(k // P, P, n // P, P).transpose(2, 1, 0, 3).reshape(n // P, P, k)

    def rows2(w, n):
        return w.reshape(4, 2, P, n).transpose(0, 2, 1, 3).reshape(4, P, 2 * n)

    def pad(w):
        out = np.zeros(w.shape[:2] + (1024,), f32)
        out[:, :, :w.shape[2]] = w
        return out

    w = a["w_in"][0]
    off = np.cumsum([0, 512, 128, 128, 512, 128, 128, 128, 128, 128, 128, 24, 1024, 1024])
    qa, ka, va, qb, kc, vc, ksl, vsl, kw, vw, gn, ga, gb = [w[:, off[i]:off[i + 1]] for i in range(13)]

    def pair(m, axis):
        shape = m.shape
        if axis == 1:
            return m.reshape(shape[0], 2, 4, DH).transpose(0, 2, 1, 3).reshape(shape)
        return m.reshape(2, 4, DH, shape[1]).transpose(1, 0, 2, 3).reshape(shape)

    up = np.concatenate([tiles(pair(a["w_up_a"][0], 0)), tiles(pair(a["w_up_b"][0], 0))], axis=2)
    ga, gb = tiles(ga), tiles(gb)
    merge = np.stack([ga, gb, up], axis=1).reshape(24, P, 1024)
    wf = tiles(a["w_ffn_in"][0])
    wf = np.stack([wf[:NF], wf[NF:]], axis=1).reshape(2 * NF, P, 1024)
    down = np.zeros((8, P, 3072), f32)
    down[:, :, :D_FF] = tiles(a["w_ffn_out"][0])
    down = down.reshape(8, P, 3, 1024).transpose(0, 2, 1, 3).reshape(24, P, 1024)
    w1 = np.concatenate([a[n][0].reshape(4, 4, P, 256).transpose(0, 2, 1, 3).reshape(4, P, 1024)
                         for n in ("cmp_w1_k", "cmp_w1_v")])
    v = a["w_in_2"][0]
    uq = a["w_uq_2"][0].reshape(2, P, 2, 384).transpose(2, 1, 0, 3).reshape(2, P, 768)
    ukv = a["w_ukv_2"][0].reshape(P, NH, 2, DH).transpose(0, 2, 1, 3).reshape(1, P, 1024)
    stream = np.concatenate([
        tiles(np.concatenate([pair(qa, 1), pair(qb, 1), ka, ksl, kw, kc, vc], axis=1)),
        pad(rows2(np.concatenate([va, vsl, vw, gn], axis=1), 408)), w1, merge, tiles(a["w_out"][0]), wf, down,
        pad(rows2(a["w_mem_kv_2"][0], 512)),
        pad(rows2(v[:, 0:416], 416)), pad(rows2(v[:, 416:928], 512)), pad(rows2(v[:, 928:1440], 512)),
        tiles(v[:, 1440:2464]), pad(uq), ukv, tiles(a["w_out_2"][0])])
    assert stream.shape == (NU, P, 1024)

    fm = lambda g: g.reshape(-1, P).T
    conv = np.concatenate([a["conv_w"][0], a["conv_b"]])
    conv = conv.reshape(4, 2, NF, P).transpose(3, 2, 1, 0).reshape(P, 8 * NF)
    twice = lambda m: np.concatenate([m, m])
    cols = np.concatenate([fm(a["norm_mix"]), fm(a["norm_ffn"]), fm(a["norm_final"]), fm(a["norm_g_2"]),
                           fm(a["mem_norm_g_2"]), fm(a["mla_q_norm_g_2"]), fm(a["mla_kv_norm_g_2"]),
                           twice(a["diff_subln_g_2"][0])[:, None], twice(a["cmp_pos_k"][0].T), twice(a["cmp_pos_v"][0].T),
                           conv], axis=1)
    inv = (f32(10000.0) ** (-np.arange(0, 32, 2, dtype=f32) / f32(32))).astype(f32)
    rows = np.concatenate([a["mla_qn_g_2"][0], a["mla_kn_g_2"][0], a["diff_qn_g_2"][0], a["diff_kn_g_2"][0],
                           a["mem_qn_g_2"][0], a["mem_kn_g_2"][0], a["attn_sinks"][0], inv,
                           a["diff_lambda_2"][0].reshape(-1)])[None]
    w2k = a["cmp_w2_k"][0].reshape(2, P, DH).transpose(1, 0, 2)
    w2v = a["cmp_w2_v"][0].reshape(2, P, DH).transpose(1, 0, 2)
    w2 = np.stack([np.concatenate([m, m], axis=2) for m in (w2k, w2v)], axis=1)
    xt = a["x"][0].T.reshape(KT, P, SEQ).transpose(1, 0, 2)
    mt = a["mem_2"][0].T.reshape(KT, P, 256).transpose(1, 0, 2).reshape(P, KT * 256)
    arrays = {"wstream": stream, "xT": xt, "memT": mt, "cols": cols, "rows": rows, "w2": w2,
              "table": a["rel_bias_table"], "onehot": _onehot(), "pos": a["positions_2"][0].reshape(NT, P).T}
    arrays = {k: np.ascontiguousarray(v_) for k, v_ in arrays.items()}

    nc = _bacc.Bacc("TRN2", target_bir_lowering=False, num_devices=1)
    t = {k: nc.dram_tensor(k, v_.shape, mybir.dt.from_np(v_.dtype), kind="ExternalInput").ap() for k, v_ in arrays.items()}
    out = nc.dram_tensor("outT", (P, KT, SEQ), F, kind="ExternalOutput").ap()
    build(nc, t, out)
    r = _run(nc, [arrays], core_ids=[0])
    got = r.results[0]["outT"]
    return np.ascontiguousarray(got.transpose(1, 0, 2).reshape(D, SEQ).T)[None]
```

```python
import math

import numpy as np
import concourse.bass as bass
from concourse import mybir

F = mybir.dt.float32
R = mybir.dt.float32r
I32 = mybir.dt.int32
ALU = mybir.AluOpType
ACT = mybir.ActivationFunctionType
AX = mybir.AxisListType

P = 128
SEQ = 512
NT = SEQ // P
D = 1024
KT = D // P
DH = 64
NH = 8
NBUCKET = 32
N_CMP = (SEQ - 32) // 16 + 1
CMP_A = 66
D_FF = 2816
NF = D_FF // P
EPS = 1e-6
NEG = -1e30
LAM_INIT = 0.8 - 0.6 * math.exp(0.0)

_PLAN = [("proj", 13), ("vtok", 4), ("cmp", 8), ("merge", 24), ("wout", 8), ("ffn", 2 * NF),
         ("down", 24), ("mem", 4), ("tok2", 12), ("z", 8), ("uq", 2), ("ukv", 1), ("wout2", 8)]
UNIT = {}
NU = 0
for _n, _c in _PLAN:
    UNIT[_n] = NU
    NU += _c

OH_A, OH_B, OH_C = 384, 640, 16 * CMP_A
OH = OH_A + OH_B + OH_C

COL = {}
_at = 0
for _n, _c in [("g_mix", 8), ("g_ffn", 8), ("g_final", 8), ("g_2", 8), ("g_mem", 8), ("g_q2", 2),
               ("g_kv2", 1), ("subln", 1), ("pos_k", 32), ("pos_v", 32), ("conv", 4 * 2 * NF)]:
    COL[_n] = _at
    _at += _c
NCOL = _at
ROW = {}
_at = 0
for _n, _c in [("qn", 96), ("kn", 96), ("dqn", 32), ("dkn", 32), ("mqn", 64), ("mkn", 64),
               ("sinks", 8), ("inv", 16), ("lam", 128)]:
    ROW[_n] = _at
    _at += _c
NROW = _at


class Chain:

    def __init__(self, eng, sem):
        self.eng, self.sem, self.n = eng, sem, 0

    def link(self, ins):
        self.n += 1
        ins.then_inc(self.sem, 1)
        self.eng.wait_ge(self.sem, self.n)


def build(nc, t, out):
    from contextlib import ExitStack
    ctx = ExitStack()
    with ctx:
        def sb(name, shape, dt=F):
            return ctx.enter_context(nc.sbuf_tensor(name, shape, dt))

        def sem(name):
            return ctx.enter_context(nc.semaphore(name))

        X = sb("X", [P, KT, SEQ])
        FX = sb("FX", [P, 8, SEQ])
        HHI = sb("HHI", [P, KT, SEQ], R)
        HLO = sb("HLO", [P, KT, SEQ], R)
        BHI = sb("BHI", [P, 24, SEQ], R)
        BLO = sb("BLO", [P, 24, SEQ], R)
        RAW = sb("RAW", [P, 2, 1024])
        WHI = sb("WHI", [P, 2, 1024], R)
        WLO = sb("WLO", [P, 2, 1024], R)
        PB = sb("PB", [P, 7 * SEQ])
        TRI = sb("TRI", [P, SEQ])
        IDN = sb("IDN", [P, P])
        ONE = sb("ONE", [P, P])
        BONE = sb("BONE", [P, P])
        CL = sb("CL", [P, NCOL])
        RW = sb("RW", [P, NROW])
        GATE = sb("GATE", [P, NT, 24])
        KR = sb("KR", [P, NT, 32])
        COS = sb("COS", [P, NT, 32])
        SIN = sb("SIN", [P, NT, 32])
        POS = sb("POS", [P, NT], I32)
        ST = sb("ST", [P, 4, 40])
        SS = sb("SS", [P, 64])
        MSK = sb("MSK", [P, NT])
        LAM = sb("LAM", [P, 4])
        TBL = sb("TBL", [NBUCKET + 1, 16])
        PS = ctx.enter_context(nc.psum_tensor("PS", [P, 8, SEQ], F))
        tb_dram = nc.dram_tensor("bias_rows", [16, OH], F, kind="Internal").ap()
        bias_a = nc.dram_tensor("bias_a", [NH, P, 256], F, kind="Internal").ap()
        bias_b = nc.dram_tensor("bias_b", [NH, P, SEQ], F, kind="Internal").ap()
        bias_c = nc.dram_tensor("bias_c", [NH, P, NT, N_CMP], F, kind="Internal").ap()

        SQ = [PB[:, s * SEQ:(s + 1) * SEQ] for s in (0, 1)]
        ACC = [PB[:, 2 * SEQ:3 * SEQ], PB[:, 4 * SEQ:5 * SEQ]]
        RSTD = PB[:, 6 * SEQ:7 * SEQ]
        RT = sb("RT", [P, 10])
        R_MEM, R_TWO = 4, 6
        YT, YSQ = PB[:, 5 * SEQ:6 * SEQ], PB[:, 6 * SEQ:7 * SEQ]
        W2 = YT.rearrange("p (w h n) -> p w h n", w=2, h=2)

        def hi(tile):
            return BHI[:, tile, :] if tile < 24 else HHI[:, tile - 24, :]

        def lo(tile):
            return BLO[:, tile, :] if tile < 24 else HLO[:, tile - 24, :]

        def part(w, tile):
            return (hi, lo)[w](tile)

        def cat(w, tile, n):
            a = ((BHI, BLO) if tile < 24 else (HHI, HLO))[w]
            tile %= 24
            return a[:, tile:tile + n, :].rearrange("p a b -> p (a b)")

        def col(name, j=0):
            return CL[:, COL[name] + j:COL[name] + j + 1]

        def row(name, n):
            return RW[:, ROW[name]:ROW[name] + n]

        ld_x = [sem(f"ld_x{j}") for j in range(4)]
        ld_cols, ld_small, ld_mem, ld_bias = sem("ld_cols"), sem("ld_small"), sem("ld_mem"), [sem("ld_bias0"), sem("ld_bias1")]
        ld_oh, ld_cmp, st_rows, ld_w2 = sem("ld_oh"), sem("ld_cmp"), sem("st_rows"), sem("ld_w2")
        raw_loaded = [sem("raw_loaded0"), sem("raw_loaded1")]
        split_hi, split_lo, unit_used = sem("split_hi"), sem("split_lo"), sem("unit_used")
        consts, dve_step, act_step = sem("consts"), sem("dve_step"), sem("act_step")
        n_sq, n_acc, n_tot, n_rin, n_rstd, n_hi, n_lo, scaled = [sem("norm_" + s) for s in
            ("sq", "acc", "tot", "rin", "rstd", "hi", "lo", "scaled")]
        SCALED = dict(proj=0, merge=11, ffn=27, z=27 + 2 * NF)
        spread, mem_sq = sem("spread"), sem("mem_sq")
        oh_mm, oh_ev, tbl_ready = sem("oh_mm"), sem("oh_ev"), sem("tbl_ready")
        ang_ready = sem("ang_ready")
        sin_ready = sem("sin_ready")
        proj_hi, proj_out = sem("proj_hi"), sem("proj_out")
        v_hi, v_lo = sem("v_hi"), sem("v_lo")
        cb_built, cb_hi, cb_lo = sem("cb_built"), sem("cb_hi"), sem("cb_lo")
        gelu_done, gelu_t, gelu_copied, cmp_mm, cmp_hi, cmp_lo = [sem(s) for s in
            ("gelu_done", "gelu_t", "gelu_copied", "cmp_mm", "cmp_hi", "cmp_lo")]
        merge_act, merge_dve = sem("merge_act"), sem("merge_dve")
        x1_done, x2_done, xf_done = sem("x1_done"), sem("x2_done"), sem("xf_done")
        ffn_act, ffn_dve = sem("ffn_act"), sem("ffn_dve")
        h_tok, h_sq, h_v, h_rin, h_rs, h_nrm, h_tr, h_hi, h_lo = [sem("head_" + s) for s in
            ("tok", "sq", "v", "rin", "rs", "nrm", "tr", "hi", "lo")]
        z_done, lam_sum, lam_exp, vm_hi, vm_lo = [sem(s) for s in ("z_done", "lam_sum", "lam_exp", "vm_hi", "vm_lo")]
        y_out, stored = sem("y_out"), sem("stored")
        ATT = {g: {s: sem(f"{g}_{s}") for s in
                   ("scores", "biased", "exped", "normed", "turned", "p_hi", "p_lo", "pv", "y_f", "y_hi", "y_lo")}
               for g in ("ab", "dm", "mla")}
        dm_sq, dm_tot, dm_rin, dm_rstd, dm_y, dm_hi, k_mm = [sem(s) for s in
            ("dm_sq", "dm_tot", "dm_rin", "dm_rstd", "dm_y", "dm_hi", "k_mm")]

        CAUSAL = dict(spans=[(0, 128), (0, 256), (0, 384), (0, 512)], place=[(0, 0), (2, 0), (0, 128), (1, 0)],
                      groups=[[1], [0, 2], [3]])
        WITH_CMP = dict(spans=CAUSAL["spans"] + [(0, 32)] * 4,
                        place=CAUSAL["place"] + [(2, 256 + 32 * q_) for q_ in range(4)], groups=[[1, 4, 5, 6, 7], [0, 2], [3]])
        WINDOW = dict(spans=[(0, 128), (0, 256), (128, 256), (256, 256)],
                      place=[(0, 0), (0, 128), (1, 0), (1, 256)], groups=[[0, 1], [2, 3]])
        MEMORY = dict(spans=[(0, 256)] * 4, place=[(0, 0), (0, 256), (1, 0), (1, 256)], groups=[[0, 1], [2, 3]])
        V_AT = 11
        PT_AB = (14, 18)
        KC = 0

        def causal_kb(kb):
            return kb * P, SEQ

        def window_kb(kb):
            return kb * P, min(SEQ, kb * P + 2 * P)

        def vtok(w, b):
            v = cat(w, V_AT, 3).rearrange("p (t n) -> p t n", t=NT)
            return lambda kb: v[:, kb, b * P:(b + 1) * P]

        ab = []
        heads = [(0, r, g) for r in range(4) for g in range(2)] + [(1, r, g) for r in range(4) for g in range(2)]
        for y, (blk, r, g) in enumerate(heads):
            rows = slice(g * DH, g * DH + DH)
            q = [part(w, 4 * blk + r)[rows] for w in (0, 1)]
            base = dict(q=q, y=y, rows=rows, ytile=4 * blk + r, bank=6 + y % 2, bias=y, h=4 * g + r, scale=DH ** -0.5)
            if blk == 0:
                ab.append(dict(base, kind="bias", k=[part(w, 8)[rows] for w in (0, 1)], v=[vtok(w, 0) for w in (0, 1)],
                               nkb=4, kb=window_kb, b0=[128, 0, 0, 0], sink=True, first=True, last=True, **WINDOW))
            else:
                for b, tile in ((1, 9), (2, 10)):
                    ab.append(dict(base, kind="bias", k=[part(w, tile)[rows] for w in (0, 1)],
                                   v=[vtok(w, b) for w in (0, 1)], nkb=4, kb=causal_kb,
                                   b0=[384 - 128 * q_ for q_ in range(4)], gate=12 * g + 3 * r + b,
                                   first=b == 1, last=b == 2, **(WITH_CMP if b == 1 else CAUSAL)))
                ab[-2].update(cmp=12 * g + 3 * r, kc=[part(w, 22)[rows, KC:KC + 32] for w in (0, 1)])
        DQ, DK, DV, MQ, MK, MV, Y_DM, PT_DM, CQ, CKV = 0, 2, 4, 6, 8, 9, 12, (16, 24), 20, 22
        LQ, LK, LV, PT_L = 0, 24, 16, (8, 20)
        dm = []
        for h in range(4):
            for m in range(2):
                f = 64 * (h % 2) + 32 * m
                rows = slice(f, f + 32)
                dv = [cat(w, DV, 2).rearrange("p (t n) -> p t n", t=NT) for w in (0, 1)]
                dm.append(dict(kind="bias", q=[part(w, DQ + h // 2)[rows] for w in (0, 1)],
                               k=[part(w, DK + h // 2)[rows] for w in (0, 1)],
                               v=[(lambda kb, w=w, h=h, dv=dv: dv[w][:, kb, (h // 2) * P:(h // 2 + 1) * P]) for w in (0, 1)],
                               nkb=4, kb=causal_kb, b0=[384 - 128 * q_ for q_ in range(4)], scale=32 ** -0.5,
                               y=h, rows=slice(64 * (h % 2), 64 * (h % 2) + 64), ytile=Y_DM + h // 2, ztile=4 + h // 2,
                               bank=6 + h % 2, first=m == 1, last=m == 1, mode=("hold", "sub")[m], diff=True, **CAUSAL))
        for h in range(4):
            rows = slice(64 * (h % 2), 64 * (h % 2) + 64)
            mk = [cat(w, MK, 1).rearrange("p (t n) -> p t n", t=2) for w in (0, 1)]
            mv = [cat(w, MV, 1).rearrange("p (t n) -> p t n", t=2) for w in (0, 1)]
            dm.append(dict(kind="mem", q=[part(w, MQ + h // 2)[rows] for w in (0, 1)],
                           k=[mk[w][rows, h // 2, :] for w in (0, 1)],
                           v=[(lambda kb, w=w, h=h, mv=mv: mv[w][:, kb, (h // 2) * P:(h // 2 + 1) * P]) for w in (0, 1)],
                           nkb=2, kb=lambda kb: (0, SEQ), scale=64 ** -0.5, y=4 + h, rows=rows,
                           ytile=Y_DM + 2 + h // 2, ztile=6 + h // 2, bank=6 + h % 2, first=True, last=True, **MEMORY))
        mla = []
        for h in range(NH):
            lv = [cat(w, LV, 4).rearrange("p (t n) -> p t n", t=NT) for w in (0, 1)]
            mla.append(dict(kind="bias", q=[part(w, LQ + h)[0:96] for w in (0, 1)],
                            k=[part(w, LK + h)[0:96] for w in (0, 1)],
                            v=[(lambda kb, w=w, h=h, lv=lv: lv[w][:, kb, (h // 2) * P:(h // 2 + 1) * P]) for w in (0, 1)],
                            nkb=4, kb=causal_kb, b0=[384 - 128 * q_ for q_ in range(4)], scale=96 ** -0.5,
                            y=h, rows=slice(64 * (h % 2), 64 * (h % 2) + 64), ytile=LQ + h // 2, ztile=h // 2,
                            bank=6 + h % 2, first=True, last=True, **CAUSAL))
        for maps in (ab, dm, mla):
            n = ng = nt = 0
            s_bank, t_bank = {}, {}
            for i, m in enumerate(maps):
                m["g0"], m["t0"] = ng, nt
                m["s_free"], m["t_free"] = [], []
                for g, qs in enumerate(m["groups"]):
                    b = m["place"][qs[0]][0]
                    m["s_free"].append(s_bank.get(b))
                    ng += 1
                    s_bank[b] = ("exped", i + 1) if m["kind"] == "mem" else ("biased", ng)
                    if m.get("mode") != "hold":
                        m["t_free"].append(t_bank.get(b))
                        nt += 1
                        t_bank[b] = nt
                m["g1"], m["t1"] = ng, nt
                m["i"], m["prev"] = i, maps[i - 1]
                m["prev2"] = maps[i - 2]["t1"] if i >= 2 else 0
                if m.get("mode") != "hold":
                    n += 1
                m["n"] = n
                if maps is mla or m["kind"] == "mem":
                    m["yf"] = m["y"] - 3 if maps is dm else m["y"] + 1
                m["ylo"] = {1: 1, 3: 2}.get(m["y"], m["y"] - 1) if maps is dm else m["y"] + 1
                at, m["p"] = 0, []
                for k0, nk in m["spans"]:
                    m["p"].append(at)
                    at += nk
        GROUP = {"ab": (ab, PT_AB), "dm": (dm, PT_DM), "mla": (mla, PT_L)}

        def prob(m):
            return PB[:, (m["i"] % 2) * 1280:(m["i"] % 2 + 1) * 1280]

        def prob_of(m, q):
            if q >= 4:
                return YT[:, (m["i"] % 2) * P + 32 * (q - 4):(m["i"] % 2) * P + 32 * (q - 3)]
            return prob(m)[:, m["p"][q]:m["p"][q] + m["spans"][q][1]]

        def prob_cmp(m):
            return YT[:, (m["i"] % 2) * P:(m["i"] % 2 + 1) * P]

        def turned_cmp(m):
            return FX[:, 1, (m["i"] % 2) * P:(m["i"] % 2 + 1) * P]

        def v_cmp(q):
            return FX[:, 0, q * P:(q + 1) * P]

        def bias_of(m, q):
            if q >= 4:
                return BCMP[:, m["h"], q - 4, :]
            return bias_row(m)[:, m["b0"][q]:m["b0"][q] + m["spans"][q][1]]

        def bias_row(m):
            if "bias" in m:
                return FX[:, 2 + m["bias"] % 2, :]
            return TRI[:, :]

        BCMP = FX[:, 4:6, :].rearrange("p a b -> p (a b)").rearrange("p (h q c) -> p h q c", h=NH, q=NT)

        def stat(m, k):
            return ST[:, m["i"] % 4, 8 * k:8 * k + (8 if "cmp" in m else 4)]

        MAX, NMAX, SUM, SINK, WT = range(5)

        TOK = PB[:, 0:2048]
        HEADS = [
            dict(nt=2, n=512, parts=[(0, 4, 64, "mkn")], rope=None, turn=[(0, 128), (128, 128)], tiles=[MK], memk=True, rt=R_MEM, v=(256, 256, MV)),
            dict(nt=4, n=416, parts=[(0, 1, 256, None), (256, 1, 128, None)], rope=None,
                 turn=[(0, 128), (128, 128), (256, 128)], tiles=[CQ, CQ + 1, CKV], rt=R_TWO, gain=[("g_q2", 0), ("g_q2", 1), ("g_kv2", 0)]),
            dict(nt=4, n=512, parts=[(0, 8, 32, "dqn"), (256, 8, 32, "dkn")], rope=(0, 16, 32, 0),
                 turn=[(128 * j, 128) for j in range(4)], tiles=[DQ, DQ + 1, DK, DK + 1], rt=R_TWO),
            dict(nt=4, n=512, parts=[(256, 4, 64, "mqn")], rope=None, turn=[(256, 128), (384, 128)], tiles=[MQ, MQ + 1],
                 rt=R_TWO, v=(0, 256, DV)),
        ] + [dict(nt=4, n=384, parts=[(0, 4, 96, g)], rope=(0, 4, 96, 64), turn=[(96 * j, 96) for j in range(4)],
                  tiles=[base + j for j in range(4)], kpart=kp)
             for g, base, kp in (("qn", LQ, False), ("qn", LQ + 4, False), ("kn", LK, True), ("kn", LK + 4, True))]

        def scratch(k):
            fx = FX[:, :, :].rearrange("p a b -> p (a b)")
            if k < 4:
                return fx[:, 0:2048], fx[:, 0:2048], fx[:, 2048:4096]
            return PB[:, 1536:3072], PB[:, 3072:3584], PB[:, 1536:2048]

        def turned_aps(m, pt, q, w):
            if q >= 4:
                return turned_cmp(m), PS[:, 5, 256:384]
            (b, o), (k0, nk) = m["place"][q], m["spans"][q]
            arena = ((BHI, BLO) if pt < 24 else (HHI, HLO))[w]
            t0, n = pt % 24 + k0 // P, nk // P
            return arena[:, t0:t0 + n, q * P:(q + 1) * P], PS[:, 3 + b, o:o + nk].rearrange("p (n c) -> p n c", n=n)

        def tile_at(buf, i, s):
            return buf[:, 2 * i + s, :] if isinstance(i, int) else \
                buf[:, bass.ds(2 * i + s, 1), :].rearrange("p a b -> p (a b)")

        def gain_at(name, i, s):
            return col(name, 2 * i + s) if isinstance(i, int) else CL[:, bass.ds(2 * i + (s + COL[name]), 1)]

        NORM_GAIN = ["g_mix", "g_ffn", "g_2"]
        memx = FX[:, 0:4, :].rearrange("p a b -> p (a b)")
        mem_part = [cat(w, 0, 4).rearrange("p (k n) -> p k n", k=KT) for w in (0, 1)]

        block = ctx.enter_context(nc.Block())

        @block.sync
        def _(sp):
            for s in range(2):
                sp.dma_start(RAW[:, s, :], t["wstream"][s]).then_inc(raw_loaded[s], 16)
            with sp.Fori(1, NU // 2) as i:
                for s in range(2):
                    sp.wait_ge(split_lo, 2 * i + (s - 1))
                    sp.dma_start(RAW[:, s, :], t["wstream"][2 * i + s]).then_inc(raw_loaded[s], 16)

        @block.gpsimd
        def _(pool):
            pool.memset(IDN[:, :], 0.0)
            pool.memset(TRI[:, :], 0.0)
            pool.memset(BONE[:, :], 0.0)
            pool.memset(ONE[:, :], 1.0).then_inc(consts, 1)
            pool.wait_ge(consts, 1)
            pool.affine_select(out=IDN[:, :], in_=IDN[:, :], compare_op=ALU.not_equal, fill=1.0, base=0,
                               pattern=[[-1, P]], channel_multiplier=1)
            pool.affine_select(out=TRI[:, :], in_=TRI[:, :], compare_op=ALU.is_ge, fill=NEG, base=SEQ - P,
                               pattern=[[-1, SEQ]], channel_multiplier=1).then_inc(consts, 1)
            pool.wait_ge(consts, 2)
            pool.memset(BONE[0:64, 0:64], 1.0).then_inc(consts, 1)
            pool.wait_ge(consts, 3)
            pool.memset(BONE[64:128, 64:128], 1.0).then_inc(consts, 1)
            pool.wait_ge(consts, 4)
            with pool.Fori(0, NU // 2) as i:
                for s in range(2):
                    pool.wait_ge(split_hi, 2 * i + (s + 1))
                    pool.tensor_tensor(WLO[:, s, :], RAW[:, s, :], WHI[:, s, :].bitcast(F), ALU.subtract).then_inc(split_lo, 1)

        @block.scalar
        def _(act):
            chain = Chain(act, act_step)

            def stream(c, n=0, i=0):
                if isinstance(c, int) and n == 0 and c >= NU:
                    return
                act.wait_ge(raw_loaded[c % 2], 16 * (c // 2 + 1) + 8 * n * i)
                if c >= 2 or n:
                    act.wait_ge(unit_used, (c - 1) + n * i)
                act.activation(WHI[:, c % 2, :], RAW[:, c % 2, :], ACT.Copy).then_inc(split_hi, 1)

            def used(c, n=0, i=0):
                act.wait_ge(unit_used, (c + 1) + n * i)

            def norm_tile(k, i, s, done=None):
                if done is not None:
                    act.wait_ge(done, 2 * i + (s + 1))
                per = 2 if k == 2 else 1
                x = tile_at(X, i, s)
                for m in range(per):
                    n = 8 * k + per * s + m
                    if not isinstance(i, int) or 2 * per * i + n >= 2:
                        act.wait_ge(n_acc, 2 * per * i + (n - 1))
                    act.activation(SQ[n % 2], x, ACT.Square, scale=gain_at("g_final", i, s) if m else 1.0).then_inc(n_sq, 1)
                act.activation(tile_at(HHI, i, s), x, ACT.Copy, scale=gain_at(NORM_GAIN[k], i, s)).then_inc(n_hi, 1)

            def norm_root(n, *bufs):
                act.wait_ge(n_rin, n)
                for b in bufs:
                    ins = act.activation(b, b, ACT.Sqrt)
                ins.then_inc(n_rstd, 1)

            act.dma_start(CL[:, :], t["cols"]).then_inc(ld_cols, 16)
            for j in range(4):
                act.dma_start(X[:, 2 * j:2 * j + 2, :], t["xT"][:, 2 * j:2 * j + 2, :]).then_inc(ld_x[j], 16)
            act.dma_start(RW[:, :], bass.AP(t["rows"].tensor, 0, [[0, P], [1, NROW]])).then_inc(ld_small, 16)
            act.dma_start(TBL[0:NBUCKET, :], t["table"]).then_inc(ld_small, 16)
            act.dma_start(POS[:, :], t["pos"]).then_inc(ld_small, 16)
            act.dma_start(FX[0:NBUCKET + 1, :, :].rearrange("p a b -> p (a b)")[:, 0:OH], t["onehot"]).then_inc(ld_oh, 16)
            act.wait_ge(ld_cols, 16)
            for i in range(4):
                act.wait_ge(ld_x[i], 16)
                for s in range(2):
                    norm_tile(0, i, s)
                if i < 2:
                    stream(i)
            norm_root(1, RSTD, RT[:, 0:4])

            act.wait_ge(oh_mm, 1)
            for b in range(5):
                a, e = OH * b // 5, OH * (b + 1) // 5
                ins = act.activation(FX[0:16, :, :].rearrange("p a b -> p (a b)")[:, a:e], PS[0:16, 2 + b, 0:e - a], ACT.Copy)
            ins.then_inc(oh_ev, 1)
            act.wait_ge(oh_ev, 1)
            act.dma_start(tb_dram, FX[0:16, :, :].rearrange("p a b -> p (a b)")[:, 0:OH]).then_inc(st_rows, 16)
            act.dma_start(W2, t["w2"]).then_inc(ld_w2, 16)

            u = UNIT["proj"]

            def proj_epilogue(c, n, i, tile):
                act.wait_ge(scaled, (c + 1) + n * i)
                act.activation(tile, PS[:, c % 2, :], ACT.Copy).then_inc(proj_hi, 1)
                stream(c + 2, n, i)

            for c in range(2):
                proj_epilogue(u + c, 0, 0, hi(c))
            with act.Fori(1, 5) as i:
                for s in range(2):
                    proj_epilogue(u + s, 2, i, BHI[:, bass.ds(2 * i + s, 1), :].rearrange("p a b -> p (a b)"))
            proj_epilogue(u + 10, 0, 0, hi(10))
            for c in (11, 12):
                stream(u + c + 2)

            def bias_load(y):
                h = (y % 8 // 2) + 4 * (y % 2) + (8 if y >= 8 else 0)
                n, src = (256, bias_a) if y < 8 else (SEQ, bias_b)
                act.dma_start(FX[:, 2 + y % 2, 0:n], src[h % 8]).then_inc(ld_bias[y % 2], 16)

            act.wait_ge(st_rows, 16)
            for dst, h0, off, n in ((bias_a, 0, 0, 256), (bias_b, 8, OH_A, SEQ)):
                src = bass.AP(tb_dram.tensor, h0 * OH + off + P - 1, [[OH, NH], [-1, P], [1, n]])
                act.dma_start(dst, src).then_inc(spread, 16)
            for qt in range(NT):
                for pg in range(8):
                    src = bass.AP(tb_dram.tensor, 8 * OH + OH_A + OH_B + 15 * CMP_A + 33 - 8 * qt - pg,
                                  [[OH, NH], [-CMP_A, 16], [1, N_CMP]])
                    act.dma_start(bias_c[:, 16 * pg:16 * pg + 16, qt, :], src).then_inc(spread, 16)

            u = UNIT["vtok"]
            act.wait_ge(n_rstd, 1)
            for c in range(4):
                if c == 2:
                    act.wait_ge(ang_ready, 1)
                    act.activation(COS[:, :, 16:32], COS[:, :, 16:32], ACT.Sin)
                    act.activation(SIN[:, :, 16:32], SIN[:, :, 16:32], ACT.Sin).then_inc(sin_ready, 1)
                if c == 3:
                    used(u + 3)
                    vh = cat(0, V_AT, 3).rearrange("p (t n) -> p t n", t=NT)
                    for tk in range(NT):
                        act.activation(vh[:, tk, :], PS[:, 2 + tk, 0:384], ACT.Copy, scale=RT[:, tk:tk + 1]).then_inc(v_hi, 1)
                    for tk in range(NT):
                        ins = act.activation(GATE[:, tk, :], PS[:, 2 + tk, 384:408], ACT.Sigmoid, scale=RT[:, tk:tk + 1])
                    ins.then_inc(v_hi, 1)
                stream(u + c + 2)

            for w in range(2):
                act.wait_ge(cb_built, w + 1)
                act.activation(cat(0, 14 + 4 * w, 4), PB[:, 0:2048], ACT.Copy).then_inc(cb_hi, 1)
            u = UNIT["cmp"]
            for c in range(8):
                stream(u + c + 2)
                if c == 0:
                    act.wait_ge(spread, 16 * 34)
                    act.wait_ge(tbl_ready, 2)
                    for h in range(NH):
                        dst = FX[:, 4 + h // 4, (h % 4) * P:(h % 4 + 1) * P].rearrange("p (q c) -> p q c", q=NT)[:, :, 0:N_CMP]
                        act.dma_start(dst, bias_c[h]).then_inc(ld_cmp, 16)
                    bias_load(0)
                    bias_load(1)
                if c % 4 == 3:
                    used(u + c)
                    w = c // 4
                    act.activation(FX[:, 6, 256 * w:256 * w + 256], PS[:, 6 + w, 0:256], ACT.Gelu_apprx_tanh).then_inc(gelu_done, 1)
            act.wait_ge(gelu_t, 1)
            act.activation(FX[:, 7, :], PS[:, 0, :], ACT.Copy).then_inc(gelu_copied, 1)
            act.wait_ge(cmp_mm, 1)
            for g in range(2):
                ins = act.activation(hi(22)[64 * g:64 * g + 64, KC:KC + 32], PS[64 * g:64 * g + 64, 1, 64 * g:64 * g + 32], ACT.Copy)
            ins.then_inc(cmp_hi, 1)

            def attention(name):
                maps, pts = GROUP[name]
                A = ATT[name]
                for i in range(-1, len(maps) + 2):
                    if 0 <= i - 1 < len(maps) and maps[i - 1].get("mode") != "hold":
                        m = maps[i - 1]
                        if m["n"] > 2:
                            act.wait_ge(A["pv"], m["n"] - 2)
                        pt = pts[m["n"] % 2]
                        for g, qs in enumerate(m["groups"]):
                            act.wait_ge(A["turned"], m["t0"] + g + 1)
                            for q in [q for q in qs if q <= 4]:
                                ins = act.activation(*turned_aps(m, pt, q, 0), ACT.Copy)
                            ins.then_inc(A["p_hi"], 1)
                    if i + 1 < len(maps):
                        m = maps[i + 1]
                        for g, qs in enumerate(m["groups"]):
                            act.wait_ge(A["biased"], m["g0"] + g + 1)
                            for q in qs:
                                if m.get("sink"):
                                    act.activation(stat(m, SINK)[:, q:q + 1], row("sinks", 8)[:, m["h"]:m["h"] + 1],
                                                   ACT.Exp, bias=stat(m, NMAX)[:, q:q + 1], scale=-1.0)
                                nk = m["spans"][q][1]
                                dst = prob_of(m, q)
                                b, o = m["place"][q]
                                if m["kind"] == "mem":
                                    src, sc = PS[:, b, o:o + nk], m["scale"]
                                else:
                                    src, sc = dst, -1.0
                                ins = act.activation(dst, src, ACT.Exp, bias=stat(m, NMAX)[:, q:q + 1], scale=sc,
                                                     accum_out=stat(m, SUM)[:, q:q + 1])
                        ins.then_inc(A["exped"], 1)
                        if "bias" in m and m["last"] and m["bias"] + 1 < 16 and m["bias"] >= 1:
                            act.wait_ge(A["biased"], m["g0"])
                            bias_load(m["bias"] + 1)
                    if 0 <= i - 2 < len(maps) and maps[i - 2]["last"]:
                        m = maps[i - 2]
                        rows, yt = m["rows"], hi(m["ytile"])
                        act.wait_ge(A["pv"], m["n"])
                        if name == "ab":
                            act.activation(yt[rows, :], PS[rows, m["bank"], :], ACT.Copy).then_inc(A["y_hi"], 1)
                        elif m.get("diff"):
                            j = m["y"] // 2
                            if m["y"] == 2:
                                act.wait_ge(A["y_lo"], 1)
                            act.activation(YT[rows, :], PS[rows, m["bank"], :], ACT.Copy).then_inc(A["y_hi"], 1)
                            if m["bank"] == 7:
                                act.wait_ge(A["y_hi"], m["y"] + 1)
                                act.activation(YSQ, YT, ACT.Square).then_inc(dm_sq, 1)
                                act.wait_ge(dm_rin, 2 * j + 2)
                                act.activation(YSQ, YSQ, ACT.Sqrt).then_inc(dm_rstd, 1)
                                act.wait_ge(dm_y, j + 1)
                                act.activation(yt, YT, ACT.Copy).then_inc(dm_hi, 1)
                        else:
                            act.wait_ge(A["y_f"], m["yf"])
                            act.activation(yt[rows, :], YT[rows, :], ACT.Copy).then_inc(A["y_hi"], 1)

            attention("ab")

            u = UNIT["merge"]
            def merge(i):
                for s in range(2):
                    for e in range(2):
                        c = u + 3 * s + e
                        act.wait_ge(scaled, 4 * i + (SCALED["merge"] + 2 * s + e + 1))
                        if not isinstance(i, int):
                            act.wait_ge(merge_dve, 8 * i + (4 * s - 8 + 2 + 1))
                        act.activation(FX[:, 2 * e + s, :], PS[:, 4 * s + e, :], ACT.Sigmoid).then_inc(merge_act, 1)
                        stream(c + 2, 6, i)
                    c = u + 3 * s + 2
                    stream(c + 2, 6, i)
                    act.wait_ge(merge_dve, 8 * i + (4 * s + 3))
                    dst = hi(14 + s) if isinstance(i, int) else \
                        BHI[:, bass.ds(2 * i + (14 + s), 1), :].rearrange("p a b -> p (a b)")
                    act.activation(dst, FX[:, 4 + s, :], ACT.Copy).then_inc(merge_act, 1)
            merge(0)
            with act.Fori(1, 4) as i:
                merge(i)

            def plain_stream(name):
                c0, n = UNIT[name], dict(_PLAN)[name]
                assert n % 2 == 0
                with act.Fori(0, n // 2) as i:
                    for s in range(2):
                        stream(c0 + s + 2, 2, i)

            def stream_and_norm(name, per, k, done, i):
                for s in range(2):
                    for e in range(per):
                        stream(UNIT[name] + per * s + e + 2, 2 * per, i)
                    norm_tile(k, i, s, done)

            stream_and_norm("wout", 1, 1, x1_done, 0)
            with act.Fori(1, 4) as i:
                stream_and_norm("wout", 1, 1, x1_done, i)
            norm_root(2, RSTD)

            u = UNIT["ffn"]
            def ffn(i):
                for s in range(2):
                    pair = 2 * i + s
                    for e in range(2):
                        c = u + 2 * s + e
                        act.wait_ge(scaled, 4 * i + (SCALED["ffn"] + 2 * s + e + 1))
                        if not isinstance(i, int):
                            act.wait_ge(ffn_dve, 12 * i + (6 * s - 12 + 5))
                        at = COL["conv"] + 4 * e + 8 * s
                        cv = CL[:, at:at + 4] if isinstance(i, int) else CL[:, bass.ds(16 * i + at, 4)]
                        act.activation(FX[:, 2 * e + s, :], PS[:, 2 * e + s, :], ACT.Identity,
                                       bias=cv[:, 3:4], scale=cv[:, 2:3]).then_inc(ffn_act, 1)
                        stream(c + 2, 4, i)
                    act.wait_ge(ffn_dve, 12 * i + (6 * s + 4))
                    act.activation(FX[:, 4 + s, :], FX[:, 2 + s, :], ACT.Silu).then_inc(ffn_act, 1)
                    act.wait_ge(ffn_dve, 12 * i + (6 * s + 5))
                    dst = hi(s) if isinstance(i, int) else BHI[:, bass.ds(pair, 1), :].rearrange("p a b -> p (a b)")
                    act.activation(dst, FX[:, 6 + s, :], ACT.Copy).then_inc(ffn_act, 1)
            ffn(0)
            with act.Fori(1, NF // 2) as i:
                ffn(i)

            act.wait_ge(ffn_dve, 6 * NF)
            act.dma_start(FX[:, 0:4, :].rearrange("p a b -> p (a b)"), t["memT"]).then_inc(ld_mem, 16)
            stream_and_norm("down", 3, 2, x2_done, 0)
            act.wait_ge(ld_mem, 16)
            act.activation(FX[:, 4:8, :].rearrange("p a b -> p (a b)"), memx, ACT.Square).then_inc(mem_sq, 1)
            with act.Fori(1, 4) as i:
                stream_and_norm("down", 3, 2, x2_done, i)
            for kt in range(KT):
                act.activation(mem_part[0][:, kt, :], memx[:, 256 * kt:256 * kt + 256], ACT.Copy,
                               scale=col("g_mem", kt)).then_inc(n_hi, 1)

            def head_evac(k):
                h = HEADS[k]
                if k:
                    act.wait_ge(h_tr, k)
                for tk in range(h["nt"]):
                    if h.get("kpart"):
                        dst = TOK[:, 0:1536].rearrange("p (t h e) -> p t h e", t=NT, h=4)[:, tk]
                        act.activation(dst[:, :, 0:64], PS[:, tk, 0:256].rearrange("p (h e) -> p h e", h=4), ACT.Copy)
                        kr = KR[:, tk, :]
                        ins = act.activation(dst[:, :, 64:96], kr[:, None, :].broadcast_to([P, 4, 32]), ACT.Copy)
                    else:
                        ins = act.activation(TOK[:, tk * h["n"]:(tk + 1) * h["n"]], PS[:, tk, 0:h["n"]], ACT.Copy,
                                             scale=1.0 if "rt" not in h else RT[:, h["rt"] + tk:h["rt"] + tk + 1])
                ins.then_inc(h_tok, 1)

            def head_square(k):
                h = HEADS[k]
                act.wait_ge(h_tok, k + 1)
                n = h["nt"] * h["n"]
                act.activation(scratch(k)[0][:, 0:n], TOK[:, 0:n], ACT.Square).then_inc(h_sq, 1)
                if "v" in h:
                    o, w, tile = h["v"]
                    v = cat(0, tile, h["nt"] * w // SEQ).rearrange("p (t n) -> p t n", t=h["nt"])
                    src = TOK[:, 0:n].rearrange("p (t n) -> p t n", t=h["nt"])[:, :, o:o + w]
                    act.activation(v, src, ACT.Copy).then_inc(h_v, 1)

            def head_root(k):
                act.wait_ge(h_rin, k + 1)
                act.activation(SS[:, :], SS[:, :], ACT.Sqrt).then_inc(h_rs, 1)

            def head_hi(k):
                h = HEADS[k]
                act.wait_ge(h_tr, k + 1)
                for j, tile in enumerate(h["tiles"]):
                    w = h["turn"][0][1]
                    if h.get("memk"):
                        ins = act.activation(hi(tile), PS[:, 4, :], ACT.Copy)
                    elif "gain" in h:
                        ins = act.activation(hi(tile), PS[:, 4 + j, :], ACT.Copy, scale=col(*h["gain"][j]))
                    else:
                        ins = act.activation(hi(tile)[0:w, :], PS[0:w, 4 + j, :], ACT.Copy)
                ins.then_inc(h_hi, 1)

            u = UNIT["mem"]
            for c in range(4):
                stream(u + c + 2)
            norm_root(3, RT[:, R_MEM:10])
            used(u + 3)
            act.wait_ge(n_rstd, 3)
            head_evac(0)
            head_square(0)
            norm_root(4, RSTD, YT)
            for k in range(1, 4):
                u = UNIT["tok2"] + 4 * (k - 1)
                stream(u + 2)
                head_root(k - 1)
                for c in range(1, 4):
                    stream(u + c + 2)
                used(u + 3)
                head_evac(k)
                head_hi(k - 1)
                head_square(k)
            head_root(3)
            u = UNIT["z"]
            act.wait_ge(h_nrm, 4)
            for c in range(10):
                if c < 8:
                    stream(u + c + 2)
                if c >= 2:
                    act.wait_ge(scaled, SCALED["z"] + c - 1)
                    act.activation(FX[:, c - 2, :], PS[:, (c - 2) % 4, :], ACT.Silu).then_inc(z_done, 1)
            head_hi(3)
            act.wait_ge(lam_sum, 1)
            act.activation(LAM[:, 2:4], LAM[:, 0:2], ACT.Exp).then_inc(lam_exp, 1)
            attention("dm")

            u = UNIT["uq"]
            stream(u + 2)
            used(u)
            head_evac(4)
            head_square(4)
            stream(u + 3)
            head_root(4)
            used(u + 1)
            head_evac(5)
            head_hi(4)
            head_square(5)
            head_root(5)
            for k in (6, 7):
                act.wait_ge(k_mm, k - 5)
                head_evac(k)
                head_hi(k - 1)
                head_square(k)
                head_root(k)
            used(UNIT["ukv"])
            vh = cat(0, LV, 4).rearrange("p (t n) -> p t n", t=NT)
            for tk in range(NT):
                act.activation(vh[:, tk, :], PS[:, tk, :], ACT.Copy).then_inc(vm_hi, 1)
            head_hi(7)
            stream(UNIT["ukv"] + 2)
            attention("mla")
            u = UNIT["wout2"]
            with act.Fori(0, 3) as i:
                for s in range(2):
                    stream(u + 2 + s, 2, i)
            for n in range(KT):
                act.wait_ge(y_out, n + 1)
                act.dma_start(out[:, n, :], X[:, n, :]).then_inc(stored, 16)
            act.wait_ge(stored, 16 * KT)

        @block.vector
        def _(dve):
            chain = Chain(dve, dve_step)
            link = chain.link

            def norm_tile(k, i, s):
                per = 2 if k == 2 else 1
                for m in range(per):
                    n = 8 * k + per * s + m
                    dve.wait_ge(n_sq, 2 * per * i + (n + 1))
                    if not isinstance(i, int) or 2 * i + s:
                        dve.wait_ge(n_acc, 2 * per * i + (n - per + 1))
                    dve.tensor_tensor(ACC[m], ACC[m], SQ[n % 2], ALU.add).then_inc(n_acc, 1)
                dve.wait_ge(n_hi, 2 * i + (8 * k + s + 1))
                dve.scalar_tensor_tensor(out=tile_at(HLO, i, s), in0=tile_at(X, i, s), scalar=gain_at(NORM_GAIN[k], i, s),
                                         in1=tile_at(HHI, i, s).bitcast(F), op0=ALU.mult, op1=ALU.subtract).then_inc(n_lo, 1)

            def mean_inverse(dst, src):
                link(dve.tensor_scalar(dst, src, 1.0 / D, EPS, ALU.mult, ALU.add))
                return dve.reciprocal(dst, dst)

            def scale(bank):
                dve.tensor_tensor(PS[:, bank, :], PS[:, bank, :], RSTD, ALU.mult).then_inc(scaled, 1)

            link(dve.memset(ACC[0], 0.0))
            dve.wait_ge(ld_cols, 16)
            for i in range(4):
                for s in range(2):
                    norm_tile(0, i, s)
            dve.wait_ge(n_tot, 1)
            link(mean_inverse(RSTD, PS[:, 7, :]))
            mean_inverse(RT[:, 0:4], PS[:, 6, 0:4]).then_inc(n_rin, 1)
            dve.wait_ge(ld_small, 48)

            dve.memset(TBL[NBUCKET:NBUCKET + 1, :], NEG)
            link(dve.tensor_scalar(TBL[0:NBUCKET, :], TBL[0:NBUCKET, :], 8.0, None, ALU.mult))
            link(dve.tensor_scalar(row("sinks", 8), row("sinks", 8), -1.0, None, ALU.mult))
            dve.memset(MSK[:, :], 1.0).then_inc(tbl_ready, 1)
            link(dve.tensor_tensor(CL[:, COL["g_2"]:COL["g_2"] + 8], CL[:, COL["g_2"]:COL["g_2"] + 8],
                                   CL[:, COL["g_final"]:COL["g_final"] + 8], ALU.mult))
            dve.wait_ge(n_rstd, 1)

            def low_from_psum(dst_lo, dst_hi, src):
                return dve.tensor_tensor(dst_lo, src, dst_hi.bitcast(F), ALU.subtract)

            for c in range(2):
                dve.wait_ge(unit_used, UNIT["proj"] + c + 1)
                scale(c)
                dve.wait_ge(proj_hi, c + 1)
                low_from_psum(lo(c), hi(c), PS[:, c, :]).then_inc(proj_out, 1)
            with dve.Fori(1, 5) as i:
                for s in range(2):
                    dve.wait_ge(unit_used, 2 * i + (UNIT["proj"] + s + 1))
                    scale(s)
                    dve.wait_ge(proj_hi, 2 * i + (s + 1))
                    low_from_psum(BLO[:, bass.ds(2 * i + s, 1), :].rearrange("p a b -> p (a b)"),
                                  BHI[:, bass.ds(2 * i + s, 1), :].rearrange("p a b -> p (a b)"),
                                  PS[:, s, :]).then_inc(proj_out, 1)
            dve.wait_ge(unit_used, UNIT["proj"] + 11)
            scale(0)
            dve.wait_ge(proj_hi, 11)
            low_from_psum(lo(10), hi(10), PS[:, 0, :]).then_inc(proj_out, 1)
            dve.wait_ge(st_rows, 16)
            for c in (11, 12):
                dve.wait_ge(unit_used, UNIT["proj"] + c + 1)
                dve.tensor_tensor(FX[:, c - 11, :], PS[:, c % 2, :], RSTD, ALU.mult).then_inc(proj_out, 1)
            link(dve.memset(MSK[0:31, 0:1], 0.0))
            dve.memset(FX[:, 4:6, :], NEG * 8).then_inc(tbl_ready, 1)

            link(dve.tensor_copy(KR[:, :, 0], POS[:, :]))
            ang = COS[:, :, 0:16]
            link(dve.tensor_tensor(ang, KR[:, :, 0:1].broadcast_to([P, NT, 16]),
                                   row("inv", 16)[:, None, :].broadcast_to([P, NT, 16]), ALU.mult))
            magic = 1.5 * 2.0 ** 23
            c1, c2, c3 = 6.28125, float(np.float32(2 * math.pi - 6.28125)), 0.0
            c3 = 2 * math.pi - c1 - c2
            for dst, shift in ((COS, 0.25), (SIN, 0.0)):
                turns, r = KR[:, :, 16:32], dst[:, :, 16:32]
                link(dve.tensor_scalar(turns, ang, 1.0 / (2 * math.pi), shift, ALU.mult, ALU.add))
                link(dve.tensor_scalar(turns, turns, magic, magic, ALU.add, ALU.subtract))
                link(dve.scalar_tensor_tensor(out=r, in0=turns, scalar=-c1, in1=ang, op0=ALU.mult, op1=ALU.add))
                for c in (c2, c3):
                    link(dve.scalar_tensor_tensor(out=r, in0=turns, scalar=-c, in1=r, op0=ALU.mult, op1=ALU.add))
                link(dve.tensor_scalar(r, r, shift * 2 * math.pi, 3.1415925, ALU.add, ALU.min))
                link(dve.tensor_scalar(r, r, -3.1415925, None, ALU.max))
            dve.memset(SS[:, :], 1.0).then_inc(ang_ready, 1)
            vh, vl = [cat(w, V_AT, 3).rearrange("p (t n) -> p t n", t=NT) for w in (0, 1)]
            for tk in range(NT):
                dve.wait_ge(v_hi, NT + 1)
                dve.scalar_tensor_tensor(out=vl[:, tk, :], in0=PS[:, 2 + tk, 0:384], scalar=RT[:, tk:tk + 1],
                                         in1=vh[:, tk, :].bitcast(F), op0=ALU.mult, op1=ALU.subtract).then_inc(v_lo, 1)
            dve.wait_ge(sin_ready, 1)
            link(dve.tensor_copy(COS[:, :, 0:16], COS[:, :, 16:32]))
            link(dve.tensor_scalar(SIN[:, :, 0:16], SIN[:, :, 16:32], -1.0, None, ALU.mult))

            cb = PB[:, 0:2048].rearrange("p (t g i) -> p t g i", t=16, g=2)
            dve.wait_ge(proj_out, 13)
            link(dve.memset(PB[:, 0:2048], 0.0))
            for w in range(2):
                if w:
                    dve.wait_ge(cb_lo, 1)
                for g in range(2):
                    rows = slice(64 * g, 64 * g + 64)
                    for par in range(2):
                        src = FX[rows, w, par:par + 1]
                        src = bass.AP(src.tensor, src.offset, [list(src.ap[0]), [2, 16], [16, N_CMP]])
                        pos = CL[rows, COL[("pos_k", "pos_v")[w]] + par:COL[("pos_k", "pos_v")[w]] + 32:2]
                        ins = dve.tensor_tensor(cb[64 * par:64 * par + 64, :, g, 0:N_CMP], src,
                                                pos[:, :, None].broadcast_to([64, 16, N_CMP]), ALU.add)
                ins.then_inc(cb_built, 1)
                dve.wait_ge(cb_hi, w + 1)
                dve.tensor_tensor(cat(1, 14 + 4 * w, 4), PB[:, 0:2048], cat(0, 14 + 4 * w, 4).bitcast(F),
                                  ALU.subtract).then_inc(cb_lo, 1)
            dve.wait_ge(cb_built, 2)
            link(dve.memset(FX[:, 0, :], 0.0))
            dve.wait_ge(cmp_hi, 1)
            for g in range(2):
                low_from_psum(lo(22)[64 * g:64 * g + 64, KC:KC + 32], hi(22)[64 * g:64 * g + 64, KC:KC + 32],
                              PS[64 * g:64 * g + 64, 1, 64 * g:64 * g + 32])
            for q in range(NT):
                ins = dve.tensor_copy(v_cmp(q)[32 * q:32 * q + 32, :], PS[0:32, 2, 0:P])
            ins.then_inc(cmp_lo, 1)

            def biased(A, m):
                pr = prob(m)
                if m["i"] and m["prev"].get("mode") == "sub":
                    dve.wait_ge(A["normed"], m["prev"]["t1"])
                if m["prev2"]:
                    dve.wait_ge(A["turned"], m["prev2"])
                if m.get("cmp") is not None and m["bias"] == 8:
                    dve.wait_ge(ld_cmp, 16 * NH)
                if m["kind"] == "mem":
                    for b in range(2):
                        dve.wait_ge(A["scores"], m["g0"] + b + 1)
                        two = slice(2 * b, 2 * b + 2)
                        link(dve.tensor_reduce(stat(m, MAX)[:, two], PS[:, b, :].rearrange("p (q c) -> p q c", q=2),
                                               AX.X, ALU.max))
                        dve.tensor_scalar(stat(m, NMAX)[:, two], stat(m, MAX)[:, two], -m["scale"], None,
                                          ALU.mult).then_inc(A["biased"], 1)
                    return
                if "bias" in m and m["first"]:
                    y = m["bias"]
                    dve.wait_ge(ld_bias[y % 2], 16 * (y // 2 + 1))
                for g, qs in enumerate(m["groups"]):
                    dve.wait_ge(A["scores"], m["g0"] + g + 1)
                    for q in qs:
                        (b, o), (_, nk) = m["place"][q], m["spans"][q]
                        init = row("sinks", 8)[:, m["h"]:m["h"] + 1] if m.get("sink") else 3e38
                        ins = dve.tensor_tensor_reduce(prob_of(m, q), PS[:, b, o:o + nk], bias_of(m, q), -m["scale"], init,
                                                       ALU.add, ALU.min, stat(m, NMAX)[:, q:q + 1])
                    ins.then_inc(A["biased"], 1)

            def normed(A, m):
                pr = prob(m)
                dve.wait_ge(A["exped"], m["i"] + 1)
                if m.get("sink"):
                    link(dve.tensor_tensor(stat(m, SUM), stat(m, SUM), stat(m, SINK), ALU.add))
                link(dve.reciprocal(stat(m, WT), stat(m, SUM)))
                w4 = stat(m, WT)[:, 0:4]
                if "cmp" in m:
                    c4 = stat(m, WT)[:, 4:8]
                    dve.tensor_tensor(c4, c4, GATE[:, :, m["cmp"]], ALU.mult).then_inc(dve_step, 1)
                    chain.n += 1
                if "gate" in m:
                    link(dve.tensor_tensor(w4, w4, GATE[:, :, m["gate"]], ALU.mult))
                if "cmp" in m:
                    link(dve.tensor_tensor(c4, c4, MSK[:, :], ALU.mult))
                if m.get("mode") == "sub":
                    link(dve.tensor_tensor(stat(m, WT), stat(m, WT), LAM[:, 0:1].broadcast_to([P, NT]), ALU.mult))
                for qs in m["groups"]:
                    for q in qs:
                        if q >= 4:
                            if q == 4:
                                p4 = prob_cmp(m).rearrange("p (q c) -> p q c", q=NT)
                                ins = dve.tensor_tensor(p4, p4, c4[:, :, None].broadcast_to([P, NT, 32]), ALU.mult)
                            continue
                        ap = prob_of(m, q)
                        w = stat(m, WT)[:, q:q + 1]
                        if m.get("mode") == "sub":
                            o = PB[:, (1 - m["i"] % 2) * 1280:(2 - m["i"] % 2) * 1280][:, m["p"][q]:m["p"][q] + m["spans"][q][1]]
                            ins = dve.scalar_tensor_tensor(out=ap, in0=ap, scalar=w, in1=o, op0=ALU.mult, op1=ALU.add)
                        else:
                            ins = dve.tensor_scalar(ap, ap, w, None, ALU.mult)
                    if m.get("mode") != "hold":
                        ins.then_inc(A["normed"], 1)
                if m.get("mode") == "hold":
                    link(ins)

            def attention(name):
                maps, pts = GROUP[name]
                A = ATT[name]
                for i in range(-1, len(maps) + (2 if name == "ab" else 3)):
                    steps = [(biased, i + 1), (normed, i)]
                    for f, j in (steps[::-1] if name == "dm" else steps):
                        if 0 <= j < len(maps):
                            f(A, maps[j])
                    if 0 <= i - 3 < len(maps) and "yf" in maps[i - 3]:
                        m = maps[i - 3]
                        rows = m["rows"]
                        dve.wait_ge(A["y_hi"], m["y"] + 1)
                        low_from_psum(lo(m["ytile"])[rows, :], hi(m["ytile"])[rows, :], YT[rows, :]).then_inc(A["y_lo"], 1)
                    if 0 <= i - 1 < len(maps) and maps[i - 1].get("mode") != "hold":
                        m = maps[i - 1]
                        pt = pts[m["n"] % 2]
                        for g, qs in enumerate(m["groups"]):
                            dve.wait_ge(A["p_hi"], m["t0"] + g + 1)
                            for q in [q for q in qs if q < 4]:
                                dst, src = turned_aps(m, pt, q, 1)
                                ins = low_from_psum(dst, turned_aps(m, pt, q, 0)[0], src)
                            ins.then_inc(A["p_lo"], 1)
                    if 0 <= i - 2 < len(maps) and maps[i - 2]["last"]:
                        m = maps[i - 2]
                        rows, yh, yl = m["rows"], hi(m["ytile"]), lo(m["ytile"])
                        ps = PS[rows, m["bank"], :]
                        if name == "ab":
                            dve.wait_ge(A["y_hi"], m["y"] + 1)
                            low_from_psum(yl[rows, :], yh[rows, :], ps).then_inc(A["y_lo"], 1)
                        elif m.get("diff"):
                            if m["bank"] == 7:
                                j = m["y"] // 2
                                dve.wait_ge(dm_tot, j + 1)
                                dve.tensor_scalar(YSQ, PS[:, 7, :], 1.0 / 64, EPS, ALU.mult, ALU.add).then_inc(dm_rin, 1)
                                dve.wait_ge(dm_rin, 2 * j + 1)
                                dve.reciprocal(YSQ, YSQ).then_inc(dm_rin, 1)
                                dve.wait_ge(dm_rstd, j + 1)
                                link(dve.scalar_tensor_tensor(out=YT, in0=YT, scalar=col("subln"), in1=YSQ,
                                                              op0=ALU.mult, op1=ALU.mult))
                                dve.scalar_tensor_tensor(out=YT, in0=YT, scalar=1.0 - LAM_INIT, in1=FX[:, m["ztile"], :],
                                                         op0=ALU.mult, op1=ALU.mult).then_inc(dm_y, 1)
                                dve.wait_ge(dm_hi, j + 1)
                                low_from_psum(yl, yh, YT).then_inc(A["y_lo"], 1)
                        else:
                            dve.wait_ge(A["pv"], m["n"])
                            if m["ylo"] > 2:
                                dve.wait_ge(A["y_lo"], m["ylo"] - 2)
                            dve.tensor_tensor(YT[rows, :], ps, FX[rows, m["ztile"], :], ALU.mult).then_inc(A["y_f"], 1)

            attention("ab")

            def merge(i):
                for s in range(2):
                    d = 8 * i + 4 * s
                    for e in range(2):
                        dve.wait_ge(unit_used, 6 * i + (UNIT["merge"] + 3 * s + e + 1))
                        scale(4 * s + e)
                    dve.wait_ge(unit_used, UNIT["merge"] + 6 * i + (3 * s + 3))
                    for e in range(2):
                        dve.wait_ge(merge_act, 6 * i + (3 * s + 1 + e))
                        dve.tensor_tensor(FX[:, 4 + 2 * e + s, :], PS[:, 4 * s + 2 + e, :], FX[:, 2 * e + s, :],
                                          ALU.mult).then_inc(merge_dve, 1)
                    dve.wait_ge(merge_dve, d + 2)
                    dve.tensor_tensor(FX[:, 4 + s, :], FX[:, 4 + s, :], FX[:, 6 + s, :], ALU.add).then_inc(merge_dve, 1)
                    dve.wait_ge(merge_act, 6 * i + (3 * s + 3))
                    if isinstance(i, int):
                        h_, l_ = hi(14 + s), lo(14 + s)
                    else:
                        h_, l_ = [a[:, bass.ds(2 * i + (14 + s), 1), :].rearrange("p a b -> p (a b)") for a in (BHI, BLO)]
                    low_from_psum(l_, h_, FX[:, 4 + s, :]).then_inc(merge_dve, 1)
            merge(0)
            with dve.Fori(1, 4) as i:
                merge(i)

            def residual(name, per, done, k=None):
                def one(i):
                    for s in range(2):
                        dve.wait_ge(unit_used, UNIT[name] + 2 * per * i + per * (s + 1))
                        x = X[:, s, :] if isinstance(i, int) else X[:, bass.ds(2 * i + s, 1), :].rearrange("p a b -> p (a b)")
                        dve.tensor_tensor(x, PS[:, s, :], x, ALU.add).then_inc(done, 1)
                        if k is not None:
                            norm_tile(k, i, s)
                one(0)
                with dve.Fori(1, 4) as i:
                    one(i)

            link(dve.memset(ACC[0], 0.0))
            residual("wout", 1, x1_done, 1)
            dve.wait_ge(n_tot, 2)
            mean_inverse(RSTD, PS[:, 7, :]).then_inc(n_rin, 1)
            dve.wait_ge(n_rstd, 2)

            def ffn(i):
                for s in range(2):
                    d = 12 * i + 6 * s
                    for e in range(2):
                        dve.wait_ge(unit_used, 4 * i + (UNIT["ffn"] + 2 * s + e + 1))
                        scale(2 * e + s)
                    for tap in (1, 0):
                        for e in range(2):
                            at = COL["conv"] + 4 * e + 8 * s
                            cv = CL[:, at:at + 4] if isinstance(i, int) else CL[:, bass.ds(16 * i + at, 4)]
                            if tap == 1:
                                dve.wait_ge(ffn_act, 8 * i + (4 * s + 1 + e))
                            else:
                                dve.wait_ge(ffn_dve, d + (1 + e))
                            sh = 2 - tap
                            y = FX[:, 2 * e + s, sh:SEQ]
                            dve.scalar_tensor_tensor(out=y, in0=PS[:, 2 * e + s, 0:SEQ - sh], scalar=cv[:, tap:tap + 1],
                                                     in1=y, op0=ALU.mult, op1=ALU.add).then_inc(ffn_dve, 1)
                    dve.wait_ge(ffn_act, 8 * i + (4 * s + 3))
                    dve.tensor_tensor(FX[:, 6 + s, :], FX[:, 4 + s, :], FX[:, s, :], ALU.mult).then_inc(ffn_dve, 1)
                    dve.wait_ge(ffn_act, 8 * i + (4 * s + 4))
                    if isinstance(i, int):
                        h_, l_ = hi(s), lo(s)
                    else:
                        h_, l_ = [a[:, bass.ds(2 * i + s, 1), :].rearrange("p a b -> p (a b)") for a in (BHI, BLO)]
                    low_from_psum(l_, h_, FX[:, 6 + s, :]).then_inc(ffn_dve, 1)
            ffn(0)
            with dve.Fori(1, NF // 2) as i:
                ffn(i)

            link(dve.memset(ACC[0], 0.0))
            link(dve.memset(ACC[1], 0.0))
            residual("down", 3, x2_done, 2)
            for kt in range(KT):
                dve.wait_ge(n_hi, 24 + kt + 1)
                dve.scalar_tensor_tensor(out=mem_part[1][:, kt, :], in0=memx[:, 256 * kt:256 * kt + 256],
                                         scalar=col("g_mem", kt), in1=mem_part[0][:, kt, :].bitcast(F),
                                         op0=ALU.mult, op1=ALU.subtract).then_inc(n_lo, 1)
            dve.wait_ge(n_tot, 3)
            def both(first, second, sum1, sum2):
                link(mean_inverse(first, sum1))
                link(dve.tensor_tensor(second, sum2, first[:, 0:second.shape[1]], ALU.mult))
                link(mean_inverse(second, second))
                return dve.tensor_tensor(second, second, first[:, 0:second.shape[1]], ALU.mult)
            both(RT[:, 0:R_TWO], RT[:, R_TWO:10], PS[:, 5, 0:R_TWO], PS[:, 5, R_TWO:10]).then_inc(n_rin, 1)
            both(RSTD, YT, PS[:, 7, :], PS[:, 6, :]).then_inc(n_rin, 1)

            def head_norm(k):
                h = HEADS[k]
                nt, n = h["nt"], h["n"]
                tok = TOK[:, 0:nt * n].rearrange("p (t n) -> p t n", t=nt)
                sq, ra, rb = scratch(k)
                dve.wait_ge(h_sq, k + 1)
                at = 0
                groups = []
                for o, g, w, gain in h["parts"]:
                    ss = SS[:, at:at + nt * g]
                    if g == 1:
                        src = sq[:, 0:nt * n].rearrange("p (t n) -> p t n", t=nt)[:, :, o:o + w]
                    else:
                        src = sq[:, 0:nt * n].rearrange("p (t n) -> p t n", t=nt)[:, :, o:o + g * w] \
                            .rearrange("p t (g w) -> p t g w", g=g)
                        ss = ss.rearrange("p (t g) -> p t g", t=nt)
                    link(dve.tensor_reduce(ss, src, AX.X, ALU.add))
                    flat = SS[:, at:at + nt * g]
                    link(dve.tensor_scalar(flat, flat, 1.0 / w, EPS, ALU.mult, ALU.add))
                    groups.append((at, o, g, w, gain))
                    at += nt * g
                dve.reciprocal(SS[:, 0:at], SS[:, 0:at]).then_inc(h_rin, 1)
                if k == 1:
                    link(dve.tensor_copy(KR[:, :, :], tok[:, :, 384:416]))
                dve.wait_ge(h_rs, k + 1)
                for a0, o, g, w, gain in groups:
                    for tk in range(nt):
                        v = tok[:, tk, o:o + g * w].rearrange("p (g w) -> p g w", g=g)
                        r = SS[:, a0 + tk * g:a0 + (tk + 1) * g]
                        ins = dve.tensor_tensor(v, v, r[:, :, None].broadcast_to([P, g, w]), ALU.mult)
                    link(ins)
                    if gain:
                        for tk in range(nt):
                            v = tok[:, tk, o:o + g * w].rearrange("p (g w) -> p g w", g=g)
                            ins = dve.tensor_tensor(v, v, row(gain, w)[:, None, :].broadcast_to([P, g, w]), ALU.mult)
                        link(ins)
                if h["rope"] is not None:
                    o, g, w, f = h["rope"]
                    for tk in range(nt):
                        v = tok[:, tk, o:o + g * w].rearrange("p (g w) -> p g w", g=g)[:, :, f:f + 32]
                        a = ra[:, tk * g * 32:(tk + 1) * g * 32].rearrange("p (g w) -> p g w", g=g)
                        b = rb[:, tk * g * 32:(tk + 1) * g * 32].rearrange("p (g w) -> p g w", g=g)
                        dve.tensor_tensor(a, v, COS[:, tk, None, :].broadcast_to([P, g, 32]), ALU.mult)
                        for x, y in ((0, 16), (16, 0)):
                            ins = dve.tensor_tensor(b[:, :, x:x + 16], v[:, :, y:y + 16],
                                                    SIN[:, tk, None, x:x + 16].broadcast_to([P, g, 16]), ALU.mult)
                    link(ins)
                    for tk in range(nt):
                        v = tok[:, tk, o:o + g * w].rearrange("p (g w) -> p g w", g=g)[:, :, f:f + 32]
                        a = ra[:, tk * g * 32:(tk + 1) * g * 32].rearrange("p (g w) -> p g w", g=g)
                        b = rb[:, tk * g * 32:(tk + 1) * g * 32].rearrange("p (g w) -> p g w", g=g)
                        ins = dve.tensor_tensor(v, a, b, ALU.add)
                    link(ins)
                if "v" in h:
                    o, w, tile = h["v"]
                    dve.wait_ge(h_v, {0: 1, 3: 2}[k])
                    v = [cat(w_, tile, nt * w // SEQ).rearrange("p (t n) -> p t n", t=nt) for w_ in (0, 1)]
                    link(dve.tensor_tensor(v[1], tok[:, :, o:o + w], v[0].bitcast(F), ALU.subtract))
                link(dve.memset(SS[:, at:at + 1], 1.0) if at < 64 else dve.memset(LAM[:, 3:4], 1.0))
                dve.nop().then_inc(h_nrm, 1)

            def head_lo(k):
                h = HEADS[k]
                dve.wait_ge(h_hi, k + 1)
                for j, tile in enumerate(h["tiles"]):
                    w = h["turn"][0][1]
                    if h.get("memk"):
                        ins = low_from_psum(lo(tile), hi(tile), PS[:, 4, :])
                    elif "gain" in h:
                        ins = dve.scalar_tensor_tensor(out=lo(tile), in0=PS[:, 4 + j, :], scalar=col(*h["gain"][j]),
                                                       in1=hi(tile).bitcast(F), op0=ALU.mult, op1=ALU.subtract)
                    else:
                        ins = low_from_psum(lo(tile)[0:w, :], hi(tile)[0:w, :], PS[0:w, 4 + j, :])
                ins.then_inc(h_lo, 1)

            head_norm(0)
            for k in range(1, 4):
                head_lo(k - 1)
                head_norm(k)
            for c in range(8):
                dve.wait_ge(n_rstd, 4)
                dve.wait_ge(unit_used, UNIT["z"] + c + 1)
                dve.tensor_tensor(PS[:, c % 4, :], PS[:, c % 4, :], YT, ALU.mult).then_inc(scaled, 1)
                link(dve.scalar_tensor_tensor(out=X[:, c, :], in0=X[:, c, :], scalar=col("g_final", c), in1=RSTD,
                                              op0=ALU.mult, op1=ALU.mult))
            lv = row("lam", 128).rearrange("p (a b c) -> p a b c", a=2, b=2)
            prod = YSQ[:, 0:64].rearrange("p (a c) -> p a c", a=2)
            link(dve.tensor_tensor(prod, lv[:, :, 0, :], lv[:, :, 1, :], ALU.mult))
            dve.tensor_reduce(LAM[:, 0:2], prod, AX.X, ALU.add).then_inc(lam_sum, 1)
            head_lo(3)
            dve.wait_ge(lam_exp, 1)
            link(dve.tensor_tensor(LAM[:, 0:1], LAM[:, 3:4], LAM[:, 2:3], ALU.subtract))
            link(dve.tensor_scalar(LAM[:, 0:1], LAM[:, 0:1], -LAM_INIT, None, ALU.add))
            attention("dm")
            head_norm(4)
            for k in range(5, 8):
                head_lo(k - 1)
                head_norm(k)
            vh, vl = [cat(w, LV, 4).rearrange("p (t n) -> p t n", t=NT) for w in (0, 1)]
            for tk in range(NT):
                dve.wait_ge(vm_hi, tk + 1)
                low_from_psum(vl[:, tk, :], vh[:, tk, :], PS[:, tk, :]).then_inc(vm_lo, 1)
            head_lo(7)
            attention("mla")

            residual("wout2", 1, y_out)

        @block.tensor
        def _(pe):
            def three(dst, a, b, first, last, **kw):
                pe.matmul(dst, a[0], b[0], start=first, stop=False, **kw)
                pe.matmul(dst, a[0], b[1], start=False, stop=False, **kw)
                return pe.matmul(dst, a[1], b[0], start=False, stop=last, **kw)

            def arrive(c, n=0, i=0):
                pe.wait_ge(split_lo, (c + 1) + n * i)

            def weight(c, sub, width=P, pitch=P):
                a = sub * pitch
                return WHI[:, c % 2, a:a + width], WLO[:, c % 2, a:a + width]

            def unit_T(c, bank, acts, n=0, i=0, subs=range(8), first=True, last=True, norm=None):
                arrive(c, n, i)
                subs = list(subs)
                for j in subs:
                    if norm is not None:
                        pe.wait_ge(n_lo, 8 * norm + j + 1)
                    ins = three(PS[:, bank, :], weight(c, j), acts(j), first and j == subs[0], last and j == subs[-1])
                return ins

            H = lambda kt: (HHI[:, kt, :], HLO[:, kt, :])

            def column_sums(dst, *srcs):
                for tk in range(dst.shape[1]):
                    for n, src in enumerate(srcs):
                        pe.matmul(dst[:, tk:tk + 1], src[:, tk * P:(tk + 1) * P], ONE[:, 0:1], start=n == 0,
                                  stop=n == len(srcs) - 1)

            pe.wait_ge(consts, 4)
            u = UNIT["proj"]
            for c in range(2):
                unit_T(u + c, c, H, norm=0 if c == 0 else None).then_inc(unit_used, 1)
                if c == 0:
                    pe.wait_ge(n_acc, 8)
                    column_sums(PS[:, 6, 0:4], ACC[0])
                    pe.matmul(PS[:, 7, :], ONE[:, :], ACC[0], start=True, stop=True).then_inc(n_tot, 1)
                else:
                    pe.wait_ge(n_rin, 1)
                    pe.wait_ge(tbl_ready, 1)
                    pe.wait_ge(ld_oh, 16)
                    fx33 = FX[0:NBUCKET + 1, :, :].rearrange("p a b -> p (a b)")
                    for b in range(5):
                        a, e = OH * b // 5, OH * (b + 1) // 5
                        ins = pe.matmul(PS[0:16, 2 + b, 0:e - a], TBL[:, :], fx33[:, a:e], start=True, stop=True)
                    ins.then_inc(oh_mm, 1)
            with pe.Fori(1, 5) as i:
                for s in range(2):
                    pe.wait_ge(proj_out, 2 * i + (s - 1))
                    unit_T(u + s, s, H, 2, i).then_inc(unit_used, 1)
            for c in (10, 11, 12):
                pe.wait_ge(proj_out, c - 1)
                unit_T(u + c, c % 2, H).then_inc(unit_used, 1)
            def unit_tok(c, n, toks, acts, banks, first, last, kts=2, pitch=None, inc=True):
                arrive(c)
                for tk in toks:
                    for j in range(kts):
                        a = acts(c, j)
                        a = (a[0][:, tk * P:(tk + 1) * P], a[1][:, tk * P:(tk + 1) * P])
                        ins = three(PS[:, banks + tk, 0:n], a, weight(c, j, n, pitch or n), first and j == 0, last and j == kts - 1)
                if inc:
                    ins.then_inc(unit_used, 1)
                return ins

            u = UNIT["vtok"]
            pe.wait_ge(oh_ev, 1)
            for c in range(4):
                unit_tok(u + c, 408, range(4), lambda c_, j, c=c: H(2 * c + j), 2, c == 0, c == 3)
            u = UNIT["cmp"]
            pe.wait_ge(v_lo, 4)
            pe.wait_ge(v_hi, 5)
            for w in range(2):
                pe.wait_ge(cb_lo, w + 1)
                cbs = [cat(x, 14 + 4 * w, 4) for x in (0, 1)]
                for c in range(4):
                    arrive(u + 4 * w + c)
                    for j in range(4):
                        tp = 4 * c + j
                        ins = three(PS[:, 6 + w, 0:256], [b[:, tp * P:(tp + 1) * P] for b in cbs],
                                    weight(u + 4 * w + c, j, 256, 256), tp == 0, tp == 15)
                    ins.then_inc(unit_used, 1)
            pe.wait_ge(gelu_done, 2)
            pe.wait_ge(proj_out, 13)
            for j in range(4):
                ins = pe.transpose(PS[:, 0, j * P:(j + 1) * P], FX[:, 6, j * P:(j + 1) * P], IDN[:, :])
            ins.then_inc(gelu_t, 1)
            pe.wait_ge(gelu_copied, 1)
            pe.wait_ge(ld_w2, 16)
            gt = FX[:, 7, :].rearrange("p (w h n) -> p w h n", w=2, h=2)
            for c in range(2):
                pe.matmul(PS[:, 1, 0:P], W2[:, 0, c, :], gt[:, 0, c, :], start=c == 0, stop=c == 1)
            for g in range(2):
                for c in range(2):
                    ins = pe.matmul(PS[0:32, 2, 64 * g:64 * g + 64], gt[:, 1, c, 64 * g:64 * g + 32], W2[:, 1, c, 0:64],
                                    start=c == 0, stop=c == 1)
            ins.then_inc(cmp_mm, 1)
            pe.wait_ge(cmp_lo, 1)

            def scores(A, m):
                for g, qs in enumerate(m["groups"]):
                    if m["s_free"][g]:
                        name, value = m["s_free"][g]
                        pe.wait_ge(A[name], value)
                    for q in qs:
                        a = [x[:, q % 4 * P:(q % 4 + 1) * P] for x in m["q"]]
                        (b, o), (k0, nk) = m["place"][q], m["spans"][q]
                        keys = m["kc"] if q >= 4 else [x[:, k0:k0 + nk] for x in m["k"]]
                        ins = three(PS[:, b, o:o + nk], a, keys, True, True)
                    ins.then_inc(A["scores"], 1)

            def turn(A, m):
                pr = prob(m)
                for g, qs in enumerate(m["groups"]):
                    pe.wait_ge(A["normed"], m["t0"] + g + 1)
                    if m["t_free"][g]:
                        pe.wait_ge(A["p_lo"], m["t_free"][g])
                    for q in qs:
                        if q >= 4:
                            if q == 4:
                                ins = pe.transpose(PS[:, 5, 256:384], prob_cmp(m), IDN[:, :])
                            continue
                        (b, o), (k0, nk) = m["place"][q], m["spans"][q]
                        for j in range(nk // P):
                            p0 = m["p"][q] + j * P
                            ins = pe.transpose(PS[:, 3 + b, o + j * P:o + (j + 1) * P], pr[:, p0:p0 + P], IDN[:, :])
                    ins.then_inc(A["turned"], 1)

            def values(name, A, m, pts):
                pe.wait_ge(A["p_lo"], m["t1"])
                y = m["y"]
                if m["first"] and y >= 2:
                    if name == "ab":
                        pe.wait_ge(A["y_lo"], y - 1)
                    elif name == "mla":
                        pe.wait_ge(A["y_f"], y - 1)
                    elif y >= 6:
                        pe.wait_ge(A["y_f"], y - 5)
                    elif y % 2:
                        pe.wait_ge(dm_rin, y - 1 if y == 3 else 4)
                    else:
                        pe.wait_ge(A["y_hi"], y - 1)
                pt = pts[m["n"] % 2]
                for kb in range(m["nkb"]):
                    q0, q1 = m["kb"](kb)
                    ins = three(PS[:, m["bank"], q0:q1], [m["v"][w](kb) for w in (0, 1)],
                                [part(w, pt + kb)[:, q0:q1] for w in (0, 1)],
                                m["first"] and kb == 0, m["last"] and kb == m["nkb"] - 1, skip_group_check=True)
                for q in range(NT if "cmp" in m else 0):
                    ins = pe.matmul(PS[:, m["bank"], q * P:(q + 1) * P], v_cmp(q), turned_cmp(m),
                                    start=False, stop=False, skip_group_check=True)
                ins.then_inc(A["pv"], 1)

            def attention(name):
                maps, pts = GROUP[name]
                A = ATT[name]
                for i in range(-2, len(maps) + 2):
                    if 0 <= i + 2 < len(maps):
                        scores(A, maps[i + 2])
                    if 0 <= i < len(maps) and maps[i].get("mode") != "hold":
                        turn(A, maps[i])
                    if 0 <= i - 1 < len(maps) and maps[i - 1].get("mode") != "hold":
                        values(name, A, maps[i - 1], pts)
                    if 0 <= i - 2 < len(maps) and maps[i - 2].get("diff") and maps[i - 2]["last"] and maps[i - 2]["bank"] == 7:
                        m = maps[i - 2]
                        pe.wait_ge(dm_sq, m["y"] // 2 + 1)
                        pe.matmul(PS[:, 7, :], BONE[:, :], YSQ, start=True, stop=True, skip_group_check=True).then_inc(dm_tot, 1)

            attention("ab")

            u = UNIT["merge"]
            def merge(i):
                for s in range(2):
                    if not isinstance(i, int):
                        pe.wait_ge(merge_dve, 8 * i + (4 * s - 8 + 2))
                    for e in range(2):
                        unit_T(u + 3 * s + e, 4 * s + e, H, 6, i).then_inc(unit_used, 1)
                    c = u + 3 * s + 2
                    ya = lambda j: (hi(j), lo(j))
                    unit_T(c, 4 * s + 2, ya, 6, i, range(0, 4))
                    unit_T(c, 4 * s + 3, ya, 6, i, range(4, 8)).then_inc(unit_used, 1)
            pe.wait_ge(ATT["ab"]["y_lo"], 16)
            merge(0)
            with pe.Fori(1, 4) as i:
                merge(i)

            def dense(name, acts, done, ready):
                c0 = UNIT[name]
                ready()
                for s in range(2):
                    unit_T(c0 + s, s, acts).then_inc(unit_used, 1)
                with pe.Fori(1, 4) as i:
                    for s in range(2):
                        pe.wait_ge(done, 2 * i + (s - 1))
                        unit_T(c0 + s, s, acts, 2, i).then_inc(unit_used, 1)

            dense("wout", lambda j: (hi(14 + j), lo(14 + j)), x1_done, lambda: pe.wait_ge(merge_dve, 32))

            u = UNIT["ffn"]
            def ffn(i):
                for s in range(2):
                    if not isinstance(i, int):
                        pe.wait_ge(ffn_dve, 12 * i + (6 * s - 12 + 4))
                    for e in range(2):
                        first = isinstance(i, int) and s == 0 and e == 0
                        unit_T(u + 2 * s + e, 2 * e + s, H, 4, i, norm=1 if first else None).then_inc(unit_used, 1)
                        if first:
                            pe.wait_ge(n_acc, 16)
                            pe.matmul(PS[:, 7, :], ONE[:, :], ACC[0], start=True, stop=True).then_inc(n_tot, 1)
            pe.wait_ge(x1_done, 7)
            ffn(0)
            with pe.Fori(1, NF // 2) as i:
                ffn(i)

            u = UNIT["down"]
            def down(i):
                for s in range(2):
                    if not isinstance(i, int):
                        pe.wait_ge(x2_done, 2 * i + (s - 1))
                    for e in range(3):
                        unit_T(u + 3 * s + e, s, lambda j, e=e: (hi(8 * e + j), lo(8 * e + j)), 6, i,
                               range(min(8, NF - 8 * e)), e == 0, e == 2).then_inc(unit_used, 1)
            pe.wait_ge(ffn_dve, 6 * NF)
            down(0)
            with pe.Fori(1, 4) as i:
                down(i)
            pe.wait_ge(mem_sq, 1)
            mem_squares = FX[:, 4:8, :].rearrange("p a b -> p (a b)")
            column_sums(PS[:, 5, R_MEM:R_TWO], *[mem_squares[:, 256 * kt:256 * kt + 256] for kt in range(KT)])
            pe.wait_ge(n_acc, 32)
            column_sums(PS[:, 5, 0:4], ACC[0])
            column_sums(PS[:, 5, R_TWO:10], ACC[1])
            pe.matmul(PS[:, 7, :], ONE[:, :], ACC[0], start=True, stop=True)
            pe.matmul(PS[:, 6, :], ONE[:, :], ACC[1], start=True, stop=True).then_inc(n_tot, 1)

            def head_turn(k):
                h = HEADS[k]
                pe.wait_ge(h_nrm, k + 1)
                if k:
                    pe.wait_ge(h_lo, k)
                for tk in range(h["nt"]):
                    for j, (o, w) in enumerate(h["turn"]):
                        dst = PS[0:w, 4, (2 * j + tk) * P:(2 * j + tk + 1) * P] if h.get("memk") \
                            else PS[0:w, 4 + j, tk * P:(tk + 1) * P]
                        ins = pe.transpose(dst, TOK[:, tk * h["n"] + o:tk * h["n"] + o + w], IDN[:, :])
                ins.then_inc(h_tr, 1)

            pe.wait_ge(n_lo, 32)
            u = UNIT["mem"]
            for c in range(4):
                unit_tok(u + c, 512, range(2), lambda c_, j, c=c: (mem_part[0][:, 2 * c + j, :], mem_part[1][:, 2 * c + j, :]),
                         0, c == 0, c == 3)
            for k in range(1, 4):
                u = UNIT["tok2"] + 4 * (k - 1)
                n = HEADS[k]["n"]
                pe.wait_ge(h_tok, k)
                for c in range(4):
                    unit_tok(u + c, n, range(4), lambda c_, j, c=c: H(2 * c + j), 0, c == 0, c == 3)
                head_turn(k - 1)
            u = UNIT["z"]
            pe.wait_ge(h_tok, 4)
            for c in range(8):
                if c >= 4:
                    pe.wait_ge(z_done, c - 3)
                unit_T(u + c, c % 4, H).then_inc(unit_used, 1)
            head_turn(3)
            pe.wait_ge(z_done, 8)
            pe.wait_ge(h_lo, 4)
            attention("dm")

            cq = lambda c_, j: (hi(CQ + j), lo(CQ + j))
            pe.wait_ge(ATT["dm"]["y_lo"], 6)
            for k in (4, 5):
                if k == 5:
                    pe.wait_ge(h_tok, 5)
                unit_tok(UNIT["uq"] + k - 4, 384, range(4), cq, 0, True, True)
                if k == 5:
                    head_turn(4)
            c = UNIT["ukv"]
            arrive(c)
            for k in (6, 7, 8):
                pe.wait_ge(h_tok, k)
                for tk in range(NT):
                    a = (hi(CKV)[:, tk * P:(tk + 1) * P], lo(CKV)[:, tk * P:(tk + 1) * P])
                    n, o = (512, 512) if k == 8 else (256, 256 * (k - 6))
                    b = (WHI[:, c % 2, o:o + n], WLO[:, c % 2, o:o + n])
                    ins = three(PS[:, tk, 0:n], a, b, True, True)
                ins.then_inc(unit_used if k == 8 else k_mm, 1)
                head_turn(k - 1)
            pe.wait_ge(vm_lo, 4)
            pe.wait_ge(h_lo, 8)
            attention("mla")

            yo = lambda j: (hi(LQ + j), lo(LQ + j)) if j < 4 else (hi(Y_DM + j - 4), lo(Y_DM + j - 4))
            dense("wout2", yo, y_out, lambda: pe.wait_ge(ATT["mla"]["y_lo"], 8))

    return nc


def _t5_bucket(dist):
    dist = np.maximum(dist, 0)
    d = np.maximum(dist, 1).astype(np.float32)
    large = 16 + (np.log(d / np.float32(16)) / np.float32(math.log(8.0)) * np.float32(16)).astype(np.int32)
    return np.where(dist < 16, dist, np.minimum(large, NBUCKET - 1))


def _onehot():
    def table(dist, valid):
        m = np.zeros((NBUCKET + 1, dist.size), np.float32)
        m[np.where(valid, _t5_bucket(dist), NBUCKET), np.arange(dist.size)] = 1.0
        return m
    da = 255 - np.arange(OH_A)
    db = SEQ - 1 - np.arange(OH_B)
    b, a = np.divmod(np.arange(OH_C), CMP_A)
    dc = SEQ - (16 * a + b)
    return np.concatenate([table(da, (da >= 0) & (da < 128)), table(db, db >= 0), table(dc, dc >= 0)], axis=1)


def kernel(**inputs):
    import concourse.bacc as _bacc
    from concourse.bass_utils import run_bass_kernel_spmd as _run

    a = {k: np.asarray(v) for k, v in inputs.items()}
    f32 = np.float32

    def tiles(w):
        k, n = w.shape
        return w.reshape(k // P, P, n // P, P).transpose(2, 1, 0, 3).reshape(n // P, P, k)

    def rows2(w, n):
        return w.reshape(4, 2, P, n).transpose(0, 2, 1, 3).reshape(4, P, 2 * n)

    def pad(w):
        out = np.zeros(w.shape[:2] + (1024,), f32)
        out[:, :, :w.shape[2]] = w
        return out

    w = a["w_in"][0]
    off = np.cumsum([0, 512, 128, 128, 512, 128, 128, 128, 128, 128, 128, 24, 1024, 1024])
    qa, ka, va, qb, kc, vc, ksl, vsl, kw, vw, gn, ga, gb = [w[:, off[i]:off[i + 1]] for i in range(13)]

    def pair(m, axis):
        shape = m.shape
        if axis == 1:
            return m.reshape(shape[0], 2, 4, DH).transpose(0, 2, 1, 3).reshape(shape)
        return m.reshape(2, 4, DH, shape[1]).transpose(1, 0, 2, 3).reshape(shape)

    up = np.concatenate([tiles(pair(a["w_up_a"][0], 0)), tiles(pair(a["w_up_b"][0], 0))], axis=2)
    ga, gb = tiles(ga), tiles(gb)
    merge = np.stack([ga, gb, up], axis=1).reshape(24, P, 1024)
    wf = tiles(a["w_ffn_in"][0])
    wf = np.stack([wf[:NF], wf[NF:]], axis=1).reshape(2 * NF, P, 1024)
    down = np.zeros((8, P, 3072), f32)
    down[:, :, :D_FF] = tiles(a["w_ffn_out"][0])
    down = down.reshape(8, P, 3, 1024).transpose(0, 2, 1, 3).reshape(24, P, 1024)
    w1 = np.concatenate([a[n][0].reshape(4, 4, P, 256).transpose(0, 2, 1, 3).reshape(4, P, 1024)
                         for n in ("cmp_w1_k", "cmp_w1_v")])
    v = a["w_in_2"][0]
    uq = a["w_uq_2"][0].reshape(2, P, 2, 384).transpose(2, 1, 0, 3).reshape(2, P, 768)
    ukv = a["w_ukv_2"][0].reshape(P, NH, 2, DH).transpose(0, 2, 1, 3).reshape(1, P, 1024)
    stream = np.concatenate([
        tiles(np.concatenate([pair(qa, 1), pair(qb, 1), ka, ksl, kw, kc, vc], axis=1)),
        pad(rows2(np.concatenate([va, vsl, vw, gn], axis=1), 408)), w1, merge, tiles(a["w_out"][0]), wf, down,
        pad(rows2(a["w_mem_kv_2"][0], 512)),
        pad(rows2(v[:, 0:416], 416)), pad(rows2(v[:, 416:928], 512)), pad(rows2(v[:, 928:1440], 512)),
        tiles(v[:, 1440:2464]), pad(uq), ukv, tiles(a["w_out_2"][0])])
    assert stream.shape == (NU, P, 1024)

    fm = lambda g: g.reshape(-1, P).T
    conv = np.concatenate([a["conv_w"][0], a["conv_b"]])
    conv = conv.reshape(4, 2, NF, P).transpose(3, 2, 1, 0).reshape(P, 8 * NF)
    twice = lambda m: np.concatenate([m, m])
    cols = np.concatenate([fm(a["norm_mix"]), fm(a["norm_ffn"]), fm(a["norm_final"]), fm(a["norm_g_2"]),
                           fm(a["mem_norm_g_2"]), fm(a["mla_q_norm_g_2"]), fm(a["mla_kv_norm_g_2"]),
                           twice(a["diff_subln_g_2"][0])[:, None], twice(a["cmp_pos_k"][0].T), twice(a["cmp_pos_v"][0].T),
                           conv], axis=1)
    inv = (f32(10000.0) ** (-np.arange(0, 32, 2, dtype=f32) / f32(32))).astype(f32)
    rows = np.concatenate([a["mla_qn_g_2"][0], a["mla_kn_g_2"][0], a["diff_qn_g_2"][0], a["diff_kn_g_2"][0],
                           a["mem_qn_g_2"][0], a["mem_kn_g_2"][0], a["attn_sinks"][0], inv,
                           a["diff_lambda_2"][0].reshape(-1)])[None]
    w2k = a["cmp_w2_k"][0].reshape(2, P, DH).transpose(1, 0, 2)
    w2v = a["cmp_w2_v"][0].reshape(2, P, DH).transpose(1, 0, 2)
    w2 = np.stack([np.concatenate([m, m], axis=2) for m in (w2k, w2v)], axis=1)
    xt = a["x"][0].T.reshape(KT, P, SEQ).transpose(1, 0, 2)
    mt = a["mem_2"][0].T.reshape(KT, P, 256).transpose(1, 0, 2).reshape(P, KT * 256)
    arrays = {"wstream": stream, "xT": xt, "memT": mt, "cols": cols, "rows": rows, "w2": w2,
              "table": a["rel_bias_table"], "onehot": _onehot(), "pos": a["positions_2"][0].reshape(NT, P).T}
    arrays = {k: np.ascontiguousarray(v_) for k, v_ in arrays.items()}

    nc = _bacc.Bacc("TRN2", target_bir_lowering=False, num_devices=1)
    t = {k: nc.dram_tensor(k, v_.shape, mybir.dt.from_np(v_.dtype), kind="ExternalInput").ap() for k, v_ in arrays.items()}
    out = nc.dram_tensor("outT", (P, KT, SEQ), F, kind="ExternalOutput").ap()
    build(nc, t, out)
    r = _run(nc, [arrays], core_ids=[0])
    got = r.results[0]["outT"]
    return np.ascontiguousarray(got.transpose(1, 0, 2).reshape(D, SEQ).T)[None]
```

```python
import math

import numpy as np
import concourse.bass as bass
from concourse import mybir

F = mybir.dt.float32
R = mybir.dt.float32r
I32 = mybir.dt.int32
ALU = mybir.AluOpType
ACT = mybir.ActivationFunctionType
AX = mybir.AxisListType

P = 128
SEQ = 512
NT = SEQ // P
D = 1024
KT = D // P
DH = 64
NH = 8
NBUCKET = 32
N_CMP = (SEQ - 32) // 16 + 1
CMP_A = 66
D_FF = 2816
NF = D_FF // P
EPS = 1e-6
NEG = -1e30
LAM_INIT = 0.8 - 0.6 * math.exp(0.0)

_PLAN = [("proj", 13), ("vtok", 4), ("cmp", 8), ("merge", 24), ("wout", 8), ("ffn", 2 * NF),
         ("down", 24), ("mem", 4), ("tok2", 12), ("z", 8), ("uq", 2), ("ukv", 1), ("wout2", 8)]
UNIT = {}
NU = 0
for _n, _c in _PLAN:
    UNIT[_n] = NU
    NU += _c

OH_A, OH_B, OH_C = 384, 640, 16 * CMP_A
OH = OH_A + OH_B + OH_C

COL = {}
_at = 0
for _n, _c in [("g_mix", 8), ("g_ffn", 8), ("g_final", 8), ("g_2", 8), ("g_mem", 8), ("g_q2", 2),
               ("g_kv2", 1), ("subln", 1), ("pos_k", 32), ("pos_v", 32), ("qn_t", 1), ("kn_t", 1), ("conv", 4 * 2 * NF)]:
    COL[_n] = _at
    _at += _c
NCOL = _at
ROW = {}
_at = 0
for _n, _c in [("qn", 96), ("kn", 96), ("dqn", 32), ("dkn", 32), ("mqn", 64), ("mkn", 64),
               ("sinks", 8), ("inv", 16), ("lam", 128)]:
    ROW[_n] = _at
    _at += _c
NROW = _at


class Chain:

    def __init__(self, eng, sem):
        self.eng, self.sem, self.n = eng, sem, 0

    def link(self, ins):
        self.n += 1
        ins.then_inc(self.sem, 1)
        self.eng.wait_ge(self.sem, self.n)


def build(nc, t, out):
    from contextlib import ExitStack
    ctx = ExitStack()
    with ctx:
        def sb(name, shape, dt=F):
            return ctx.enter_context(nc.sbuf_tensor(name, shape, dt))

        def sem(name):
            return ctx.enter_context(nc.semaphore(name))

        X = sb("X", [P, KT, SEQ])
        FX = sb("FX", [P, 8, SEQ])
        HHI = sb("HHI", [P, KT, SEQ], R)
        HLO = sb("HLO", [P, KT, SEQ], R)
        BHI = sb("BHI", [P, 24, SEQ], R)
        BLO = sb("BLO", [P, 24, SEQ], R)
        RAW = sb("RAW", [P, 2, 1024])
        WHI = sb("WHI", [P, 2, 1024], R)
        WLO = sb("WLO", [P, 2, 1024], R)
        PB = sb("PB", [P, 7 * SEQ])
        TRI = sb("TRI", [P, SEQ])
        IDN = sb("IDN", [P, P])
        ONE = sb("ONE", [P, P])
        BONE = sb("BONE", [P, P])
        CL = sb("CL", [P, NCOL])
        RW = sb("RW", [P, NROW])
        GATE = sb("GATE", [P, NT, 24])
        KR = sb("KR", [P, NT, 32])
        COS = sb("COS", [P, NT, 32])
        SIN = sb("SIN", [P, NT, 32])
        POS = sb("POS", [P, NT], I32)
        ST = sb("ST", [P, 4, 40])
        SS = sb("SS", [P, 64])
        MSK = sb("MSK", [P, NT])
        LAM = sb("LAM", [P, 4])
        TBL = sb("TBL", [NBUCKET + 1, 16])
        PS = ctx.enter_context(nc.psum_tensor("PS", [P, 8, SEQ], F))
        tb_dram = nc.dram_tensor("bias_rows", [16, OH], F, kind="Internal").ap()
        bias_a = nc.dram_tensor("bias_a", [NH, P, 256], F, kind="Internal").ap()
        bias_b = nc.dram_tensor("bias_b", [NH, P, SEQ], F, kind="Internal").ap()
        bias_c = nc.dram_tensor("bias_c", [NH, P, NT, N_CMP], F, kind="Internal").ap()

        SQ = [PB[:, s * SEQ:(s + 1) * SEQ] for s in (0, 1)]
        ACC = [PB[:, 2 * SEQ:3 * SEQ], PB[:, 4 * SEQ:5 * SEQ]]
        RSTD = PB[:, 6 * SEQ:7 * SEQ]
        RT = sb("RT", [P, 10])
        R_MEM, R_TWO = 4, 6
        YT, YSQ = PB[:, 5 * SEQ:6 * SEQ], PB[:, 6 * SEQ:7 * SEQ]
        W2 = YT.rearrange("p (w h n) -> p w h n", w=2, h=2)

        def hi(tile):
            return BHI[:, tile, :] if tile < 24 else HHI[:, tile - 24, :]

        def lo(tile):
            return BLO[:, tile, :] if tile < 24 else HLO[:, tile - 24, :]

        def part(w, tile):
            return (hi, lo)[w](tile)

        def cat(w, tile, n):
            a = ((BHI, BLO) if tile < 24 else (HHI, HLO))[w]
            tile %= 24
            return a[:, tile:tile + n, :].rearrange("p a b -> p (a b)")

        def col(name, j=0):
            return CL[:, COL[name] + j:COL[name] + j + 1]

        def row(name, n):
            return RW[:, ROW[name]:ROW[name] + n]

        ld_x = [sem(f"ld_x{j}") for j in range(4)]
        ld_cols, ld_small, ld_mem, ld_bias = sem("ld_cols"), sem("ld_small"), sem("ld_mem"), [sem("ld_bias0"), sem("ld_bias1")]
        ld_oh, ld_cmp, st_rows, ld_w2 = sem("ld_oh"), sem("ld_cmp"), sem("st_rows"), sem("ld_w2")
        raw_loaded = [sem("raw_loaded0"), sem("raw_loaded1")]
        split_hi, split_lo, unit_used = sem("split_hi"), sem("split_lo"), sem("unit_used")
        consts, dve_step, act_step = sem("consts"), sem("dve_step"), sem("act_step")
        n_sq, n_acc, n_tot, n_rin, n_rstd, n_hi, n_lo, scaled = [sem("norm_" + s) for s in
            ("sq", "acc", "tot", "rin", "rstd", "hi", "lo", "scaled")]
        SCALED = dict(proj=0, merge=11, ffn=27, z=27 + 2 * NF)
        spread, mem_sq = sem("spread"), sem("mem_sq")
        mem_hi, mem_lo = sem("mem_hi"), sem("mem_lo")
        mla_sq = sem("mla_sq")
        oh_mm, oh_ev, tbl_ready = sem("oh_mm"), sem("oh_ev"), sem("tbl_ready")
        ang_ready = sem("ang_ready")
        sin_ready = sem("sin_ready")
        proj_hi, proj_out = sem("proj_hi"), sem("proj_out")
        v_hi, v_lo = sem("v_hi"), sem("v_lo")
        cb_built, cb_hi, cb_lo = sem("cb_built"), sem("cb_hi"), sem("cb_lo")
        gelu_done, gelu_t, gelu_copied, cmp_mm, cmp_hi, cmp_lo = [sem(s) for s in
            ("gelu_done", "gelu_t", "gelu_copied", "cmp_mm", "cmp_hi", "cmp_lo")]
        merge_act, merge_dve = sem("merge_act"), sem("merge_dve")
        x1_done, x2_done = sem("x1_done"), sem("x2_done")
        ffn_act, ffn_dve = sem("ffn_act"), sem("ffn_dve")
        h_tok, h_sq, h_v, h_rin, h_rs, h_nrm, h_tr, h_hi, h_lo = [sem("head_" + s) for s in
            ("tok", "sq", "v", "rin", "rs", "nrm", "tr", "hi", "lo")]
        z_done, lam_sum, lam_exp, vm_hi, vm_lo = [sem(s) for s in ("z_done", "lam_sum", "lam_exp", "vm_hi", "vm_lo")]
        y_out, stored = sem("y_out"), sem("stored")
        ATT = {g: {s: sem(f"{g}_{s}") for s in
                   ("scores", "biased", "exped", "normed", "turned", "p_hi", "p_lo", "pv", "y_f", "y_hi", "y_lo")}
               for g in ("ab", "dm", "mla")}
        dm_sq, dm_tot, dm_rin, dm_rstd, dm_y, dm_hi, dm_lo, k_mm = [sem(s) for s in
            ("dm_sq", "dm_tot", "dm_rin", "dm_rstd", "dm_y", "dm_hi", "dm_lo", "k_mm")]

        CAUSAL = dict(spans=[(0, 128), (0, 256), (0, 384), (0, 512)], place=[(0, 0), (2, 0), (0, 128), (1, 0)],
                      groups=[[1], [0, 2], [3]])
        WITH_CMP = dict(spans=CAUSAL["spans"] + [(0, 32)] * 4,
                        place=CAUSAL["place"] + [(2, 256 + 32 * q_) for q_ in range(4)], groups=[[1, 4, 5, 6, 7], [0, 2], [3]])
        WINDOW = dict(spans=[(0, 128), (0, 256), (128, 256), (256, 256)],
                      place=[(0, 0), (0, 128), (1, 0), (1, 256)], groups=[[0, 1], [2, 3]])
        MEMORY = dict(spans=[(0, 256)] * 4, place=[(0, 0), (0, 256), (1, 0), (1, 256)], groups=[[0, 1], [2, 3]])
        V_AT = 11
        PT_AB = (14, 18)
        KC = 0

        def causal_kb(kb):
            return kb * P, SEQ

        def window_kb(kb):
            return kb * P, min(SEQ, kb * P + 2 * P)

        def vtok(w, b):
            v = cat(w, V_AT, 3).rearrange("p (t n) -> p t n", t=NT)
            return lambda kb: v[:, kb, b * P:(b + 1) * P]

        ab = []
        heads = [(0, r, g) for r in range(4) for g in range(2)] + [(1, r, g) for r in range(4) for g in range(2)]
        for y, (blk, r, g) in enumerate(heads):
            rows = slice(g * DH, g * DH + DH)
            q = [part(w, 4 * blk + r)[rows] for w in (0, 1)]
            base = dict(q=q, y=y, rows=rows, ytile=4 * blk + r, bank=6 + y % 2, bias=y, h=4 * g + r, scale=DH ** -0.5)
            if blk == 0:
                ab.append(dict(base, kind="bias", k=[part(w, 8)[rows] for w in (0, 1)], v=[vtok(w, 0) for w in (0, 1)],
                               nkb=4, kb=window_kb, b0=[128, 0, 0, 0], sink=True, first=True, last=True, **WINDOW))
            else:
                for b, tile in ((1, 9), (2, 10)):
                    ab.append(dict(base, kind="bias", k=[part(w, tile)[rows] for w in (0, 1)],
                                   v=[vtok(w, b) for w in (0, 1)], nkb=4, kb=causal_kb,
                                   b0=[384 - 128 * q_ for q_ in range(4)], gate=12 * g + 3 * r + b,
                                   first=b == 1, last=b == 2, **(WITH_CMP if b == 1 else CAUSAL)))
                ab[-2].update(cmp=12 * g + 3 * r, kc=[part(w, 22)[rows, KC:KC + 32] for w in (0, 1)])
        DQ, DK, DV, MQ, MK, MV, Y_DM, PT_DM, CQ, CKV = 0, 2, 4, 6, 8, 9, 12, (16, 24), 20, 22
        LQ, LK, LV, PT_L = 0, 24, 16, (8, 20)
        dm = []
        for h in range(4):
            for m in range(2):
                f = 64 * (h % 2) + 32 * m
                rows = slice(f, f + 32)
                dv = [cat(w, DV, 2).rearrange("p (t n) -> p t n", t=NT) for w in (0, 1)]
                dm.append(dict(kind="bias", q=[part(w, DQ + h // 2)[rows] for w in (0, 1)],
                               k=[part(w, DK + h // 2)[rows] for w in (0, 1)],
                               v=[(lambda kb, w=w, h=h, dv=dv: dv[w][:, kb, (h // 2) * P:(h // 2 + 1) * P]) for w in (0, 1)],
                               nkb=4, kb=causal_kb, b0=[384 - 128 * q_ for q_ in range(4)], scale=32 ** -0.5,
                               y=h, rows=slice(64 * (h % 2), 64 * (h % 2) + 64), ytile=Y_DM + h // 2, ztile=4 + h // 2,
                               bank=6 + h % 2, first=m == 1, last=m == 1, mode=("hold", "sub")[m], diff=True, **CAUSAL))
        for h in range(4):
            rows = slice(64 * (h % 2), 64 * (h % 2) + 64)
            mk = [cat(w, MK, 1).rearrange("p (t n) -> p t n", t=2) for w in (0, 1)]
            mv = [cat(w, MV, 1).rearrange("p (t n) -> p t n", t=2) for w in (0, 1)]
            dm.append(dict(kind="mem", q=[part(w, MQ + h // 2)[rows] for w in (0, 1)],
                           k=[mk[w][rows, h // 2, :] for w in (0, 1)],
                           v=[(lambda kb, w=w, h=h, mv=mv: mv[w][:, kb, (h // 2) * P:(h // 2 + 1) * P]) for w in (0, 1)],
                           nkb=2, kb=lambda kb: (0, SEQ), scale=64 ** -0.5, y=4 + h, rows=rows,
                           ytile=Y_DM + 2 + h // 2, ztile=6 + h // 2, bank=6 + h % 2, first=True, last=True, **MEMORY))
        mla = []
        for h in range(NH):
            lv = [cat(w, LV, 4).rearrange("p (t n) -> p t n", t=NT) for w in (0, 1)]
            mla.append(dict(kind="bias", q=[part(w, LQ + h)[0:96] for w in (0, 1)],
                            k=[part(w, LK + h)[0:96] for w in (0, 1)],
                            v=[(lambda kb, w=w, h=h, lv=lv: lv[w][:, kb, (h // 2) * P:(h // 2 + 1) * P]) for w in (0, 1)],
                            nkb=4, kb=causal_kb, b0=[384 - 128 * q_ for q_ in range(4)], scale=96 ** -0.5,
                            y=h, rows=slice(64 * (h % 2), 64 * (h % 2) + 64), ytile=LQ + h // 2, ztile=h // 2,
                            bank=6 + h % 2, first=True, last=True, **CAUSAL))
        for maps in (ab, dm, mla):
            n = ng = nt = 0
            s_bank, t_bank = {}, {}
            for i, m in enumerate(maps):
                m["g0"], m["t0"] = ng, nt
                m["s_free"], m["t_free"] = [], []
                for g, qs in enumerate(m["groups"]):
                    b = m["place"][qs[0]][0]
                    m["s_free"].append(s_bank.get(b))
                    ng += 1
                    s_bank[b] = ("exped", i + 1) if m["kind"] == "mem" else ("biased", ng)
                    if m.get("mode") != "hold":
                        m["t_free"].append(t_bank.get(b))
                        nt += 1
                        t_bank[b] = nt
                m["g1"], m["t1"] = ng, nt
                m["i"], m["prev"] = i, maps[i - 1]
                m["prev2"] = maps[i - 2]["t1"] if i >= 2 else 0
                if m.get("mode") != "hold":
                    n += 1
                m["n"] = n
                if maps is mla or m["kind"] == "mem":
                    m["yf"] = m["y"] - 3 if maps is dm else m["y"] + 1
                at, m["p"] = 0, []
                for k0, nk in m["spans"]:
                    m["p"].append(at)
                    at += nk
        GROUP = {"ab": (ab, PT_AB), "dm": (dm, PT_DM), "mla": (mla, PT_L)}

        def diff_tile(maps, i):
            if 0 <= i < len(maps) and maps[i].get("diff") and maps[i]["last"] and maps[i]["bank"] == 7:
                return maps[i]["y"] // 2
            return None

        DIFF_BANK = (7, 5)

        def prob(m):
            return PB[:, (m["i"] % 2) * 1280:(m["i"] % 2 + 1) * 1280]

        def prob_of(m, q):
            if q >= 4:
                return YT[:, (m["i"] % 2) * P + 32 * (q - 4):(m["i"] % 2) * P + 32 * (q - 3)]
            return prob(m)[:, m["p"][q]:m["p"][q] + m["spans"][q][1]]

        def prob_cmp(m):
            return YT[:, (m["i"] % 2) * P:(m["i"] % 2 + 1) * P]

        def turned_cmp(m):
            return FX[:, 1, (m["i"] % 2) * P:(m["i"] % 2 + 1) * P]

        def v_cmp(q):
            return FX[:, 0, q * P:(q + 1) * P]

        def bias_of(m, q):
            if q >= 4:
                return BCMP[:, m["h"], q - 4, :]
            return bias_row(m)[:, m["b0"][q]:m["b0"][q] + m["spans"][q][1]]

        def bias_row(m):
            if "bias" in m:
                return FX[:, 2 + m["bias"] % 2, :]
            return TRI[:, :]

        BCMP = FX[:, 4:6, :].rearrange("p a b -> p (a b)").rearrange("p (h q c) -> p h q c", h=NH, q=NT)

        def stat(m, k):
            return ST[:, m["i"] % 4, 8 * k:8 * k + (8 if "cmp" in m else 4)]

        MAX, NMAX, SUM, SINK, WT = range(5)

        TOK = PB[:, 0:2048]
        HEADS = [
            dict(nt=2, n=512, parts=[(0, 4, 64, "mkn")], rope=None, turn=[(0, 128), (128, 128)], tiles=[MK], memk=True, rt=R_MEM, v=(256, 256, MV)),
            dict(nt=4, n=416, parts=[(0, 1, 256, None), (256, 1, 128, None)], rope=None,
                 turn=[(0, 128), (128, 128), (256, 128)], tiles=[CQ, CQ + 1, CKV], rt=R_TWO, gain=[("g_q2", 0), ("g_q2", 1), ("g_kv2", 0)]),
            dict(nt=4, n=512, parts=[(0, 8, 32, "dqn"), (256, 8, 32, "dkn")], rope=(0, 16, 32, 0),
                 turn=[(128 * j, 128) for j in range(4)], tiles=[DQ, DQ + 1, DK, DK + 1], rt=R_TWO),
            dict(nt=4, n=512, parts=[(256, 4, 64, "mqn")], rope=None, turn=[(256, 128), (384, 128)], tiles=[MQ, MQ + 1],
                 rt=R_TWO, v=(0, 256, DV)),
        ] + [dict(nt=4, n=384, parts=[(0, 4, 96, g)], rope=(0, 4, 96, 64), turn=[(96 * j, 96) for j in range(4)],
                  tiles=[base + j for j in range(4)], kpart=kp, gain_t=g + "_t")
             for g, base, kp in (("qn", LQ, False), ("qn", LQ + 4, False), ("kn", LK, True), ("kn", LK + 4, True))]

        def tiles_before(k):
            return sum(h["nt"] for h in HEADS[:k])

        HEAD_AT = {tiles_before(k): k for k in range(8)}

        def scratch(k):
            fx = FX[:, :, :].rearrange("p a b -> p (a b)")
            return fx[:, 0:2048], fx[:, 0:2048], fx[:, 2048:4096]

        MLA_SQ = PB[:, 1536:3072].rearrange("p (t h e) -> p t h e", t=NT, h=4)
        MLA_ROT = PB[:, 3072:3584].rearrange("p (x t h e) -> p x t h e", x=2, t=2, h=4)

        def turned_aps(m, pt, q, w):
            if q >= 4:
                return turned_cmp(m), PS[:, 5, 256:384]
            (b, o), (k0, nk) = m["place"][q], m["spans"][q]
            arena = ((BHI, BLO) if pt < 24 else (HHI, HLO))[w]
            t0, n = pt % 24 + k0 // P, nk // P
            return arena[:, t0:t0 + n, q * P:(q + 1) * P], PS[:, 3 + b, o:o + nk].rearrange("p (n c) -> p n c", n=n)

        def tile_at(buf, i, s):
            return buf[:, 2 * i + s, :] if isinstance(i, int) else \
                buf[:, bass.ds(2 * i + s, 1), :].rearrange("p a b -> p (a b)")

        def gain_at(name, i, s):
            return col(name, 2 * i + s) if isinstance(i, int) else CL[:, bass.ds(2 * i + (s + COL[name]), 1)]

        NORM_GAIN = ["g_mix", "g_ffn", "g_2"]
        memx = FX[:, 0:4, :].rearrange("p a b -> p (a b)")
        mem_part = [cat(w, 0, 4).rearrange("p (k n) -> p k n", k=KT) for w in (0, 1)]

        block = ctx.enter_context(nc.Block())

        @block.sync
        def _(sp):
            for s in range(2):
                sp.dma_start(RAW[:, s, :], t["wstream"][s]).then_inc(raw_loaded[s], 16)

            def load(i, s):
                sp.wait_ge(split_lo, 2 * i + (s - 1))
                sp.dma_start(RAW[:, s, :], t["wstream"][2 * i + s]).then_inc(raw_loaded[s], 16)

            with sp.Fori(1, 4) as i:
                for s in range(2):
                    load(i, s)
            sp.wait_ge(st_rows, 16)
            for dst, h0, off, n in ((bias_a, 0, 0, 256), (bias_b, 8, OH_A, SEQ)):
                src = bass.AP(tb_dram.tensor, h0 * OH + off + P - 1, [[OH, NH], [-1, P], [1, n]])
                sp.dma_start(dst, src).then_inc(spread, 16)
            for qt in range(NT):
                for s in range(2):
                    load(4 + qt, s)
                    for pg in range(4 * s, 4 * s + 4):
                        src = bass.AP(tb_dram.tensor, 8 * OH + OH_A + OH_B + 15 * CMP_A + 33 - 8 * qt - pg,
                                      [[OH, NH], [-CMP_A, 16], [1, N_CMP]])
                        sp.dma_start(bias_c[:, 16 * pg:16 * pg + 16, qt, :], src).then_inc(spread, 16)
            for i in (8, 9):
                for s in range(2):
                    load(i, s)
            sp.wait_ge(spread, 16 * 34)
            sp.wait_ge(tbl_ready, 2)
            for h in range(NH):
                dst = FX[:, 4 + h // 4, (h % 4) * P:(h % 4 + 1) * P].rearrange("p (q c) -> p q c", q=NT)[:, :, 0:N_CMP]
                sp.dma_start(dst, bias_c[h]).then_inc(ld_cmp, 16)
            with sp.Fori(10, NU // 2) as i:
                for s in range(2):
                    load(i, s)

        @block.gpsimd
        def _(pool):
            pool.memset(IDN[:, :], 0.0)
            pool.memset(TRI[:, :], 0.0)
            pool.memset(BONE[:, :], 0.0)
            pool.memset(ONE[:, :], 1.0).then_inc(consts, 1)
            pool.wait_ge(consts, 1)
            pool.affine_select(out=IDN[:, :], in_=IDN[:, :], compare_op=ALU.not_equal, fill=1.0, base=0,
                               pattern=[[-1, P]], channel_multiplier=1)
            pool.affine_select(out=TRI[:, :], in_=TRI[:, :], compare_op=ALU.is_ge, fill=NEG, base=SEQ - P,
                               pattern=[[-1, SEQ]], channel_multiplier=1).then_inc(consts, 1)
            pool.wait_ge(consts, 2)
            pool.memset(BONE[0:64, 0:64], 1.0).then_inc(consts, 1)
            pool.wait_ge(consts, 3)
            pool.memset(BONE[64:128, 64:128], 1.0).then_inc(consts, 1)
            pool.wait_ge(consts, 4)
            with pool.Fori(0, NU // 2) as i:
                for s in range(2):
                    pool.wait_ge(split_hi, 2 * i + (s + 1))
                    pool.tensor_tensor(WLO[:, s, :], RAW[:, s, :], WHI[:, s, :].bitcast(F), ALU.subtract).then_inc(split_lo, 1)

        @block.scalar
        def _(act):
            chain = Chain(act, act_step)

            def stream(c, n=0, i=0):
                if isinstance(c, int) and n == 0 and c >= NU:
                    return
                act.wait_ge(raw_loaded[c % 2], 16 * (c // 2 + 1) + 8 * n * i)
                if c >= 2 or n:
                    act.wait_ge(unit_used, (c - 1) + n * i)
                act.activation(WHI[:, c % 2, :], RAW[:, c % 2, :], ACT.Copy).then_inc(split_hi, 1)

            def used(c, n=0, i=0):
                act.wait_ge(unit_used, (c + 1) + n * i)

            def norm_tile(k, i, s, done=None):
                per = 2 if k == 2 else 1
                n = 8 * k + per * s
                if not isinstance(i, int) or 2 * per * i + n >= 2:
                    act.wait_ge(n_acc, 2 * per * i + (n + per - 2))
                if done is not None:
                    act.wait_ge(done, 2 * i + (s + 1))
                x = tile_at(X, i, s)
                act.activation(tile_at(HHI, i, s), x, ACT.Copy, scale=gain_at(NORM_GAIN[k], i, s)).then_inc(n_hi, 1)
                for m in range(per):
                    act.activation(SQ[(n + m) % 2], x, ACT.Square, scale=gain_at("g_final", i, s) if m else 1.0).then_inc(n_sq, 1)

            def norm_root(n, *bufs):
                act.wait_ge(n_rin, n)
                for b in bufs:
                    ins = act.activation(b, b, ACT.Sqrt)
                ins.then_inc(n_rstd, 1)

            act.dma_start(CL[:, :], t["cols"]).then_inc(ld_cols, 16)
            for j in range(4):
                act.dma_start(X[:, 2 * j:2 * j + 2, :], t["xT"][:, 2 * j:2 * j + 2, :]).then_inc(ld_x[j], 16)
            act.dma_start(RW[:, :], bass.AP(t["rows"].tensor, 0, [[0, P], [1, NROW]])).then_inc(ld_small, 16)
            act.dma_start(TBL[0:NBUCKET, :], t["table"]).then_inc(ld_small, 16)
            act.dma_start(POS[:, :], t["pos"]).then_inc(ld_small, 16)
            act.dma_start(FX[0:NBUCKET + 1, :, :].rearrange("p a b -> p (a b)")[:, 0:OH], t["onehot"]).then_inc(ld_oh, 16)
            stream(0)
            act.wait_ge(ld_cols, 16)
            for i in range(4):
                act.wait_ge(ld_x[i], 16)
                for s in range(2):
                    norm_tile(0, i, s)
                if i == 0:
                    stream(1)
            stream(2)
            norm_root(1, RSTD, RT[:, 0:4])

            u = UNIT["proj"]

            def proj_epilogue(c, n, i, tile):
                if n or c:
                    stream(c + 2, n, i)
                act.wait_ge(scaled, (c + 1) + n * i)
                act.activation(tile, PS[:, c % 2, :], ACT.Copy).then_inc(proj_hi, 1)

            for c in range(2):
                proj_epilogue(u + c, 0, 0, hi(c))

            act.wait_ge(oh_mm, 1)
            for b in range(5):
                a, e = OH * b // 5, OH * (b + 1) // 5
                ins = act.activation(FX[0:16, :, :].rearrange("p a b -> p (a b)")[:, a:e], PS[0:16, 2 + b, 0:e - a], ACT.Copy)
            ins.then_inc(oh_ev, 1)
            act.wait_ge(oh_ev, 1)
            act.dma_start(tb_dram, FX[0:16, :, :].rearrange("p a b -> p (a b)")[:, 0:OH]).then_inc(st_rows, 16)
            act.dma_start(W2, t["w2"]).then_inc(ld_w2, 16)

            with act.Fori(1, 5) as i:
                for s in range(2):
                    proj_epilogue(u + s, 2, i, BHI[:, bass.ds(2 * i + s, 1), :].rearrange("p a b -> p (a b)"))
            proj_epilogue(u + 10, 0, 0, hi(10))
            for c in (11, 12):
                stream(u + c + 2)

            def bias_load(y):
                h = (y % 8 // 2) + 4 * (y % 2) + (8 if y >= 8 else 0)
                n, src = (256, bias_a) if y < 8 else (SEQ, bias_b)
                act.dma_start(FX[:, 2 + y % 2, 0:n], src[h % 8]).then_inc(ld_bias[y % 2], 16)

            u = UNIT["vtok"]
            act.wait_ge(n_rstd, 1)
            for c in range(4):
                if c in (1, 2):
                    act.wait_ge(cb_built, c)
                    act.activation(cat(0, 10 + 4 * c, 4), PB[:, 0:2048], ACT.Copy).then_inc(cb_hi, 1)
                if c == 3:
                    used(u + 3)
                    vh = cat(0, V_AT, 3).rearrange("p (t n) -> p t n", t=NT)
                    for tk in range(NT):
                        act.activation(vh[:, tk, :], PS[:, 2 + tk, 0:384], ACT.Copy, scale=RT[:, tk:tk + 1]).then_inc(v_hi, 1)
                    for tk in range(NT):
                        ins = act.activation(GATE[:, tk, :], PS[:, 2 + tk, 384:408], ACT.Sigmoid, scale=RT[:, tk:tk + 1])
                    ins.then_inc(v_hi, 1)
                stream(u + c + 2)

            act.wait_ge(ang_ready, 1)
            act.activation(COS[:, :, 16:32], COS[:, :, 16:32], ACT.Sin)
            act.activation(SIN[:, :, 16:32], SIN[:, :, 16:32], ACT.Sin).then_inc(sin_ready, 1)
            u = UNIT["cmp"]
            for c in range(8):
                stream(u + c + 2)
                if c == 0:
                    act.wait_ge(spread, 16 * 34)
                    bias_load(0)
                    bias_load(1)
                if c % 4 == 3:
                    used(u + c)
                    w = c // 4
                    act.activation(FX[:, 6, 256 * w:256 * w + 256], PS[:, 6 + w, 0:256], ACT.Gelu_apprx_tanh).then_inc(gelu_done, 1)

            def attention(name):
                maps, pts = GROUP[name]
                A = ATT[name]
                for i in range(-1, len(maps) + 2):
                    if name == "ab" and i == 1:
                        act.wait_ge(gelu_t, 1)
                        act.activation(FX[:, 7, :], PS[:, 5, :], ACT.Copy).then_inc(gelu_copied, 1)
                    if name == "ab" and i == 3:
                        act.wait_ge(cmp_mm, 1)
                        for g in range(2):
                            half = slice(64 * g, 64 * g + 64)
                            ins = act.activation(hi(22)[half, KC:KC + 32], PS[half, 2, 64 * g:64 * g + 32], ACT.Copy)
                        ins.then_inc(cmp_hi, 1)
                    tile = diff_tile(maps, i - 4)
                    if tile is not None:
                        act.wait_ge(dm_rin, 2 * tile + 2)
                        act.activation(YSQ, YSQ, ACT.Sqrt).then_inc(dm_rstd, 1)
                    if 0 <= i - 1 < len(maps) and maps[i - 1].get("mode") != "hold":
                        m = maps[i - 1]
                        if m["n"] > 2:
                            act.wait_ge(A["pv"], m["n"] - 2)
                        pt = pts[m["n"] % 2]
                        for g, qs in enumerate(m["groups"]):
                            act.wait_ge(A["turned"], m["t0"] + g + 1)
                            for q in [q for q in qs if q <= 4]:
                                ins = act.activation(*turned_aps(m, pt, q, 0), ACT.Copy)
                            ins.then_inc(A["p_hi"], 1)
                    if i + 1 < len(maps):
                        m = maps[i + 1]
                        for g, qs in enumerate(m["groups"]):
                            act.wait_ge(A["biased"], m["g0"] + g + 1)
                            for q in qs:
                                if m.get("sink"):
                                    act.activation(stat(m, SINK)[:, q:q + 1], row("sinks", 8)[:, m["h"]:m["h"] + 1],
                                                   ACT.Exp, bias=stat(m, NMAX)[:, q:q + 1], scale=-1.0)
                                nk = m["spans"][q][1]
                                dst = prob_of(m, q)
                                b, o = m["place"][q]
                                if m["kind"] == "mem":
                                    src, sc = PS[:, b, o:o + nk], m["scale"]
                                else:
                                    src, sc = dst, -1.0
                                ins = act.activation(dst, src, ACT.Exp, bias=stat(m, NMAX)[:, q:q + 1], scale=sc,
                                                     accum_out=stat(m, SUM)[:, q:q + 1])
                        ins.then_inc(A["exped"], 1)
                        if "bias" in m and m["last"] and m["bias"] + 1 < 16 and m["bias"] >= 1:
                            act.wait_ge(A["biased"], m["g0"])
                            bias_load(m["bias"] + 1)
                    if tile is not None:
                        act.wait_ge(dm_y, tile + 1)
                        act.activation(hi(Y_DM + tile), YT, ACT.Copy).then_inc(dm_hi, 1)
                    if 0 <= i - 2 < len(maps) and maps[i - 2]["last"]:
                        m = maps[i - 2]
                        rows, yt = m["rows"], hi(m["ytile"])
                        act.wait_ge(A["pv"], m["n"])
                        if name == "ab":
                            act.activation(yt[rows, :], PS[rows, m["bank"], :], ACT.Copy).then_inc(A["y_hi"], 1)
                        elif m.get("diff"):
                            if m["y"] == 2:
                                act.wait_ge(dm_lo, 1)
                            act.activation(YT[rows, :], PS[rows, m["bank"], :], ACT.Copy).then_inc(A["y_hi"], 1)
                            if m["bank"] == 7:
                                act.wait_ge(A["y_hi"], m["y"] + 1)
                                act.activation(YSQ, YT, ACT.Square).then_inc(dm_sq, 1)
                        else:
                            act.wait_ge(A["y_f"], m["yf"])
                            act.activation(yt[rows, :], PS[rows, m["bank"], :], ACT.Copy).then_inc(A["y_hi"], 1)

            attention("ab")

            u = UNIT["merge"]
            def merge(i):
                for s in range(2):
                    for e in range(2):
                        c = u + 3 * s + e
                        act.wait_ge(scaled, 4 * i + (SCALED["merge"] + 2 * s + e + 1))
                        if not isinstance(i, int):
                            act.wait_ge(merge_dve, 8 * i + (4 * s - 8 + 2 + 1))
                        act.activation(FX[:, 2 * e + s, :], PS[:, 4 * s + e, :], ACT.Sigmoid).then_inc(merge_act, 1)
                        stream(c + 2, 6, i)
                    c = u + 3 * s + 2
                    stream(c + 2, 6, i)
                    act.wait_ge(merge_dve, 8 * i + (4 * s + 3))
                    dst = hi(14 + s) if isinstance(i, int) else \
                        BHI[:, bass.ds(2 * i + (14 + s), 1), :].rearrange("p a b -> p (a b)")
                    act.activation(dst, FX[:, 4 + s, :], ACT.Copy).then_inc(merge_act, 1)
            merge(0)
            with act.Fori(1, 4) as i:
                merge(i)

            def memory_high():
                used(UNIT["down"] + 21)
                for kt in range(KT):
                    act.activation(mem_part[0][:, kt, :], memx[:, 256 * kt:256 * kt + 256], ACT.Copy,
                                   scale=col("g_mem", kt)).then_inc(mem_hi, 1)

            def stream_and_norm(name, per, k, done, i):
                for s in range(2):
                    for e in range(per):
                        stream(UNIT[name] + per * s + e + 2, 2 * per, i)
                        if name == "down" and isinstance(i, int) and (i, s, e) == (3, 1, 0):
                            memory_high()
                    norm_tile(k, i, s, done)

            stream_and_norm("wout", 1, 1, x1_done, 0)
            with act.Fori(1, 4) as i:
                stream_and_norm("wout", 1, 1, x1_done, i)
            norm_root(2, RSTD)

            u = UNIT["ffn"]
            def ffn(i):
                for s in range(2):
                    pair = 2 * i + s
                    for e in range(2):
                        c = u + 2 * s + e
                        stream(c + 2, 4, i)
                        act.wait_ge(scaled, 4 * i + (SCALED["ffn"] + 2 * s + e + 1))
                        if not isinstance(i, int):
                            act.wait_ge(ffn_dve, 12 * i + (6 * s - 12 + 5))
                        at = COL["conv"] + 4 * e + 8 * s
                        cv = CL[:, at:at + 4] if isinstance(i, int) else CL[:, bass.ds(16 * i + at, 4)]
                        act.activation(FX[:, 2 * e + s, :], PS[:, 2 * e + s, :], ACT.Identity,
                                       bias=cv[:, 3:4], scale=cv[:, 2:3]).then_inc(ffn_act, 1)
                    act.wait_ge(ffn_dve, 12 * i + (6 * s + 4))
                    act.activation(FX[:, 4 + s, :], FX[:, 2 + s, :], ACT.Silu).then_inc(ffn_act, 1)
                    act.wait_ge(ffn_dve, 12 * i + (6 * s + 5))
                    dst = hi(s) if isinstance(i, int) else BHI[:, bass.ds(pair, 1), :].rearrange("p a b -> p (a b)")
                    act.activation(dst, FX[:, 6 + s, :], ACT.Copy).then_inc(ffn_act, 1)
            ffn(0)
            with act.Fori(1, NF // 2) as i:
                ffn(i)

            act.wait_ge(ffn_dve, 6 * NF)
            act.dma_start(FX[:, 0:4, :].rearrange("p a b -> p (a b)"), t["memT"]).then_inc(ld_mem, 16)
            stream_and_norm("down", 3, 2, x2_done, 0)
            act.wait_ge(ld_mem, 16)
            act.activation(FX[:, 4:8, :].rearrange("p a b -> p (a b)"), memx, ACT.Square).then_inc(mem_sq, 1)
            with act.Fori(1, 3) as i:
                stream_and_norm("down", 3, 2, x2_done, i)
            stream_and_norm("down", 3, 2, x2_done, 3)

            def head_evac(k):
                h = HEADS[k]
                if k:
                    act.wait_ge(h_tr, k)
                for tk in range(h["nt"]):
                    ins = act.activation(TOK[:, tk * h["n"]:(tk + 1) * h["n"]], PS[:, tk, 0:h["n"]], ACT.Copy,
                                         scale=RT[:, h["rt"] + tk:h["rt"] + tk + 1])
                    ins.then_inc(h_tok, 1)

            def head_square(k):
                h = HEADS[k]
                act.wait_ge(h_tok, tiles_before(k + 1))
                n = h["nt"] * h["n"]
                act.activation(scratch(k)[0][:, 0:n], TOK[:, 0:n], ACT.Square).then_inc(h_sq, 1)
                if "v" in h:
                    o, w, tile = h["v"]
                    v = cat(0, tile, h["nt"] * w // SEQ).rearrange("p (t n) -> p t n", t=h["nt"])
                    src = TOK[:, 0:n].rearrange("p (t n) -> p t n", t=h["nt"])[:, :, o:o + w]
                    act.activation(v, src, ACT.Copy).then_inc(h_v, 1)

            def head_root(k):
                act.wait_ge(h_rin, k + 1)
                n = 64 if k < 4 else 16
                act.activation(SS[:, 0:n], SS[:, 0:n], ACT.Sqrt).then_inc(h_rs, 1)

            def head_hi(k):
                h = HEADS[k]
                act.wait_ge(h_tr, k + 1)
                for j, tile in enumerate(h["tiles"]):
                    w = h["turn"][0][1]
                    if h.get("memk"):
                        ins = act.activation(hi(tile), PS[:, 4, :], ACT.Copy)
                    elif "gain" in h:
                        ins = act.activation(hi(tile), PS[:, 4 + j, :], ACT.Copy, scale=col(*h["gain"][j]))
                    else:
                        ins = act.activation(hi(tile)[0:w, :], PS[0:w, 4 + j, :], ACT.Copy,
                                             scale=CL[0:w, COL[h["gain_t"]]:COL[h["gain_t"]] + 1] if "gain_t" in h else 1.0)
                ins.then_inc(h_hi, 1)

            def mla_squares(k):
                if k > 4:
                    act.wait_ge(h_rin, k)
                kpart = HEADS[k]["kpart"]
                w = 64 if kpart else 96
                for tk in range(NT):
                    if kpart:
                        act.activation(MLA_SQ[:, tk, :, 64:96], KR[:, tk, None, :].broadcast_to([P, 4, 32]), ACT.Square)
                    ins = act.activation(MLA_SQ[:, tk, :, 0:w], PS[:, tk, 0:4 * w].rearrange("p (h e) -> p h e", h=4), ACT.Square)
                ins.then_inc(mla_sq, 1)

            u = UNIT["mem"]
            for c in range(4):
                stream(u + c + 2)
            norm_root(3, RT[:, R_MEM:10])
            used(u + 3)
            act.wait_ge(n_rstd, 3)
            head_evac(0)
            head_square(0)
            for k in range(1, 4):
                u = UNIT["tok2"] + 4 * (k - 1)
                stream(u + 2)
                head_root(k - 1)
                if k == 2:
                    norm_root(4, RSTD, YT)
                for c in range(1, 4):
                    stream(u + c + 2)
                used(u + 3)
                head_evac(k)
                head_hi(k - 1)
                head_square(k)
            head_root(3)
            u = UNIT["z"]
            for c in range(10):
                if c < 8:
                    stream(u + c + 2)
                if c == 2:
                    act.wait_ge(h_nrm, 4)
                    act.wait_ge(lam_sum, 1)
                    act.activation(LAM[:, 2:4], LAM[:, 0:2], ACT.Exp).then_inc(lam_exp, 1)
                if c == 7:
                    head_hi(3)
                if c >= 2:
                    act.wait_ge(scaled, SCALED["z"] + c - 1)
                    act.activation(FX[:, c - 2, :], PS[:, (c - 2) % 4, :], ACT.Silu).then_inc(z_done, 1)
            attention("dm")

            u = UNIT["uq"]
            stream(u + 2)
            used(u)
            mla_squares(4)
            head_root(4)
            stream(u + 3)
            used(u + 1)
            mla_squares(5)
            head_root(5)
            head_hi(4)
            for k in (6, 7):
                act.wait_ge(k_mm, k - 5)
                mla_squares(k)
                head_root(k)
                head_hi(k - 1)
            used(UNIT["ukv"])
            vh = cat(0, LV, 4).rearrange("p (t n) -> p t n", t=NT)
            for tk in range(NT):
                act.activation(vh[:, tk, :], PS[:, tk, :], ACT.Copy).then_inc(vm_hi, 1)
            head_hi(7)
            stream(UNIT["ukv"] + 2)
            attention("mla")
            u = UNIT["wout2"]
            with act.Fori(0, 3) as i:
                for s in range(2):
                    stream(u + 2 + s, 2, i)
            for n in range(KT):
                act.wait_ge(y_out, n + 1)
                act.dma_start(out[:, n, :], X[:, n, :]).then_inc(stored, 16)
            act.wait_ge(stored, 16 * KT)

        @block.vector
        def _(dve):
            chain = Chain(dve, dve_step)
            link = chain.link

            def norm_tile(k, i, s):
                dve.wait_ge(n_hi, 2 * i + (8 * k + s + 1))
                dve.scalar_tensor_tensor(out=tile_at(HLO, i, s), in0=tile_at(X, i, s), scalar=gain_at(NORM_GAIN[k], i, s),
                                         in1=tile_at(HHI, i, s).bitcast(F), op0=ALU.mult, op1=ALU.subtract).then_inc(n_lo, 1)
                per = 2 if k == 2 else 1
                for m in range(per):
                    n = 8 * k + per * s + m
                    dve.wait_ge(n_sq, 2 * per * i + (n + 1))
                    if not isinstance(i, int) or 2 * i + s:
                        dve.wait_ge(n_acc, 2 * per * i + (n - per + 1))
                    dve.tensor_tensor(ACC[m], ACC[m], SQ[n % 2], ALU.add).then_inc(n_acc, 1)

            def mean_inverse(dst, src):
                link(dve.tensor_scalar(dst, src, 1.0 / D, EPS, ALU.mult, ALU.add))
                return dve.reciprocal(dst, dst)

            def scale(bank):
                dve.tensor_tensor(PS[:, bank, :], PS[:, bank, :], RSTD, ALU.mult).then_inc(scaled, 1)

            link(dve.memset(ACC[0], 0.0))
            dve.wait_ge(ld_cols, 16)
            for i in range(4):
                for s in range(2):
                    norm_tile(0, i, s)
            dve.wait_ge(n_tot, 1)
            link(mean_inverse(RSTD, PS[:, 7, :]))
            mean_inverse(RT[:, 0:4], PS[:, 6, 0:4]).then_inc(n_rin, 1)
            dve.wait_ge(ld_small, 48)

            dve.memset(TBL[NBUCKET:NBUCKET + 1, :], NEG)
            link(dve.tensor_scalar(TBL[0:NBUCKET, :], TBL[0:NBUCKET, :], 8.0, None, ALU.mult))
            link(dve.tensor_scalar(row("sinks", 8), row("sinks", 8), -1.0, None, ALU.mult))
            dve.memset(MSK[:, :], 1.0).then_inc(tbl_ready, 1)
            link(dve.tensor_tensor(CL[:, COL["g_2"]:COL["g_2"] + 8], CL[:, COL["g_2"]:COL["g_2"] + 8],
                                   CL[:, COL["g_final"]:COL["g_final"] + 8], ALU.mult))
            dve.wait_ge(n_rstd, 1)

            def low_from_psum(dst_lo, dst_hi, src):
                return dve.tensor_tensor(dst_lo, src, dst_hi.bitcast(F), ALU.subtract)

            for c in range(2):
                dve.wait_ge(unit_used, UNIT["proj"] + c + 1)
                scale(c)
                dve.wait_ge(proj_hi, c + 1)
                low_from_psum(lo(c), hi(c), PS[:, c, :]).then_inc(proj_out, 1)
            with dve.Fori(1, 5) as i:
                for s in range(2):
                    dve.wait_ge(unit_used, 2 * i + (UNIT["proj"] + s + 1))
                    scale(s)
                    dve.wait_ge(proj_hi, 2 * i + (s + 1))
                    low_from_psum(BLO[:, bass.ds(2 * i + s, 1), :].rearrange("p a b -> p (a b)"),
                                  BHI[:, bass.ds(2 * i + s, 1), :].rearrange("p a b -> p (a b)"),
                                  PS[:, s, :]).then_inc(proj_out, 1)
            dve.wait_ge(unit_used, UNIT["proj"] + 11)
            scale(0)
            dve.wait_ge(proj_hi, 11)
            low_from_psum(lo(10), hi(10), PS[:, 0, :]).then_inc(proj_out, 1)
            dve.wait_ge(st_rows, 16)
            for c in (11, 12):
                dve.wait_ge(unit_used, UNIT["proj"] + c + 1)
                dve.tensor_tensor(FX[:, c - 11, :], PS[:, c % 2, :], RSTD, ALU.mult).then_inc(proj_out, 1)
            link(dve.memset(MSK[0:31, 0:1], 0.0))
            dve.memset(FX[:, 4:6, :], NEG * 8).then_inc(tbl_ready, 1)

            cb = PB[:, 0:2048].rearrange("p (t g i) -> p t g i", t=16, g=2)
            dve.wait_ge(proj_out, 13)
            link(dve.memset(PB[:, 0:2048], 0.0))
            for w in range(2):
                if w:
                    dve.wait_ge(cb_lo, 1)
                for g in range(2):
                    rows = slice(64 * g, 64 * g + 64)
                    for par in range(2):
                        src = FX[rows, w, par:par + 1]
                        src = bass.AP(src.tensor, src.offset, [list(src.ap[0]), [2, 16], [16, N_CMP]])
                        pos = CL[rows, COL[("pos_k", "pos_v")[w]] + par:COL[("pos_k", "pos_v")[w]] + 32:2]
                        ins = dve.tensor_tensor(cb[64 * par:64 * par + 64, :, g, 0:N_CMP], src,
                                                pos[:, :, None].broadcast_to([64, 16, N_CMP]), ALU.add)
                ins.then_inc(cb_built, 1)
                dve.wait_ge(cb_hi, w + 1)
                dve.tensor_tensor(cat(1, 14 + 4 * w, 4), PB[:, 0:2048], cat(0, 14 + 4 * w, 4).bitcast(F),
                                  ALU.subtract).then_inc(cb_lo, 1)
            dve.wait_ge(cb_built, 2)
            link(dve.memset(FX[:, 0, :], 0.0))
            link(dve.tensor_copy(KR[:, :, 0], POS[:, :]))
            ang = COS[:, :, 0:16]
            link(dve.tensor_tensor(ang, KR[:, :, 0:1].broadcast_to([P, NT, 16]),
                                   row("inv", 16)[:, None, :].broadcast_to([P, NT, 16]), ALU.mult))
            magic = 1.5 * 2.0 ** 23
            c1, c2, c3 = 6.28125, float(np.float32(2 * math.pi - 6.28125)), 0.0
            c3 = 2 * math.pi - c1 - c2
            for dst, shift in ((COS, 0.25), (SIN, 0.0)):
                turns, r = KR[:, :, 16:32], dst[:, :, 16:32]
                link(dve.tensor_scalar(turns, ang, 1.0 / (2 * math.pi), shift, ALU.mult, ALU.add))
                link(dve.tensor_scalar(turns, turns, magic, magic, ALU.add, ALU.subtract))
                link(dve.scalar_tensor_tensor(out=r, in0=turns, scalar=-c1, in1=ang, op0=ALU.mult, op1=ALU.add))
                for c in (c2, c3):
                    link(dve.scalar_tensor_tensor(out=r, in0=turns, scalar=-c, in1=r, op0=ALU.mult, op1=ALU.add))
                link(dve.tensor_scalar(r, r, shift * 2 * math.pi, 3.1415925, ALU.add, ALU.min))
                link(dve.tensor_scalar(r, r, -3.1415925, None, ALU.max))
            dve.memset(SS[:, :], 1.0).then_inc(ang_ready, 1)
            vh, vl = [cat(w, V_AT, 3).rearrange("p (t n) -> p t n", t=NT) for w in (0, 1)]
            for tk in range(NT):
                dve.wait_ge(v_hi, NT + 1)
                dve.scalar_tensor_tensor(out=vl[:, tk, :], in0=PS[:, 2 + tk, 0:384], scalar=RT[:, tk:tk + 1],
                                         in1=vh[:, tk, :].bitcast(F), op0=ALU.mult, op1=ALU.subtract).then_inc(v_lo, 1)
            dve.wait_ge(sin_ready, 1)
            link(dve.tensor_copy(COS[:, :, 0:16], COS[:, :, 16:32]))
            link(dve.tensor_scalar(SIN[:, :, 0:16], SIN[:, :, 16:32], -1.0, None, ALU.mult))


            def biased(A, m):
                pr = prob(m)
                if m["i"] and m["prev"].get("mode") == "sub":
                    dve.wait_ge(A["normed"], m["prev"]["t1"])
                if m["prev2"]:
                    dve.wait_ge(A["turned"], m["prev2"])
                if m.get("cmp") is not None and m["bias"] == 8:
                    dve.wait_ge(ld_cmp, 16 * NH)
                if m["kind"] == "mem":
                    for b in range(2):
                        dve.wait_ge(A["scores"], m["g0"] + b + 1)
                        two = slice(2 * b, 2 * b + 2)
                        link(dve.tensor_reduce(stat(m, MAX)[:, two], PS[:, b, :].rearrange("p (q c) -> p q c", q=2),
                                               AX.X, ALU.max))
                        dve.tensor_scalar(stat(m, NMAX)[:, two], stat(m, MAX)[:, two], -m["scale"], None,
                                          ALU.mult).then_inc(A["biased"], 1)
                    return
                if "bias" in m and m["first"]:
                    y = m["bias"]
                    dve.wait_ge(ld_bias[y % 2], 16 * (y // 2 + 1))
                for g, qs in enumerate(m["groups"]):
                    dve.wait_ge(A["scores"], m["g0"] + g + 1)
                    for q in qs:
                        (b, o), (_, nk) = m["place"][q], m["spans"][q]
                        init = row("sinks", 8)[:, m["h"]:m["h"] + 1] if m.get("sink") else 3e38
                        ins = dve.tensor_tensor_reduce(prob_of(m, q), PS[:, b, o:o + nk], bias_of(m, q), -m["scale"], init,
                                                       ALU.add, ALU.min, stat(m, NMAX)[:, q:q + 1])
                    ins.then_inc(A["biased"], 1)

            def normed(A, m):
                pr = prob(m)
                dve.wait_ge(A["exped"], m["i"] + 1)
                if m.get("sink"):
                    link(dve.tensor_tensor(stat(m, SUM), stat(m, SUM), stat(m, SINK), ALU.add))
                link(dve.reciprocal(stat(m, WT), stat(m, SUM)))
                w4 = stat(m, WT)[:, 0:4]
                if "cmp" in m:
                    c4 = stat(m, WT)[:, 4:8]
                    dve.tensor_tensor(c4, c4, GATE[:, :, m["cmp"]], ALU.mult).then_inc(dve_step, 1)
                    chain.n += 1
                if "gate" in m:
                    link(dve.tensor_tensor(w4, w4, GATE[:, :, m["gate"]], ALU.mult))
                if "cmp" in m:
                    link(dve.tensor_tensor(c4, c4, MSK[:, :], ALU.mult))
                if m.get("mode") == "sub":
                    link(dve.tensor_tensor(stat(m, WT), stat(m, WT), LAM[:, 0:1].broadcast_to([P, NT]), ALU.mult))
                for qs in m["groups"]:
                    for q in qs:
                        if q >= 4:
                            if q == 4:
                                p4 = prob_cmp(m).rearrange("p (q c) -> p q c", q=NT)
                                ins = dve.tensor_tensor(p4, p4, c4[:, :, None].broadcast_to([P, NT, 32]), ALU.mult)
                            continue
                        ap = prob_of(m, q)
                        w = stat(m, WT)[:, q:q + 1]
                        if m.get("mode") == "sub":
                            o = PB[:, (1 - m["i"] % 2) * 1280:(2 - m["i"] % 2) * 1280][:, m["p"][q]:m["p"][q] + m["spans"][q][1]]
                            ins = dve.scalar_tensor_tensor(out=ap, in0=ap, scalar=w, in1=o, op0=ALU.mult, op1=ALU.add)
                        else:
                            ins = dve.tensor_scalar(ap, ap, w, None, ALU.mult)
                    if m.get("mode") != "hold":
                        ins.then_inc(A["normed"], 1)
                if m.get("mode") == "hold":
                    link(ins)

            def attention(name):
                maps, pts = GROUP[name]
                A = ATT[name]
                for i in range(-1, len(maps) + (2 if name == "ab" else 3)):
                    if name == "ab" and i == 4:
                        dve.wait_ge(cmp_hi, 1)
                        for g in range(2):
                            half = slice(64 * g, 64 * g + 64)
                            low_from_psum(lo(22)[half, KC:KC + 32], hi(22)[half, KC:KC + 32], PS[half, 2, 64 * g:64 * g + 32])
                        for q in range(NT):
                            ins = dve.tensor_copy(v_cmp(q)[32 * q:32 * q + 32, :], PS[0:32, 2, P:2 * P])
                        ins.then_inc(cmp_lo, 1)
                    steps = [(biased, i + 1), (normed, i)]
                    for f, j in (steps[::-1] if name == "dm" else steps):
                        if 0 <= j < len(maps):
                            f(A, maps[j])
                    tile = diff_tile(maps, i - 4)
                    if tile is not None:
                        dve.wait_ge(dm_rstd, tile + 1)
                        link(dve.scalar_tensor_tensor(out=YT, in0=YT, scalar=col("subln"), in1=YSQ,
                                                      op0=ALU.mult, op1=ALU.mult))
                        dve.scalar_tensor_tensor(out=YT, in0=YT, scalar=1.0 - LAM_INIT, in1=FX[:, 4 + tile, :],
                                                 op0=ALU.mult, op1=ALU.mult).then_inc(dm_y, 1)
                    if 0 <= i - 3 < len(maps) and "yf" in maps[i - 3]:
                        m = maps[i - 3]
                        rows = m["rows"]
                        dve.wait_ge(A["y_hi"], m["y"] + 1)
                        low_from_psum(lo(m["ytile"])[rows, :], hi(m["ytile"])[rows, :], PS[rows, m["bank"], :]).then_inc(A["y_lo"], 1)
                    if 0 <= i - 1 < len(maps) and maps[i - 1].get("mode") != "hold":
                        m = maps[i - 1]
                        pt = pts[m["n"] % 2]
                        for g, qs in enumerate(m["groups"]):
                            dve.wait_ge(A["p_hi"], m["t0"] + g + 1)
                            for q in [q for q in qs if q < 4]:
                                dst, src = turned_aps(m, pt, q, 1)
                                ins = low_from_psum(dst, turned_aps(m, pt, q, 0)[0], src)
                            ins.then_inc(A["p_lo"], 1)
                    if tile is not None:
                        dve.wait_ge(dm_hi, tile + 1)
                        low_from_psum(lo(Y_DM + tile), hi(Y_DM + tile), YT).then_inc(dm_lo, 1)
                    if 0 <= i - 2 < len(maps) and maps[i - 2]["last"]:
                        m = maps[i - 2]
                        rows, yh, yl = m["rows"], hi(m["ytile"]), lo(m["ytile"])
                        ps = PS[rows, m["bank"], :]
                        if name == "ab":
                            dve.wait_ge(A["y_hi"], m["y"] + 1)
                            low_from_psum(yl[rows, :], yh[rows, :], ps).then_inc(A["y_lo"], 1)
                        elif not m.get("diff"):
                            dve.wait_ge(A["pv"], m["n"])
                            dve.tensor_tensor(ps, ps, FX[rows, m["ztile"], :], ALU.mult).then_inc(A["y_f"], 1)
                    if diff_tile(maps, i - 3) is not None:
                        tile = diff_tile(maps, i - 3)
                        dve.wait_ge(dm_tot, tile + 1)
                        dve.tensor_scalar(YSQ, PS[:, DIFF_BANK[tile], :], 1.0 / 64, EPS, ALU.mult, ALU.add).then_inc(dm_rin, 1)
                        dve.wait_ge(dm_rin, 2 * tile + 1)
                        dve.reciprocal(YSQ, YSQ).then_inc(dm_rin, 1)

            attention("ab")

            def merge(i):
                for s in range(2):
                    d = 8 * i + 4 * s
                    for e in range(2):
                        dve.wait_ge(unit_used, 6 * i + (UNIT["merge"] + 3 * s + e + 1))
                        scale(4 * s + e)
                    dve.wait_ge(unit_used, UNIT["merge"] + 6 * i + (3 * s + 3))
                    for e in range(2):
                        dve.wait_ge(merge_act, 6 * i + (3 * s + 1 + e))
                        dve.tensor_tensor(FX[:, 4 + 2 * e + s, :], PS[:, 4 * s + 2 + e, :], FX[:, 2 * e + s, :],
                                          ALU.mult).then_inc(merge_dve, 1)
                    dve.wait_ge(merge_dve, d + 2)
                    dve.tensor_tensor(FX[:, 4 + s, :], FX[:, 4 + s, :], FX[:, 6 + s, :], ALU.add).then_inc(merge_dve, 1)
                    dve.wait_ge(merge_act, 6 * i + (3 * s + 3))
                    if isinstance(i, int):
                        h_, l_ = hi(14 + s), lo(14 + s)
                    else:
                        h_, l_ = [a[:, bass.ds(2 * i + (14 + s), 1), :].rearrange("p a b -> p (a b)") for a in (BHI, BLO)]
                    low_from_psum(l_, h_, FX[:, 4 + s, :]).then_inc(merge_dve, 1)
            merge(0)
            with dve.Fori(1, 4) as i:
                merge(i)

            def memory_low():
                for kt in range(KT):
                    dve.wait_ge(mem_hi, kt + 1)
                    dve.scalar_tensor_tensor(out=mem_part[1][:, kt, :], in0=memx[:, 256 * kt:256 * kt + 256],
                                             scalar=col("g_mem", kt), in1=mem_part[0][:, kt, :].bitcast(F),
                                             op0=ALU.mult, op1=ALU.subtract).then_inc(mem_lo, 1)

            def residual(name, per, done, k=None):
                def one(i):
                    for s in range(2):
                        if name == "down" and isinstance(i, int) and (i, s) == (3, 1):
                            memory_low()
                        dve.wait_ge(unit_used, UNIT[name] + 2 * per * i + per * (s + 1))
                        x = tile_at(X, i, s)
                        dve.tensor_tensor(x, PS[:, s, :], x, ALU.add).then_inc(done, 1)
                        if k is not None:
                            norm_tile(k, i, s)
                one(0)
                with dve.Fori(1, 3) as i:
                    one(i)
                one(3)

            link(dve.memset(ACC[0], 0.0))
            residual("wout", 1, x1_done, 1)
            dve.wait_ge(n_tot, 2)
            mean_inverse(RSTD, PS[:, 7, :]).then_inc(n_rin, 1)
            dve.wait_ge(n_rstd, 2)

            def ffn(i):
                for s in range(2):
                    d = 12 * i + 6 * s
                    for e in range(2):
                        dve.wait_ge(unit_used, 4 * i + (UNIT["ffn"] + 2 * s + e + 1))
                        scale(2 * e + s)
                    for tap in (1, 0):
                        for e in range(2):
                            at = COL["conv"] + 4 * e + 8 * s
                            cv = CL[:, at:at + 4] if isinstance(i, int) else CL[:, bass.ds(16 * i + at, 4)]
                            if tap == 1:
                                dve.wait_ge(ffn_act, 8 * i + (4 * s + 1 + e))
                            else:
                                dve.wait_ge(ffn_dve, d + (1 + e))
                            sh = 2 - tap
                            y = FX[:, 2 * e + s, sh:SEQ]
                            dve.scalar_tensor_tensor(out=y, in0=PS[:, 2 * e + s, 0:SEQ - sh], scalar=cv[:, tap:tap + 1],
                                                     in1=y, op0=ALU.mult, op1=ALU.add).then_inc(ffn_dve, 1)
                    dve.wait_ge(ffn_act, 8 * i + (4 * s + 3))
                    dve.tensor_tensor(FX[:, 6 + s, :], FX[:, 4 + s, :], FX[:, s, :], ALU.mult).then_inc(ffn_dve, 1)
                    dve.wait_ge(ffn_act, 8 * i + (4 * s + 4))
                    if isinstance(i, int):
                        h_, l_ = hi(s), lo(s)
                    else:
                        h_, l_ = [a[:, bass.ds(2 * i + s, 1), :].rearrange("p a b -> p (a b)") for a in (BHI, BLO)]
                    low_from_psum(l_, h_, FX[:, 6 + s, :]).then_inc(ffn_dve, 1)
            ffn(0)
            with dve.Fori(1, NF // 2) as i:
                ffn(i)

            link(dve.memset(ACC[0], 0.0))
            link(dve.memset(ACC[1], 0.0))
            residual("down", 3, x2_done, 2)
            dve.wait_ge(n_tot, 3)
            def both(first, second, sum1, sum2):
                link(mean_inverse(first, sum1))
                link(dve.tensor_tensor(second, sum2, first[:, 0:second.shape[1]], ALU.mult))
                link(mean_inverse(second, second))
                return dve.tensor_tensor(second, second, first[:, 0:second.shape[1]], ALU.mult)
            both(RT[:, 0:R_TWO], RT[:, R_TWO:10], PS[:, 5, 0:R_TWO], PS[:, 5, R_TWO:10]).then_inc(n_rin, 1)

            def head_norm(k):
                h = HEADS[k]
                nt, n = h["nt"], h["n"]
                tok = TOK[:, 0:nt * n].rearrange("p (t n) -> p t n", t=nt)
                sq, ra, rb = scratch(k)
                dve.wait_ge(h_sq, k + 1)
                at = 0
                groups = []
                for o, g, w, gain in h["parts"]:
                    ss = SS[:, at:at + nt * g]
                    if g == 1:
                        src = sq[:, 0:nt * n].rearrange("p (t n) -> p t n", t=nt)[:, :, o:o + w]
                    else:
                        src = sq[:, 0:nt * n].rearrange("p (t n) -> p t n", t=nt)[:, :, o:o + g * w] \
                            .rearrange("p t (g w) -> p t g w", g=g)
                        ss = ss.rearrange("p (t g) -> p t g", t=nt)
                    link(dve.tensor_reduce(ss, src, AX.X, ALU.add))
                    flat = SS[:, at:at + nt * g]
                    link(dve.tensor_scalar(flat, flat, 1.0 / w, EPS, ALU.mult, ALU.add))
                    groups.append((at, o, g, w, gain))
                    at += nt * g
                dve.reciprocal(SS[:, 0:at], SS[:, 0:at]).then_inc(h_rin, 1)
                if k == 1:
                    link(dve.tensor_copy(KR[:, :, :], tok[:, :, 384:416]))
                dve.wait_ge(h_rs, k + 1)
                for a0, o, g, w, gain in groups:
                    for tk in range(nt):
                        v = tok[:, tk, o:o + g * w].rearrange("p (g w) -> p g w", g=g)
                        r = SS[:, a0 + tk * g:a0 + (tk + 1) * g]
                        ins = dve.tensor_tensor(v, v, r[:, :, None].broadcast_to([P, g, w]), ALU.mult)
                    link(ins)
                    if gain:
                        for tk in range(nt):
                            v = tok[:, tk, o:o + g * w].rearrange("p (g w) -> p g w", g=g)
                            ins = dve.tensor_tensor(v, v, row(gain, w)[:, None, :].broadcast_to([P, g, w]), ALU.mult)
                        link(ins)
                if h["rope"] is not None:
                    o, g, w, f = h["rope"]
                    for tk in range(nt):
                        v = tok[:, tk, o:o + g * w].rearrange("p (g w) -> p g w", g=g)[:, :, f:f + 32]
                        a = ra[:, tk * g * 32:(tk + 1) * g * 32].rearrange("p (g w) -> p g w", g=g)
                        b = rb[:, tk * g * 32:(tk + 1) * g * 32].rearrange("p (g w) -> p g w", g=g)
                        dve.tensor_tensor(a, v, COS[:, tk, None, :].broadcast_to([P, g, 32]), ALU.mult)
                        for x, y in ((0, 16), (16, 0)):
                            ins = dve.tensor_tensor(b[:, :, x:x + 16], v[:, :, y:y + 16],
                                                    SIN[:, tk, None, x:x + 16].broadcast_to([P, g, 16]), ALU.mult)
                    link(ins)
                    for tk in range(nt):
                        v = tok[:, tk, o:o + g * w].rearrange("p (g w) -> p g w", g=g)[:, :, f:f + 32]
                        a = ra[:, tk * g * 32:(tk + 1) * g * 32].rearrange("p (g w) -> p g w", g=g)
                        b = rb[:, tk * g * 32:(tk + 1) * g * 32].rearrange("p (g w) -> p g w", g=g)
                        ins = dve.tensor_tensor(v, a, b, ALU.add)
                    link(ins)
                if "v" in h:
                    o, w, tile = h["v"]
                    dve.wait_ge(h_v, {0: 1, 3: 2}[k])
                    v = [cat(w_, tile, nt * w // SEQ).rearrange("p (t n) -> p t n", t=nt) for w_ in (0, 1)]
                    link(dve.tensor_tensor(v[1], tok[:, :, o:o + w], v[0].bitcast(F), ALU.subtract))
                link(dve.memset(SS[:, at:at + 1], 1.0) if at < 64 else dve.memset(LAM[:, 3:4], 1.0))
                dve.nop().then_inc(h_nrm, 1)

            def head_lo(k):
                h = HEADS[k]
                dve.wait_ge(h_hi, k + 1)
                for j, tile in enumerate(h["tiles"]):
                    w = h["turn"][0][1]
                    if h.get("memk"):
                        ins = low_from_psum(lo(tile), hi(tile), PS[:, 4, :])
                    elif "gain" in h:
                        ins = dve.scalar_tensor_tensor(out=lo(tile), in0=PS[:, 4 + j, :], scalar=col(*h["gain"][j]),
                                                       in1=hi(tile).bitcast(F), op0=ALU.mult, op1=ALU.subtract)
                    elif "gain_t" in h:
                        at = COL[h["gain_t"]]
                        ins = dve.scalar_tensor_tensor(out=lo(tile)[0:w, :], in0=PS[0:w, 4 + j, :], scalar=CL[0:w, at:at + 1],
                                                       in1=hi(tile)[0:w, :].bitcast(F), op0=ALU.mult, op1=ALU.subtract)
                    else:
                        ins = low_from_psum(lo(tile)[0:w, :], hi(tile)[0:w, :], PS[0:w, 4 + j, :])
                ins.then_inc(h_lo, 1)

            def mla_norm(k):
                h = HEADS[k]
                tok = TOK[:, 0:1536].rearrange("p (t h e) -> p t h e", t=NT, h=4)
                r = SS[:, 0:16].rearrange("p (t h) -> p t h", t=NT)
                dve.wait_ge(mla_sq, k - 3)
                link(dve.tensor_reduce(r, MLA_SQ, AX.X, ALU.add))
                link(dve.tensor_scalar(SS[:, 0:16], SS[:, 0:16], 1.0 / 96, EPS, ALU.mult, ALU.add))
                dve.reciprocal(SS[:, 0:16], SS[:, 0:16]).then_inc(h_rin, 1)
                dve.wait_ge(h_rs, k + 1)
                if k > 4:
                    dve.wait_ge(h_tr, k)
                w = 64 if h["kpart"] else 96
                for tk in range(NT):
                    rt = r[:, tk, :, None]
                    if h["kpart"]:
                        dve.tensor_tensor(tok[:, tk, :, 64:96], KR[:, tk, None, :].broadcast_to([P, 4, 32]),
                                          rt.broadcast_to([P, 4, 32]), ALU.mult)
                    dve.tensor_tensor(tok[:, tk, :, 0:w], PS[:, tk, 0:4 * w].rearrange("p (h e) -> p h e", h=4),
                                      rt.broadcast_to([P, 4, w]), ALU.mult).then_inc(h_tok, 1)
                if k > 4:
                    head_lo(k - 1)
                dve.wait_ge(h_tok, tiles_before(k + 1))
                name = h["gain_t"][:2]
                g = RW[:, ROW[name] + 64:ROW[name] + 96]
                v = tok[:, :, :, 64:96]
                link(dve.tensor_tensor(v, v, g[:, None, None, :].broadcast_to([P, NT, 4, 32]), ALU.mult))
                for half in range(2):
                    two = slice(2 * half, 2 * half + 2)
                    v = tok[:, two, :, 64:96]
                    dve.tensor_tensor(MLA_ROT[:, 0], v, COS[:, two, None, :].broadcast_to([P, 2, 4, 32]), ALU.mult)
                    for x, y in ((0, 16), (16, 0)):
                        ins = dve.tensor_tensor(MLA_ROT[:, 1, :, :, x:x + 16], v[:, :, :, y:y + 16],
                                                SIN[:, two, None, x:x + 16].broadcast_to([P, 2, 4, 16]), ALU.mult)
                    link(ins)
                    ins = dve.tensor_tensor(v, MLA_ROT[:, 0], MLA_ROT[:, 1], ALU.add)
                    if half == 0:
                        link(ins)
                ins.then_inc(h_nrm, 1)

            head_norm(0)
            dve.wait_ge(n_tot, 4)
            both(RSTD, YT, PS[:, 7, :], PS[:, 6, :]).then_inc(n_rin, 1)
            for k in range(1, 4):
                head_lo(k - 1)
                head_norm(k)
            lv = row("lam", 128).rearrange("p (a b c) -> p a b c", a=2, b=2)
            prod = PB[:, 4 * SEQ:4 * SEQ + 64].rearrange("p (a c) -> p a c", a=2)
            link(dve.tensor_tensor(prod, lv[:, :, 0, :], lv[:, :, 1, :], ALU.mult))
            dve.tensor_reduce(LAM[:, 0:2], prod, AX.X, ALU.add).then_inc(lam_sum, 1)
            for c in range(8):
                if c == 7:
                    head_lo(3)
                dve.wait_ge(n_rstd, 4)
                dve.wait_ge(unit_used, UNIT["z"] + c + 1)
                dve.tensor_tensor(PS[:, c % 4, :], PS[:, c % 4, :], YT, ALU.mult).then_inc(scaled, 1)
                link(dve.scalar_tensor_tensor(out=X[:, c, :], in0=X[:, c, :], scalar=col("g_final", c), in1=RSTD,
                                              op0=ALU.mult, op1=ALU.mult))
            dve.wait_ge(lam_exp, 1)
            link(dve.tensor_tensor(LAM[:, 0:1], LAM[:, 3:4], LAM[:, 2:3], ALU.subtract))
            link(dve.tensor_scalar(LAM[:, 0:1], LAM[:, 0:1], -LAM_INIT, None, ALU.add))
            attention("dm")
            for k in range(4, 8):
                mla_norm(k)
            vh, vl = [cat(w, LV, 4).rearrange("p (t n) -> p t n", t=NT) for w in (0, 1)]
            for tk in range(NT):
                dve.wait_ge(vm_hi, tk + 1)
                low_from_psum(vl[:, tk, :], vh[:, tk, :], PS[:, tk, :]).then_inc(vm_lo, 1)
            head_lo(7)
            attention("mla")

            residual("wout2", 1, y_out)

        @block.tensor
        def _(pe):
            def three(dst, a, b, first, last, **kw):
                pe.matmul(dst, a[0], b[0], start=first, stop=False, **kw)
                pe.matmul(dst, a[0], b[1], start=False, stop=False, **kw)
                return pe.matmul(dst, a[1], b[0], start=False, stop=last, **kw)

            def arrive(c, n=0, i=0):
                pe.wait_ge(split_lo, (c + 1) + n * i)

            def weight(c, sub, width=P, pitch=P):
                a = sub * pitch
                return WHI[:, c % 2, a:a + width], WLO[:, c % 2, a:a + width]

            def unit_T(c, bank, acts, n=0, i=0, subs=range(8), first=True, last=True, norm=None, tile_ready={}):
                arrive(c, n, i)
                subs = list(subs)
                for j in subs:
                    if j in tile_ready:
                        pe.wait_ge(*tile_ready[j])
                    if norm is not None:
                        pe.wait_ge(n_lo, 8 * norm + j + 1)
                    ins = three(PS[:, bank, :], weight(c, j), acts(j), first and j == subs[0], last and j == subs[-1])
                return ins

            H = lambda kt: (HHI[:, kt, :], HLO[:, kt, :])

            def column_sums(dst, *srcs):
                for tk in range(dst.shape[1]):
                    for n, src in enumerate(srcs):
                        ins = pe.matmul(dst[:, tk:tk + 1], src[:, tk * P:(tk + 1) * P], ONE[:, 0:1], start=n == 0,
                                        stop=n == len(srcs) - 1)
                return ins

            pe.wait_ge(consts, 4)
            u = UNIT["proj"]
            for c in range(2):
                unit_T(u + c, c, H, norm=0 if c == 0 else None).then_inc(unit_used, 1)
                if c == 0:
                    pe.wait_ge(n_acc, 8)
                    column_sums(PS[:, 6, 0:4], ACC[0])
                    pe.matmul(PS[:, 7, :], ONE[:, :], ACC[0], start=True, stop=True).then_inc(n_tot, 1)
                else:
                    pe.wait_ge(n_rin, 1)
                    pe.wait_ge(tbl_ready, 1)
                    pe.wait_ge(ld_oh, 16)
                    fx33 = FX[0:NBUCKET + 1, :, :].rearrange("p a b -> p (a b)")
                    for b in range(5):
                        a, e = OH * b // 5, OH * (b + 1) // 5
                        ins = pe.matmul(PS[0:16, 2 + b, 0:e - a], TBL[:, :], fx33[:, a:e], start=True, stop=True)
                    ins.then_inc(oh_mm, 1)
            with pe.Fori(1, 5) as i:
                for s in range(2):
                    pe.wait_ge(proj_out, 2 * i + (s - 1))
                    unit_T(u + s, s, H, 2, i).then_inc(unit_used, 1)
            for c in (10, 11, 12):
                pe.wait_ge(proj_out, c - 1)
                unit_T(u + c, c % 2, H).then_inc(unit_used, 1)
            def unit_tok(c, n, toks, acts, banks, first, last, kts=2, pitch=None, inc=True, free=None):
                arrive(c)
                for tk in toks:
                    if free is not None:
                        pe.wait_ge(h_tok, min(free + tk + 1, free + HEADS[HEAD_AT[free]]["nt"]))
                    for j in range(kts):
                        a = acts(c, j)
                        a = (a[0][:, tk * P:(tk + 1) * P], a[1][:, tk * P:(tk + 1) * P])
                        ins = three(PS[:, banks + tk, 0:n], a, weight(c, j, n, pitch or n), first and j == 0, last and j == kts - 1)
                if inc:
                    ins.then_inc(unit_used, 1)
                return ins

            u = UNIT["vtok"]
            pe.wait_ge(oh_ev, 1)
            for c in range(4):
                unit_tok(u + c, 408, range(4), lambda c_, j, c=c: H(2 * c + j), 2, c == 0, c == 3)
            u = UNIT["cmp"]
            for w in range(2):
                pe.wait_ge(cb_lo, w + 1)
                cbs = [cat(x, 14 + 4 * w, 4) for x in (0, 1)]
                for c in range(4):
                    arrive(u + 4 * w + c)
                    for j in range(4):
                        tp = 4 * c + j
                        ins = three(PS[:, 6 + w, 0:256], [b[:, tp * P:(tp + 1) * P] for b in cbs],
                                    weight(u + 4 * w + c, j, 256, 256), tp == 0, tp == 15)
                    ins.then_inc(unit_used, 1)
            pe.wait_ge(v_lo, 4)
            pe.wait_ge(v_hi, 5)

            def compressed(step):
                if step == 0:
                    pe.wait_ge(gelu_done, 2)
                    for j in range(4):
                        ins = pe.transpose(PS[:, 5, j * P:(j + 1) * P], FX[:, 6, j * P:(j + 1) * P], IDN[:, :])
                    ins.then_inc(gelu_t, 1)
                else:
                    pe.wait_ge(gelu_copied, 1)
                    pe.wait_ge(ld_w2, 16)
                    gt = FX[:, 7, :].rearrange("p (w h n) -> p w h n", w=2, h=2)
                    for c in range(2):
                        pe.matmul(PS[:, 2, 0:P], W2[:, 0, c, :], gt[:, 0, c, :], start=c == 0, stop=c == 1)
                    for g in range(2):
                        for c in range(2):
                            ins = pe.matmul(PS[0:32, 2, P + 64 * g:P + 64 * g + 64], gt[:, 1, c, 64 * g:64 * g + 32],
                                            W2[:, 1, c, 0:64], start=c == 0, stop=c == 1)
                    ins.then_inc(cmp_mm, 1)

            def scores(A, m):
                for g, qs in enumerate(m["groups"]):
                    if m["s_free"][g]:
                        name, value = m["s_free"][g]
                        pe.wait_ge(A[name], value)
                    for q in qs:
                        a = [x[:, q % 4 * P:(q % 4 + 1) * P] for x in m["q"]]
                        (b, o), (k0, nk) = m["place"][q], m["spans"][q]
                        keys = m["kc"] if q >= 4 else [x[:, k0:k0 + nk] for x in m["k"]]
                        ins = three(PS[:, b, o:o + nk], a, keys, True, True)
                    ins.then_inc(A["scores"], 1)

            def turn(A, m):
                pr = prob(m)
                for g, qs in enumerate(m["groups"]):
                    pe.wait_ge(A["normed"], m["t0"] + g + 1)
                    if m["t_free"][g]:
                        pe.wait_ge(A["p_lo"], m["t_free"][g])
                    for q in qs:
                        if q >= 4:
                            if q == 4:
                                ins = pe.transpose(PS[:, 5, 256:384], prob_cmp(m), IDN[:, :])
                            continue
                        (b, o), (k0, nk) = m["place"][q], m["spans"][q]
                        for j in range(nk // P):
                            p0 = m["p"][q] + j * P
                            ins = pe.transpose(PS[:, 3 + b, o + j * P:o + (j + 1) * P], pr[:, p0:p0 + P], IDN[:, :])
                    ins.then_inc(A["turned"], 1)

            def values(name, A, m, pts):
                pe.wait_ge(A["p_lo"], m["t1"])
                y = m["y"]
                if m["first"] and y >= 2:
                    if name != "dm":
                        pe.wait_ge(A["y_lo"], y - 1)
                    elif y >= 6:
                        pe.wait_ge(A["y_lo"], y - 5)
                    elif y == 3:
                        pe.wait_ge(dm_rin, 1)
                    else:
                        pe.wait_ge(A["y_hi"], y - 1)
                pt = pts[m["n"] % 2]
                for kb in range(m["nkb"]):
                    q0, q1 = m["kb"](kb)
                    ins = three(PS[:, m["bank"], q0:q1], [m["v"][w](kb) for w in (0, 1)],
                                [part(w, pt + kb)[:, q0:q1] for w in (0, 1)],
                                m["first"] and kb == 0, m["last"] and kb == m["nkb"] - 1, skip_group_check=True)
                for q in range(NT if "cmp" in m else 0):
                    ins = pe.matmul(PS[:, m["bank"], q * P:(q + 1) * P], v_cmp(q), turned_cmp(m),
                                    start=False, stop=False, skip_group_check=True)
                ins.then_inc(A["pv"], 1)

            def attention(name):
                maps, pts = GROUP[name]
                A = ATT[name]
                for i in range(-2, len(maps) + 2):
                    if name == "ab" and i in (0, 2):
                        compressed(i)
                    if name == "mla" and i == 0:
                        pe.wait_ge(h_lo, 8)
                    if name == "ab" and i + 2 == 8:
                        pe.wait_ge(cmp_lo, 1)
                    if 0 <= i + 2 < len(maps):
                        scores(A, maps[i + 2])
                    if 0 <= i < len(maps) and maps[i].get("mode") != "hold":
                        turn(A, maps[i])
                    if diff_tile(maps, i - 3) is not None:
                        tile = diff_tile(maps, i - 3)
                        pe.wait_ge(dm_sq, tile + 1)
                        pe.matmul(PS[:, DIFF_BANK[tile], :], BONE[:, :], YSQ, start=True, stop=True,
                                  skip_group_check=True).then_inc(dm_tot, 1)
                    if 0 <= i - 1 < len(maps) and maps[i - 1].get("mode") != "hold":
                        values(name, A, maps[i - 1], pts)

            attention("ab")

            u = UNIT["merge"]
            def merge(i):
                for s in range(2):
                    if not isinstance(i, int):
                        pe.wait_ge(merge_dve, 8 * i + (4 * s - 8 + 2))
                    for e in range(2):
                        unit_T(u + 3 * s + e, 4 * s + e, H, 6, i).then_inc(unit_used, 1)
                    if isinstance(i, int) and s == 0:
                        pe.wait_ge(ATT["ab"]["y_lo"], 16)
                    c = u + 3 * s + 2
                    ya = lambda j: (hi(j), lo(j))
                    unit_T(c, 4 * s + 2, ya, 6, i, range(0, 4))
                    unit_T(c, 4 * s + 3, ya, 6, i, range(4, 8)).then_inc(unit_used, 1)
            merge(0)
            with pe.Fori(1, 4) as i:
                merge(i)

            def dense(name, acts, done, order, tile_ready):
                c0 = UNIT[name]
                unit_T(c0, 0, acts, subs=order, tile_ready=tile_ready).then_inc(unit_used, 1)
                unit_T(c0 + 1, 1, acts).then_inc(unit_used, 1)
                with pe.Fori(1, 4) as i:
                    for s in range(2):
                        pe.wait_ge(done, 2 * i + (s - 1))
                        unit_T(c0 + s, s, acts, 2, i).then_inc(unit_used, 1)

            dense("wout", lambda j: (hi(14 + j), lo(14 + j)), x1_done, range(8),
                  {0: (merge_dve, 26), 6: (merge_dve, 28), 7: (merge_dve, 32)})

            u = UNIT["ffn"]
            def ffn(i):
                for s in range(2):
                    if not isinstance(i, int):
                        pe.wait_ge(ffn_dve, 12 * i + (6 * s - 12 + 4))
                    for e in range(2):
                        first = isinstance(i, int) and s == 0 and e == 0
                        unit_T(u + 2 * s + e, 2 * e + s, H, 4, i, norm=1 if first else None).then_inc(unit_used, 1)
                        if first:
                            pe.wait_ge(n_acc, 16)
                            pe.matmul(PS[:, 7, :], ONE[:, :], ACC[0], start=True, stop=True).then_inc(n_tot, 1)
            pe.wait_ge(x1_done, 7)
            ffn(0)
            with pe.Fori(1, NF // 2) as i:
                ffn(i)

            u = UNIT["down"]
            def down(i):
                for s in range(2):
                    if not isinstance(i, int):
                        pe.wait_ge(x2_done, 2 * i + (s - 1))
                    for e in range(3):
                        if isinstance(i, int) and s == 0 and e == 2:
                            pe.wait_ge(ffn_dve, 6 * NF)
                        unit_T(u + 3 * s + e, s, lambda j, e=e: (hi(8 * e + j), lo(8 * e + j)), 6, i,
                               range(min(8, NF - 8 * e)), e == 0, e == 2).then_inc(unit_used, 1)
            pe.wait_ge(ffn_dve, 6 * (NF - 1))
            down(0)
            down(1)
            pe.wait_ge(mem_sq, 1)
            mem_squares = FX[:, 4:8, :].rearrange("p a b -> p (a b)")
            column_sums(PS[:, 5, R_MEM:R_TWO], *[mem_squares[:, 256 * kt:256 * kt + 256] for kt in range(KT)])
            with pe.Fori(2, 4) as i:
                down(i)

            def head_turn(k):
                h = HEADS[k]
                pe.wait_ge(h_nrm, k + 1)
                if k:
                    pe.wait_ge(h_lo, k)
                for tk in range(h["nt"]):
                    for j, (o, w) in enumerate(h["turn"]):
                        dst = PS[0:w, 4, (2 * j + tk) * P:(2 * j + tk + 1) * P] if h.get("memk") \
                            else PS[0:w, 4 + j, tk * P:(tk + 1) * P]
                        ins = pe.transpose(dst, TOK[:, tk * h["n"] + o:tk * h["n"] + o + w], IDN[:, :])
                ins.then_inc(h_tr, 1)

            pe.wait_ge(x2_done, 8)
            pe.wait_ge(mem_lo, 8)
            u = UNIT["mem"]
            for c in range(4):
                unit_tok(u + c, 512, range(2), lambda c_, j, c=c: (mem_part[0][:, 2 * c + j, :], mem_part[1][:, 2 * c + j, :]),
                         0, c == 0, c == 3)
                if c == 0:
                    pe.wait_ge(n_acc, 32)
                    column_sums(PS[:, 5, 0:4], ACC[0])
                    column_sums(PS[:, 5, R_TWO:10], ACC[1]).then_inc(n_tot, 1)
                if c == 1:
                    pe.matmul(PS[:, 7, :], ONE[:, :], ACC[0], start=True, stop=True)
                    pe.matmul(PS[:, 6, :], ONE[:, :], ACC[1], start=True, stop=True).then_inc(n_tot, 1)
            for k in range(1, 4):
                u = UNIT["tok2"] + 4 * (k - 1)
                n = HEADS[k]["n"]
                for c in range(4):
                    unit_tok(u + c, n, range(4), lambda c_, j, c=c: H(2 * c + j), 0, c == 0, c == 3,
                             free=tiles_before(k - 1) if c == 0 else None)
                head_turn(k - 1)
            u = UNIT["z"]
            for c in range(8):
                if c < 4:
                    pe.wait_ge(h_tok, tiles_before(3) + c + 1)
                else:
                    pe.wait_ge(z_done, c - 3)
                unit_T(u + c, c % 4, H).then_inc(unit_used, 1)
                if c == 4:
                    head_turn(3)
            pe.wait_ge(z_done, 8)
            pe.wait_ge(h_lo, 4)
            attention("dm")

            cq = lambda c_, j: (hi(CQ + j), lo(CQ + j))
            for k in (4, 5):
                unit_tok(UNIT["uq"] + k - 4, 384, range(4), cq, 0, True, True, free=tiles_before(4) if k == 5 else None)
                if k == 5:
                    pe.wait_ge(ATT["dm"]["y_lo"], 4)
                    pe.wait_ge(dm_lo, 2)
                    head_turn(4)
            c = UNIT["ukv"]
            arrive(c)
            for k in (6, 7, 8):
                for tk in range(NT):
                    pe.wait_ge(h_tok, tiles_before(k - 1) + tk + 1)
                    a = (hi(CKV)[:, tk * P:(tk + 1) * P], lo(CKV)[:, tk * P:(tk + 1) * P])
                    n, o = (512, 512) if k == 8 else (256, 256 * (k - 6))
                    b = (WHI[:, c % 2, o:o + n], WLO[:, c % 2, o:o + n])
                    ins = three(PS[:, tk, 0:n], a, b, True, True)
                ins.then_inc(unit_used if k == 8 else k_mm, 1)
                head_turn(k - 1)
            pe.wait_ge(vm_lo, 4)
            attention("mla")

            yo = lambda j: (hi(LQ + j), lo(LQ + j)) if j < 4 else (hi(Y_DM + j - 4), lo(Y_DM + j - 4))
            dense("wout2", yo, y_out, [4, 5, 6, 7, 0, 1, 2, 3],
                  {4: (ATT["mla"]["biased"], mla[-1]["g1"]), 0: (ATT["mla"]["y_lo"], 4), 2: (ATT["mla"]["y_lo"], 6),
                   3: (ATT["mla"]["y_lo"], 8)})

    return nc


def _t5_bucket(dist):
    dist = np.maximum(dist, 0)
    d = np.maximum(dist, 1).astype(np.float32)
    large = 16 + (np.log(d / np.float32(16)) / np.float32(math.log(8.0)) * np.float32(16)).astype(np.int32)
    return np.where(dist < 16, dist, np.minimum(large, NBUCKET - 1))


def _onehot():
    def table(dist, valid):
        m = np.zeros((NBUCKET + 1, dist.size), np.float32)
        m[np.where(valid, _t5_bucket(dist), NBUCKET), np.arange(dist.size)] = 1.0
        return m
    da = 255 - np.arange(OH_A)
    db = SEQ - 1 - np.arange(OH_B)
    b, a = np.divmod(np.arange(OH_C), CMP_A)
    dc = SEQ - (16 * a + b)
    return np.concatenate([table(da, (da >= 0) & (da < 128)), table(db, db >= 0), table(dc, dc >= 0)], axis=1)


def kernel(**inputs):
    import concourse.bacc as _bacc
    from concourse.bass_utils import run_bass_kernel_spmd as _run

    a = {k: np.asarray(v) for k, v in inputs.items()}
    f32 = np.float32

    def tiles(w):
        k, n = w.shape
        return w.reshape(k // P, P, n // P, P).transpose(2, 1, 0, 3).reshape(n // P, P, k)

    def rows2(w, n):
        return w.reshape(4, 2, P, n).transpose(0, 2, 1, 3).reshape(4, P, 2 * n)

    def pad(w):
        out = np.zeros(w.shape[:2] + (1024,), f32)
        out[:, :, :w.shape[2]] = w
        return out

    w = a["w_in"][0]
    off = np.cumsum([0, 512, 128, 128, 512, 128, 128, 128, 128, 128, 128, 24, 1024, 1024])
    qa, ka, va, qb, kc, vc, ksl, vsl, kw, vw, gn, ga, gb = [w[:, off[i]:off[i + 1]] for i in range(13)]

    def pair(m, axis):
        shape = m.shape
        if axis == 1:
            return m.reshape(shape[0], 2, 4, DH).transpose(0, 2, 1, 3).reshape(shape)
        return m.reshape(2, 4, DH, shape[1]).transpose(1, 0, 2, 3).reshape(shape)

    up = np.concatenate([tiles(pair(a["w_up_a"][0], 0)), tiles(pair(a["w_up_b"][0], 0))], axis=2)
    ga, gb = tiles(ga), tiles(gb)
    merge = np.stack([ga, gb, up], axis=1).reshape(24, P, 1024)
    wf = tiles(a["w_ffn_in"][0])
    wf = np.stack([wf[:NF], wf[NF:]], axis=1).reshape(2 * NF, P, 1024)
    down = np.zeros((8, P, 3072), f32)
    down[:, :, :D_FF] = tiles(a["w_ffn_out"][0])
    down = down.reshape(8, P, 3, 1024).transpose(0, 2, 1, 3).reshape(24, P, 1024)
    w1 = np.concatenate([a[n][0].reshape(4, 4, P, 256).transpose(0, 2, 1, 3).reshape(4, P, 1024)
                         for n in ("cmp_w1_k", "cmp_w1_v")])
    v = a["w_in_2"][0]
    uq = a["w_uq_2"][0].reshape(2, P, 2, 384).transpose(2, 1, 0, 3).reshape(2, P, 768)
    ukv = a["w_ukv_2"][0].reshape(P, NH, 2, DH).transpose(0, 2, 1, 3).reshape(1, P, 1024)
    stream = np.concatenate([
        tiles(np.concatenate([pair(qa, 1), pair(qb, 1), ka, ksl, kw, kc, vc], axis=1)),
        pad(rows2(np.concatenate([va, vsl, vw, gn], axis=1), 408)), w1, merge, tiles(a["w_out"][0]), wf, down,
        pad(rows2(a["w_mem_kv_2"][0], 512)),
        pad(rows2(v[:, 0:416], 416)), pad(rows2(v[:, 416:928], 512)), pad(rows2(v[:, 928:1440], 512)),
        tiles(v[:, 1440:2464]), pad(uq), ukv, tiles(a["w_out_2"][0])])
    assert stream.shape == (NU, P, 1024)

    fm = lambda g: g.reshape(-1, P).T
    conv = np.concatenate([a["conv_w"][0], a["conv_b"]])
    conv = conv.reshape(4, 2, NF, P).transpose(3, 2, 1, 0).reshape(P, 8 * NF)
    twice = lambda m: np.concatenate([m, m])
    plain = lambda g: np.concatenate([g[:64], np.ones(P - 64, f32)])[:, None]
    cols = np.concatenate([fm(a["norm_mix"]), fm(a["norm_ffn"]), fm(a["norm_final"]), fm(a["norm_g_2"]),
                           fm(a["mem_norm_g_2"]), fm(a["mla_q_norm_g_2"]), fm(a["mla_kv_norm_g_2"]),
                           twice(a["diff_subln_g_2"][0])[:, None], twice(a["cmp_pos_k"][0].T), twice(a["cmp_pos_v"][0].T),
                           plain(a["mla_qn_g_2"][0]), plain(a["mla_kn_g_2"][0]), conv], axis=1)
    inv = (f32(10000.0) ** (-np.arange(0, 32, 2, dtype=f32) / f32(32))).astype(f32)
    rows = np.concatenate([a["mla_qn_g_2"][0], a["mla_kn_g_2"][0], a["diff_qn_g_2"][0], a["diff_kn_g_2"][0],
                           a["mem_qn_g_2"][0], a["mem_kn_g_2"][0], a["attn_sinks"][0], inv,
                           a["diff_lambda_2"][0].reshape(-1)])[None]
    w2k = a["cmp_w2_k"][0].reshape(2, P, DH).transpose(1, 0, 2)
    w2v = a["cmp_w2_v"][0].reshape(2, P, DH).transpose(1, 0, 2)
    w2 = np.stack([np.concatenate([m, m], axis=2) for m in (w2k, w2v)], axis=1)
    xt = a["x"][0].T.reshape(KT, P, SEQ).transpose(1, 0, 2)
    mt = a["mem_2"][0].T.reshape(KT, P, 256).transpose(1, 0, 2).reshape(P, KT * 256)
    arrays = {"wstream": stream, "xT": xt, "memT": mt, "cols": cols, "rows": rows, "w2": w2,
              "table": a["rel_bias_table"], "onehot": _onehot(), "pos": a["positions_2"][0].reshape(NT, P).T}
    arrays = {k: np.ascontiguousarray(v_) for k, v_ in arrays.items()}

    nc = _bacc.Bacc("TRN2", target_bir_lowering=False, num_devices=1)
    t = {k: nc.dram_tensor(k, v_.shape, mybir.dt.from_np(v_.dtype), kind="ExternalInput").ap() for k, v_ in arrays.items()}
    out = nc.dram_tensor("outT", (P, KT, SEQ), F, kind="ExternalOutput").ap()
    build(nc, t, out)
    r = _run(nc, [arrays], core_ids=[0])
    got = r.results[0]["outT"]
    return np.ascontiguousarray(got.transpose(1, 0, 2).reshape(D, SEQ).T)[None]
```
